# Optimizing a Trainium2 kernel written in Bass

```python
import jax, jax.numpy as jnp
from jax import lax
import numpy as np

D_MODEL = 1024
BATCH = 1
SEQ = 512
DEPTH = 1
DEC_BATCH = 8
DEC_SEQ = 8
PAST_LEN = 2048
PAGE_SIZE = 128

SW_HEADS = 8
SW_KV_HEADS = 2
SW_GROUP = SW_HEADS // SW_KV_HEADS
SW_HEAD_DIM = 64
WINDOW = 128
SW_BLOCK = 128
HG_HEADS = 4
HG_KEY_DIM = 128
HG_VAL_DIM = 128
HG_CHUNK = 64
MEM_LEN = 256
MX_HEADS = 4
MX_HEAD_DIM = 128

SW_Q = SW_HEADS * SW_HEAD_DIM
SW_KV = SW_KV_HEADS * SW_HEAD_DIM
HG_K = HG_HEADS * HG_KEY_DIM
HG_V = HG_HEADS * HG_VAL_DIM
MX_W = MX_HEADS * MX_HEAD_DIM
N_BRANCH = 3
IN_SIZES = (SW_Q, SW_KV, SW_KV, HG_K, HG_K, HG_V, HG_V, MX_W, N_BRANCH * D_MODEL)
IN_WIDTH = sum(IN_SIZES)
IN_OFFSETS = tuple(int(o) for o in np.cumsum(IN_SIZES)[:-1])
D_FF = ((8 * D_MODEL + 3 * 256 - 1) // (3 * 256)) * 256
ALPHA = (2.0 * DEPTH) ** 0.25
BETA = (8.0 * DEPTH) ** -0.25
LN_EPS = 1e-5
RMS_EPS = 1e-6

kernel_name = 'hybrid_swa_sink_hgrn2_memory_decode_step'

def layer_norm(x, w, b):
    xf = x.astype(jnp.float32)
    mu = jnp.mean(xf, axis=-1, keepdims=True)
    var = jnp.mean(jnp.square(xf - mu), axis=-1, keepdims=True)
    return ((xf - mu) * lax.rsqrt(var + LN_EPS) * w.astype(jnp.float32) + b.astype(jnp.float32)).astype(x.dtype)

def alibi_slopes(n):
    return 2.0 ** (-8.0 * jnp.arange(1, n + 1, dtype=jnp.float32) / n)

def sink_attention(q, k, v, dist, valid, sinks):
    s = jnp.einsum('bnqkgd,bnskd->bnkgqs', q, k, preferred_element_type=jnp.float32) * (SW_HEAD_DIM ** -0.5)
    slopes = alibi_slopes(SW_HEADS).reshape(SW_KV_HEADS, SW_GROUP)[:, :, None, None]
    s = s - slopes * dist[:, None, None].astype(jnp.float32)
    s = jnp.where(valid[:, None, None], s, -jnp.inf)
    sink = sinks.astype(jnp.float32).reshape(SW_KV_HEADS, SW_GROUP)[:, :, None, None]
    m = jnp.maximum(jnp.max(s, axis=-1, keepdims=True), sink)
    p = jnp.exp(s - m)
    denom = jnp.sum(p, axis=-1, keepdims=True) + jnp.exp(sink - m)
    return jnp.einsum('bnkgqs,bnskd->bnqkgd', (p / denom).astype(v.dtype), v)

def window_attention_prompt(q, k, v, sinks):
    B, T = q.shape[:2]
    nb = T // SW_BLOCK
    qb = q.reshape(B, nb, SW_BLOCK, SW_KV_HEADS, SW_GROUP, SW_HEAD_DIM)

    def with_prev(a):
        a = a.reshape(B, nb, SW_BLOCK, SW_KV_HEADS, SW_HEAD_DIM)
        prev = jnp.concatenate([jnp.zeros_like(a[:, :1]), a[:, :-1]], axis=1)
        return jnp.concatenate([prev, a], axis=2)

    kk, vv = with_prev(k), with_prev(v)
    blk = jnp.arange(nb)[:, None] * SW_BLOCK
    qpos = blk + jnp.arange(SW_BLOCK)[None]
    kpos = blk - SW_BLOCK + jnp.arange(2 * SW_BLOCK)[None]
    dist = qpos[:, :, None] - kpos[:, None, :]
    valid = (dist >= 0) & (dist < WINDOW) & (kpos[:, None, :] >= 0)
    o = sink_attention(qb, kk, vv, dist, valid, sinks)
    return o.reshape(B, T, SW_Q)

def window_attention_sample(q, k, v, k_buf, v_buf, sinks):
    B, T = q.shape[:2]
    W = k_buf.shape[1]
    kk = jnp.concatenate([k_buf, k], axis=1)
    vv = jnp.concatenate([v_buf, v], axis=1)
    qpos = PAST_LEN + jnp.arange(T)
    kpos = jnp.concatenate([PAST_LEN - W + jnp.arange(W), PAST_LEN + jnp.arange(T)])
    dist = (qpos[:, None] - kpos[None, :])[None]
    valid = (dist >= 0) & (dist < WINDOW)
    o = sink_attention(q.reshape(B, 1, T, SW_KV_HEADS, SW_GROUP, SW_HEAD_DIM),
                       kk[:, None], vv[:, None], dist, valid, sinks)
    return o.reshape(B, T, SW_Q), kk[:, -W:], vv[:, -W:]

def hgrn2_chunkwise(q, k, v, logf, s0):
    B, T = q.shape[:2]
    C = min(HG_CHUNK, T)
    nc = -(-T // C)
    pad = nc * C - T

    def blocks(a):
        a = jnp.pad(a, ((0, 0), (0, pad), (0, 0), (0, 0)))
        return a.reshape(B, nc, C, a.shape[2], a.shape[3]).transpose(1, 0, 3, 2, 4)

    causal = jnp.tril(jnp.ones((C, C), dtype=bool))[:, :, None]

    def step(S, inp):
        qc, kc, vc, gc = inp
        b = jnp.cumsum(gc, axis=2)
        o_inter = jnp.einsum('bhtd,bhde->bhte', qc * jnp.exp(b), S)
        diff = b[:, :, :, None, :] - b[:, :, None, :, :]
        decay = jnp.exp(jnp.where(causal, diff, -jnp.inf))
        A = jnp.einsum('bhtd,bhsd,bhtsd->bhts', qc, kc, decay)
        o = o_inter + jnp.einsum('bhts,bhse->bhte', A, vc)
        b_last = b[:, :, -1:, :]
        S_new = jnp.exp(b_last[:, :, 0, :])[..., None] * S + jnp.einsum('bhsd,bhse->bhde', kc * jnp.exp(b_last - b), vc)
        return S_new, o

    S_fin, o = lax.scan(step, s0, (blocks(q), blocks(k), blocks(v), blocks(logf)))
    o = o.transpose(1, 0, 3, 2, 4).reshape(B, nc * C, q.shape[2], v.shape[3])[:, :T]
    return o, S_fin

def memory_attention(q, mem_k, mem_v):
    B, T = q.shape[:2]
    s = jnp.einsum('bthd,bshd->bhts', q, mem_k, preferred_element_type=jnp.float32) * (MX_HEAD_DIM ** -0.5)
    p = jax.nn.softmax(s, axis=-1)
    return jnp.einsum('bhts,bshd->bthd', p.astype(mem_v.dtype), mem_v).reshape(B, T, MX_W)

def decoder_layer(x, k_buf, v_buf, hg_s0, mem_k, mem_v, lw):
    B, T, _ = x.shape
    f32 = jnp.float32
    proj = x @ lw['w_in']
    sq, sk, sv, hq, hf, hi, hg, mq, gl = jnp.split(proj, IN_OFFSETS, axis=-1)
    sq = sq.reshape(B, T, SW_HEADS, SW_HEAD_DIM)
    sk = sk.reshape(B, T, SW_KV_HEADS, SW_HEAD_DIM)
    sv = sv.reshape(B, T, SW_KV_HEADS, SW_HEAD_DIM)
    if k_buf is None:
        o_sw = window_attention_prompt(sq, sk, sv, lw['sinks'])
        new_k, new_v = sk[:, T - WINDOW:], sv[:, T - WINDOW:]
    else:
        o_sw, new_k, new_v = window_attention_sample(sq, sk, sv, k_buf, v_buf, lw['sinks'])
    lb = lw['hg_lb']
    f = lb + (1.0 - lb) * jax.nn.sigmoid(hf.astype(f32))
    hshape = (B, T, HG_HEADS, HG_KEY_DIM)
    q_h = jax.nn.silu(hq.astype(f32)).reshape(hshape)
    k_h = (1.0 - f).reshape(hshape)
    logf = jnp.log(f).reshape(hshape)
    v_h = hi.astype(f32).reshape(B, T, HG_HEADS, HG_VAL_DIM)
    s0 = jnp.zeros((B, HG_HEADS, HG_KEY_DIM, HG_VAL_DIM), f32) if hg_s0 is None else hg_s0.astype(f32)
    o_h, s_fin = hgrn2_chunkwise(q_h, k_h, v_h, logf, s0)
    o_h = o_h * lax.rsqrt(jnp.mean(jnp.square(o_h), axis=-1, keepdims=True) + RMS_EPS) * lw['hg_norm_w'].astype(f32)
    o_h = (o_h.reshape(B, T, HG_V) * jax.nn.silu(hg.astype(f32))).astype(x.dtype)
    o_m = memory_attention(mq.reshape(B, T, MX_HEADS, MX_HEAD_DIM), mem_k, mem_v)
    g = jax.nn.sigmoid(gl.astype(f32)).reshape(B, T, N_BRANCH, D_MODEL).astype(x.dtype)
    mix = (g[:, :, 0] * (o_sw @ lw['w_up_sw'])
           + g[:, :, 1] * (o_h @ lw['w_up_hg'])
           + g[:, :, 2] * (o_m @ lw['w_up_mx']))
    h = layer_norm(ALPHA * x + mix @ lw['w_o'], lw['ln1_w'], lw['ln1_b'])
    ff_gate, ff_up = jnp.split(h @ lw['w_ffn_in'], 2, axis=-1)
    y = layer_norm(ALPHA * h + (jax.nn.silu(ff_gate) * ff_up) @ lw['w_ffn_out'], lw['ln2_w'], lw['ln2_b'])
    return y, new_k, new_v, s_fin

def setup_inputs(seed: int = 0) -> dict:
    key = jax.random.key(seed)
    ks = jax.random.split(key, 26)

    def nrm(k, shape, scale=1.0):
        return jax.random.normal(k, shape, jnp.float32) * scale

    win_buf = min(WINDOW, PAST_LEN)
    return {
        'x_prompt': nrm(ks[0], (BATCH, SEQ, D_MODEL)),
        'x_sample': nrm(ks[1], (DEC_BATCH, DEC_SEQ, D_MODEL)),
        'cache_k_win': nrm(ks[2], (DEPTH, DEC_BATCH, win_buf, SW_KV_HEADS, SW_HEAD_DIM)),
        'cache_v_win': nrm(ks[3], (DEPTH, DEC_BATCH, win_buf, SW_KV_HEADS, SW_HEAD_DIM)),
        'state_hgrn': nrm(ks[4], (DEPTH, DEC_BATCH, HG_HEADS, HG_KEY_DIM, HG_VAL_DIM), 0.5),
        'cache_mem_k': nrm(ks[5], (DEPTH, DEC_BATCH, MEM_LEN, MX_HEADS, MX_HEAD_DIM)),
        'cache_mem_v': nrm(ks[6], (DEPTH, DEC_BATCH, MEM_LEN, MX_HEADS, MX_HEAD_DIM)),
        'mem_prompt': nrm(ks[7], (BATCH, MEM_LEN, D_MODEL)),
        'ln0_w': 1.0 + nrm(ks[8], (D_MODEL,), 0.02),
        'ln0_b': nrm(ks[9], (D_MODEL,), 0.02),
        'w_in': nrm(ks[10], (DEPTH, D_MODEL, IN_WIDTH), D_MODEL ** -0.5),
        'w_up_sw': nrm(ks[11], (DEPTH, SW_Q, D_MODEL), SW_Q ** -0.5),
        'w_up_hg': nrm(ks[12], (DEPTH, HG_V, D_MODEL), HG_V ** -0.5),
        'w_up_mx': nrm(ks[13], (DEPTH, MX_W, D_MODEL), MX_W ** -0.5),
        'sw_sinks': nrm(ks[14], (DEPTH, SW_HEADS), 0.5),
        'hg_lower_bound': nrm(ks[15], (DEPTH + 1, HG_K), 0.1),
        'hg_norm_w': 1.0 + nrm(ks[16], (DEPTH, HG_VAL_DIM), 0.02),
        'w_mem_kv': nrm(ks[17], (DEPTH, D_MODEL, 2 * MX_W), D_MODEL ** -0.5),
        'w_o': nrm(ks[18], (DEPTH, D_MODEL, D_MODEL), BETA * D_MODEL ** -0.5),
        'ln1_w': 1.0 + nrm(ks[19], (DEPTH, D_MODEL), 0.02),
        'ln1_b': nrm(ks[20], (DEPTH, D_MODEL), 0.02),
        'w_ffn_in': nrm(ks[21], (DEPTH, D_MODEL, 2 * D_FF), D_MODEL ** -0.5),
        'w_ffn_out': nrm(ks[22], (DEPTH, D_FF, D_MODEL), BETA * D_FF ** -0.5),
        'ln2_w': 1.0 + nrm(ks[23], (DEPTH, D_MODEL), 0.02),
        'ln2_b': nrm(ks[24], (DEPTH, D_MODEL), 0.02),
    }

def reference(x_prompt, x_sample, cache_k_win, cache_v_win, state_hgrn, cache_mem_k, cache_mem_v, mem_prompt,
              ln0_w, ln0_b, w_in, w_up_sw, w_up_hg, w_up_mx, sw_sinks, hg_lower_bound, hg_norm_w, w_mem_kv,
              w_o, ln1_w, ln1_b, w_ffn_in, w_ffn_out, ln2_w, ln2_b):
    lower = jnp.cumsum(jax.nn.softmax(hg_lower_bound.astype(jnp.float32), axis=0), axis=0)
    xp = layer_norm(x_prompt, ln0_w, ln0_b)
    xs = layer_norm(x_sample, ln0_w, ln0_b)
    bp = mem_prompt.shape[0]
    kp_l, vp_l, sp_l, mkp_l, mvp_l, ks_l, vs_l, ss_l = [], [], [], [], [], [], [], []
    for l in range(DEPTH):
        lw = {'w_in': w_in[l], 'w_up_sw': w_up_sw[l], 'w_up_hg': w_up_hg[l], 'w_up_mx': w_up_mx[l],
              'sinks': sw_sinks[l], 'hg_lb': lower[l], 'hg_norm_w': hg_norm_w[l], 'w_o': w_o[l],
              'ln1_w': ln1_w[l], 'ln1_b': ln1_b[l], 'w_ffn_in': w_ffn_in[l], 'w_ffn_out': w_ffn_out[l],
              'ln2_w': ln2_w[l], 'ln2_b': ln2_b[l]}
        mkv = (mem_prompt @ w_mem_kv[l]).reshape(bp, MEM_LEN, 2, MX_HEADS, MX_HEAD_DIM)
        mk, mv = mkv[:, :, 0], mkv[:, :, 1]
        xp, kp, vp, sp = decoder_layer(xp, None, None, None, mk, mv, lw)
        xs, ks_, vs_, ss = decoder_layer(xs, cache_k_win[l], cache_v_win[l], state_hgrn[l],
                                         cache_mem_k[l], cache_mem_v[l], lw)
        kp_l.append(kp); vp_l.append(vp); sp_l.append(sp); mkp_l.append(mk); mvp_l.append(mv)
        ks_l.append(ks_); vs_l.append(vs_); ss_l.append(ss)
    return (xp, xs,
            jnp.stack(kp_l), jnp.stack(vp_l), jnp.stack(sp_l), jnp.stack(mkp_l), jnp.stack(mvp_l),
            jnp.stack(ks_l), jnp.stack(vs_l), jnp.stack(ss_l))


_drawn_inputs = setup_inputs


def setup_inputs(seed=0):
    import zlib

    import numpy as np

    out = dict(_drawn_inputs(seed))
    spreads = {}
    factors = {'ln0_w': 2.762,
     'sw_sinks': 39.718,
     'hg_norm_w': 21.386,
     'ln1_w': 2.727,
     'ln1_b': 2.834,
     'ln2_w': 24.473,
     'ln2_b': 24.029,
     'cache_mem_k': 4.613,
     'cache_mem_v': 4.5,
     'w_up_mx': 4.404}
    for name, (base, spread) in spreads.items():
        noise = np.random.default_rng([zlib.crc32(name.encode()), seed]).standard_normal(out[name].shape)
        drawn = base * np.exp(spread * noise) if base else spread * noise
        out[name] = __import__('jax').numpy.asarray(drawn.astype(out[name].dtype))
    for name, factor in factors.items():
        out[name] = (out[name] * factor).astype(out[name].dtype)
    return out
```

```python
from contextlib import ExitStack

import numpy as np

import concourse.bass as bass
from concourse import mybir

F32 = mybir.dt.float32
F32R = mybir.dt.float32r
BF16 = mybir.dt.bfloat16
ALU = mybir.AluOpType
ACT = mybir.ActivationFunctionType
AX = mybir.AxisListType

P = 128
D = 1024
KT = D // P
SEQ, NB, NS = 512, 8, 8
T = SEQ + NB * NS
TH = T // 2
WIN, MEM = 128, 256
NBLK = SEQ // P
FF = 2816
FT_ = FF // P
LN_EPS, RMS_EPS = 1e-5, 1e-6
ALPHA = 2.0 ** 0.25
LEVELS = [64, 32, 16, 8, 4, 2, 1]
SAMPLE_LEVELS = [4, 2, 1]
MASKED = -3.0e37
GATE_OF = (0, 2, 1)
TOKENS = [(P * t, P) for t in range(NBLK)] + [(SEQ, NB * NS)]

C_SK, C_SV, C_HQ, C_HF, C_HI, C_HG, C_MQ, C_GATE = 512, 640, 768, 1280, 1792, 2304, 2816, 3328


def shape_constants():
    i = np.arange(P)[:, None]
    j = np.arange(2 * P)[None, :]
    dist = i + P - j
    negd = np.where((dist >= 0) & (dist < WIN), -dist, MASKED).astype(np.float32)
    row = np.arange(P)
    c, jj, ii = row // 32, (row // 8) % 4, row % 8
    negs = np.full((P, 4, WIN + NB * NS), MASKED, np.float32)
    for r in range(4):
        b = 2 * r + c // 2
        past = ii[:, None] + WIN - np.arange(WIN)[None, :]
        negs[:, r, :WIN] = np.where(past < WIN, -past, MASKED)
        tok = np.arange(NB * NS)[None, :]
        own = (tok // NS == b[:, None]) & (tok % NS <= ii[:, None])
        negs[:, r, WIN:] = np.where(own, -(ii[:, None] - tok % NS), MASKED)
    head = jj + 4 * (c % 2)
    slope8 = (8.0 * 2.0 ** -(head + 1.0)).astype(np.float32)[:, None]
    s = np.arange(P)[:, None]
    t = np.arange(P)[None, :]
    masks = [(s // (2 * m) == t // (2 * m)) & (s % (2 * m) < m) & (t % (2 * m) >= m) for m in LEVELS] + [s == t]
    masks = np.stack(masks, 1).astype(np.float32)
    own8 = (np.arange(P)[:, None] // NS == np.arange(NB)[None, :]).astype(np.float32)
    return {
        "c_negd": negd, "c_negs": negs, "c_masks": masks,
        "c_small": np.concatenate([slope8, own8], 1).astype(np.float32),
        "c_ident": np.eye(P, dtype=np.float32),
    }


def weight_units():
    units, outs = [], {}

    def unit(name, k0, nk, c0, nc_):
        units.append((name, k0, nk, c0, nc_))
        return len(units) - 1

    def full(kind, idx, name, c0):
        u = unit(name, 0, KT, c0, P)
        for half in range(2):
            outs[kind, idx, half] = [(u, k, k) for k in range(KT)]

    order = []

    def plan(keys):
        order.extend(keys)

    for idx in range(8):
        u = unit("mem", 0, KT, idx * P, P)
        outs["mem", idx, 0] = [(u, k, k) for k in range(KT)]
        plan([("mem", idx, 0)])
    proj = [("sq", j, None) for j in range(4)] + [("sk", 0, C_SK), ("sv", 0, C_SV)]
    for kind, c0 in (("mq", C_MQ), ("hq", C_HQ), ("hf", C_HF), ("hi", C_HI), ("hg", C_HG)):
        proj += [(kind, h, c0 + h * P) for h in range(4)]
    for kind, idx, c0 in proj:
        full(kind, idx, "sq" if kind == "sq" else "w_in", idx if kind == "sq" else c0)
        plan([(kind, idx, 0), (kind, idx, 1)])
    for br in range(3):
        for c in range(0, KT, 2):
            for cc in (c, c + 1):
                full(f"gate{br}", cc, "w_in", C_GATE + GATE_OF[br] * D + cc * P)
                plan([(f"gate{br}", cc, 0), (f"gate{br}", cc, 1)])
            u = unit(f"up{br}", 0, 4, c * P, 2 * P)
            for cc in (c, c + 1):
                for half in range(2):
                    outs[f"up{br}", cc, half] = [(u, 2 * k + cc - c, k) for k in range(4)]
                    plan([(f"up{br}", cc, half)])
    for half in range(2):
        for c in range(KT):
            u = unit("w_o", 0, KT, c * P, P)
            outs["o", c, half] = [(u, k, k) for k in range(KT)]
            plan([("o", c, half)])
    for j in range(FT_):
        for kind, c0 in (("fg", j * P), ("fu", FF + j * P)):
            full(kind, j, "ffn_in", c0)
            plan([(kind, j, 0), (kind, j, 1)])
    for half in range(2):
        for c in range(KT):
            parts = []
            for k0 in range(0, FT_, 8):
                nk = min(8, FT_ - k0)
                u = unit("ffn_out", k0, nk, c * P, P)
                parts += [(u, k, k0 + k) for k in range(nk)]
            outs["y", c, half] = parts
            plan([("y", c, half)])
    return units, outs, order


UNITS, OUTS, ORDER = weight_units()


def schedule():
    steps = [("setup",), ("split", 0)]
    seen = set()
    number = {}

    def out(key):
        for u, _, _ in OUTS[key]:
            if u not in seen:
                seen.add(u)
                if u + 1 < len(UNITS):
                    steps.append(("split", u + 1))
        number[key] = len(number)
        steps.append(("out",) + key)

    att = [("ws",)] + [("w", n, g) for n in range(NBLK) for g in range(2)] + [("mp", n) for n in range(NBLK)]
    att += [("ms", 0), ("ms", 1)]
    hg = [("h", n, h) for n in range(NBLK + 1) for h in range(4)]
    state = {"side": [], "pos": 0}

    def slot(keys):
        side, s = state["side"], state["pos"]
        out(keys[0])
        if 2 <= s < len(side) + 2:
            steps.append(("C",) + side[s - 2])
        if 1 <= s < len(side) + 1:
            steps.append(("N",) + side[s - 1])
        for key in keys[1:]:
            out(key)
        if s < len(side):
            steps.append(("A",) + side[s])
        if 1 <= s < len(side) + 1:
            steps.append(("B",) + side[s - 1])
        state["pos"] += 1

    def finish_side():
        while state["pos"] < len(state["side"]) + 2:
            side, s = state["side"], state["pos"]
            if 2 <= s < len(side) + 2:
                steps.append(("C",) + side[s - 2])
            if 1 <= s < len(side) + 1:
                steps.append(("N",) + side[s - 1])
            if s < len(side):
                steps.append(("A",) + side[s])
            if 1 <= s < len(side) + 1:
                steps.append(("B",) + side[s - 1])
            state["pos"] += 1

    steps += [("memx", 0), ("memx", 1), ("stats0",)]
    for idx in range(8):
        out(("mem", idx, 0))
        if idx < 5:
            steps.append(("ln0", idx))
        steps.append(("turn_mem", idx))
    for kind, n in (("sq", 4), ("sk", 1), ("sv", 1)):
        for j in range(n):
            out((kind, j, 0))
            out((kind, j, 1))
            if kind in ("sk", "sv"):
                steps.append(("turn", kind, j))
    steps.append(("wk",))
    state["side"], state["pos"] = att, 0
    for kind in ("mq", "hq", "hf", "hi", "hg"):
        for j in range(4):
            slot([(kind, j, 0), (kind, j, 1)])
            if kind == "hf" and j == 3:
                steps += [("scan", i) for i in range(4)]
            if kind == "hi":
                steps.append(("turn", kind, j))
    finish_side()
    state["side"], state["pos"] = hg, 0
    for br in range(3):
        for j in range(4):
            steps.append(("branch", br, j))
        for c in range(0, KT, 2):
            for kind in (f"gate{br}", f"up{br}"):
                for cc in (c, c + 1):
                    slot([(kind, cc, 0), (kind, cc, 1)])
                    if 24 <= state["pos"] < 28:
                        steps.append(("rms_sum", state["pos"] - 24))
                    if state["pos"] == 28:
                        steps += [("rms", h) for h in range(4)]
                    if kind == "up2":
                        steps.append(("mix", cc))
    for c in range(KT):
        out(("o", c, 0))
        steps.append(("mean", 1, 0, c))
    steps.append(("var", 1, 0))
    for c in range(KT):
        out(("o", c, 1))
        steps.append(("mean", 1, 1, c))
        if c == 2:
            steps.append(("norm", 1, 0))
    steps.append(("var", 1, 1))
    steps.append(("norm", 1, 1))
    for j in range(FT_):
        for kind in ("fg", "fu"):
            out((kind, j, 0))
            out((kind, j, 1))
    for c in range(KT):
        out(("y", c, 0))
        steps.append(("mean", 2, 0, c))
    steps.append(("var", 2, 0))
    out(("y", 0, 1))
    steps.append(("mean", 2, 1, 0))
    steps.append(("norm", 2, 0))
    for c in range(1, KT):
        out(("y", c, 1))
        steps.append(("mean", 2, 1, c))
    steps.append(("var", 2, 1))
    steps.append(("norm", 2, 1))
    return steps, number


SCHEDULE, OUT_NO = schedule()
MAIN_BANKS = 3
S0_, S1_, T0_, T1_, V_ = 3, 4, 5, 6, 7

OUT_CHUNKS = {0: [(0, 128), (128, 128), (256, 32)], 1: [(288, 128), (416, 96), (512, 64)]}


def build_decoder_layer(nc, a, outs_):
    ctx = ExitStack()
    with ctx:
        place = {"at": 16512}

        def sb(name, shape, dt, offset=None):
            size = int(np.prod(shape[1:])) * mybir.dt.size(dt)
            if offset is None:
                offset = place["at"]
                place["at"] += -(-size // 32) * 32
            return nc.alloc_sbuf_tensor_at(name, list(shape), dt, offset=offset)

        def sem(name):
            return ctx.enter_context(nc.semaphore(name))

        XH = sb("x_hi", [P, KT, T], F32R)
        XL = sb("x_lo", [P, KT, T], F32R)
        RAW = [sb(f"w_raw{i}", [P, 8, P], F32) for i in range(3)]
        WH = [sb(f"w_hi{i}", [P, 8, P], F32R) for i in range(2)]
        WL = [sb(f"w_lo{i}", [P, 8, P], F32R) for i in range(2)]
        IDENT = sb("ident", [P, P], F32)
        ONES = sb("ones", [P, P], F32)
        VEC = sb("vectors", [P, 64], F32)
        SMALL = sb("small", [P, 9], F32)
        SINK = sb("sinks8", [P, 9], F32)
        LB = sb("lower_bound", [P, 8], F32)
        LBT = sb("lower_tmp", [P, 12], F32)
        EPS = sb("eps", [P, 2], F32)
        ST = sb("softmax_stats", [P, 2, 28], F32)
        BNS = sb("bn", [P, 5, 12], F32)
        BNV = sb("bn_mean_var", [P, 5, 2], F32)
        BNR = sb("bn_rstd", [P, 5], F32)
        EBL = sb("exp_b_last", [P, 4, NB], F32)
        EX = [sb(f"exp{i}", [P, TH], F32) for i in range(2)]
        sg0 = place["at"]
        SG = [sb(f"gate{i}", [P, TH], F32) for i in range(4)]
        FT = [sb(f"to_turn{i}", [P, T], F32, sg0 + 4 * T * i) for i in range(2)]
        arena = place["at"]
        MIX = sb("mix", [P, KT, T], F32)
        OSH = sb("branch_hi", [P, 4, T], F32R)
        OSL = sb("branch_lo", [P, 4, T], F32R)
        o = arena
        XP = sb("probs", [P, 2, 4, 2 * P], F32, o); o += 8192
        PT = sb("probs_T", [P, 4, 2, P], F32, o); o += 4096
        NEGD = sb("negd", [P, 2 * P], F32, o); o += 1024
        NEGS = sb("negs", [P, 4, WIN + NB * NS], F32, o); o += 3072
        RING = [sb(f"mem_ring{i}", [P, 2, 512], F32, o + 4096 * i) for i in range(4)]; o += 16384
        QM = sb("q_masked", [P, NB, 4, 32], F32, o)
        MKTM = sb("mem_k_tokens", [P, 2, 512], F32, o)
        proj0 = place["at"]
        SQ = sb("sq", [P, 4, T], F32)
        MQ = sb("mq", [P, 4, T], F32)
        HQ = sb("hq", [P, 4, T], F32)
        HB = sb("hb", [P, 4, T], F32)
        HK = sb("hk", [P, 4, T], F32)
        HV = sb("hv", [P, NBLK + 1, 512], F32)
        HG = sb("hg", [P, 4, T], F32)
        skv = place["at"]
        SK = sb("sk", [P, T], F32)
        SV = sb("sv", [P, NBLK + 1, P], F32)
        mkv = place["at"]
        MKT = sb("mem_kT", [P, 4, MEM], F32)
        MV = sb("mem_v", [P, 2, 512], F32)
        hq0 = proj0 + 2 * 4 * T * 4
        MX = [sb(f"mem_x{i}", [P, D], F32, hq0 + 4096 * i) for i in range(2)]
        MH = sb("mem_hi", [P, KT, MEM], F32R, hq0 + 8192)
        ML = sb("mem_lo", [P, KT, MEM], F32R, hq0 + 16384)
        hv0 = hq0 + 3 * 4 * T * 4
        XS = [sb(f"x_tokens{i}", [P, D], F32, arena + 4096 * i if i < 3 else hv0 + 4096 * (i - 3))
              for i in range(5)]
        XT = sb("x_normed", [P, KT, P], F32, hv0 + (NBLK + 1) * 512 * 4)
        VR = sb("vector_rows", [64, P], F32, hv0 + (NBLK + 1) * 512 * 4 + 4096)
        hs = place["at"]
        E = sb("decay", [P, 8, P], F32)
        EK = sb("decay_k", [P, 8, P], F32)
        EQ = sb("decay_q", [P, 8, P], F32)
        ASB = sb("a_sum", [P, P], F32)
        QE = sb("exp_b", [P, P], F32)
        QW = [sb(f"q_exp_b{i}", [P, P], F32) for i in range(2)]
        KTM = [sb(f"k_tokens{i}", [P, P], F32) for i in range(2)]
        RRS = sb("rms_rstd", [P, 8, TH], F32, hs)
        RSQ = sb("rms_squares", [P, 2, TH], F32, hs + 8 * TH * 4)
        MASKS = sb("masks", [P, 8, P], F32)
        RST = sb("reset", [P, T], BF16)
        STATE = sb("state", [P, 4, P], F32)
        AM = sb("a_masked", [P, 8, P], F32, hs + 8192)
        KC = sb("win_k", [P, NB, P], F32, hs)
        VC = sb("win_v", [P, NB, P], F32, hs + 4096)
        KTS = sb("win_kT", [P, NB, P], F32, hs + 8192)
        MKB = sb("mem_kT_batch", [P, 4, MEM], F32, hs)
        SKTM = sb("sk_tokens", [P, 2, P], F32, hs + 12288)
        QSB = sb("sample_q", [P, NB, 32], F32, hs + 13312)
        SIN = sb("sample_state", [P, NB, P], F32, mkv)
        SOUT = sb("sample_state_new", [P, NB, P], F32, mkv + 4096)
        VB = sb("v_by_batch", [64, NB, P], F32, skv)
        assert place["at"] <= 229368, place["at"]
        MIXH = sb("mix_hi", [P, KT, T], F32R, proj0)
        MIXL = sb("mix_lo", [P, KT, T], F32R, proj0 + KT * T * 4)
        GH = sb("hidden_hi", [P, FT_, T], F32R, arena)
        GL = sb("hidden_lo", [P, FT_, T], F32R, arena + FT_ * T * 4)
        o = arena + 2 * FT_ * T * 4
        Y = sb("pre_norm", [P, KT, T], F32, o); o += KT * T * 4
        SQR = sb("squares", [P, KT, TH], F32, o); o += KT * TH * 4
        OUTT = [sb(f"out_tokens{i}", [P, D], F32, o + 4096 * i) for i in range(2)]
        assert o + 8192 <= 229368

        BANK = [ctx.enter_context(nc.psum_tensor(f"bank{i}", [P, 512], F32)) for i in range(8)]

        raw_in = [sem(f"raw_in{i}") for i in range(3)]
        w_hi, w_lo, w_used, out_ready = sem("w_hi"), sem("w_lo"), sem("w_used"), sem("out_ready")
        bank_free = [sem(f"bank_free{i}") for i in range(8)]
        dve_step, act_step, pool_step = sem("dve_step"), sem("act_step"), sem("pool_step")
        silu_tanh, gate_used, ex_free = sem("silu_tanh"), sem("gate_used"), [sem(f"ex_free{i}") for i in range(2)]
        const_in, vec_in, sink_in, attc_in, mask_in = (
            sem(n) for n in ("const_in", "vec_in", "sink_in", "attc_in", "mask_in"))
        memx_in = [sem(f"memx_in{i}") for i in range(2)]
        xs_in = [sem(f"xs_in{i}") for i in range(5)]
        vecT_ready, setup_done, lb_shifted, lb_exp = (
            sem(n) for n in ("vecT_ready", "setup_done", "lb_shifted", "lb_exp"))
        x_var, x_rstd, x_scaled, xT_ready, x_hi_done, x_lo_done = (
            sem(n) for n in ("x_var", "x_rstd", "x_scaled", "xT_ready", "x_hi_done", "x_lo_done"))
        memT_ready, mem_hi_done, turn_ready = sem("memT_ready"), sem("mem_hi_done"), sem("turn_ready")
        f_ready, logf_done = sem("f_ready"), sem("logf_done")
        cache_in, cacheT_ready, sample_q = sem("cache_in"), sem("cacheT_ready"), sem("sample_q")
        ring_in = [sem(f"ring_in{i}") for i in range(4)]
        ring_used, memK_turned, mkb_used, qm_ready = (
            sem(n) for n in ("ring_used", "memK_turned", "mkb_used", "qm_ready"))
        scores_ready, max_ready, p_exp, p_ready, pT_ready, pv_ready = (
            sem(n) for n in ("scores_ready", "max_ready", "p_exp", "p_ready", "pT_ready", "pv_ready"))
        d_ready, e_ready, ekq_ready, a_ready, a_sum, kT_ready, ho_ready = (
            sem(n) for n in ("d_ready", "e_ready", "ekq_ready", "a_ready", "a_sum", "kT_ready", "ho_ready"))
        state_in, vb_ready, state_out, kv_stored = (
            sem(n) for n in ("state_in", "vb_ready", "state_out", "kv_stored"))
        rms_sq, rms_sum, rms_rstd, branch_split = (
            sem(n) for n in ("rms_sq", "rms_sum", "rms_rstd", "branch_split"))
        mix_split, y_ready, mean_ready, centered, squared, var_ready, ln_rstd = (
            sem(n) for n in ("mix_split", "y_ready", "mean_ready", "centered", "squared", "var_ready", "ln_rstd"))
        hidden_done, ln_scaled, ln_hi, ln_lo, outT_ready = (
            sem(n) for n in ("hidden_done", "ln_scaled", "ln_hi", "ln_lo", "outT_ready"))
        out_dma = [sem(f"out_dma{i}") for i in range(2)]
        cache_moved, prompt_state_out = sem("cache_moved"), sem("prompt_state_out")

        vec = {n: VEC[:, 8 * i:8 * i + 8] for i, n in
               enumerate(("ln0_w", "ln0_b", "ln1_w", "ln1_b", "ln2_w", "ln2_b", "hg_lb"))}
        NORMW = VEC[:, 56:57]
        att_units = [s[1:] for s in SCHEDULE if s[0] == "A" and s[1] != "h"]
        att_no = {u: i for i, u in enumerate(att_units)}
        n_att = len(att_units)
        hg_units = [s[1:] for s in SCHEDULE if s[0] == "A" and s[1] == "h"]
        hg_no = {u: i for i, u in enumerate(hg_units)}

        first_use, last_use = {}, {}
        for key in ORDER:
            for n, (u, _, _) in enumerate(OUTS[key]):
                first_use.setdefault(u, (key, n))
                last_use[u] = (key, n)
        inner_uses = [u for u in range(len(UNITS)) if last_use[u][1] < len(OUTS[last_use[u][0]]) - 1]
        inner_no = {u: i + 1 for i, u in enumerate(inner_uses)}

        def unit_used(eng, u):
            if u in inner_no:
                eng.wait_ge(w_used, inner_no[u])
            else:
                eng.wait_ge(out_ready, OUT_NO[last_use[u][0]] + 1)

        def main_bank(key):
            return OUT_NO[key] % MAIN_BANKS

        def out_saved(eng, key):
            eng.wait_ge(bank_free[main_bank(key)], OUT_NO[key] // MAIN_BANKS + 1)

        bank_use = {}

        def saved(eng, *what):
            bank, count = bank_use[what]
            eng.wait_ge(bank_free[bank], count)

        def moving(key, k):
            kind, _, half = key
            cols = slice(half * TH, half * TH + TH)
            if kind == "mem":
                return MH[:, k, :], ML[:, k, :]
            if kind[:2] == "up":
                return OSH[:, k, cols], OSL[:, k, cols]
            if kind == "o":
                return MIXH[:, k, cols], MIXL[:, k, cols]
            if kind == "y":
                return GH[:, k, cols], GL[:, k, cols]
            return XH[:, k, cols], XL[:, k, cols]

        def bcast(ap, n):
            return ap.unsqueeze(2).to_broadcast([ap.shape[0], ap.shape[1], n])

        def over(ap, n):
            return ap.unsqueeze(1).to_broadcast([ap.shape[0], n, ap.shape[1]])

        def f32(ap):
            return ap.bitcast(F32)

        def unit_source(u):
            name, k0, nk, c0, ncols = UNITS[u]
            raw = RAW[u % 3]
            if name == "sq":
                w = a["w_in"].rearrange("(k p) n -> p k n", p=P)
                return [(raw[:, :, 0:64], w[:, :, c0 * 64:c0 * 64 + 64]),
                        (raw[:, :, 64:128], w[:, :, (c0 + 4) * 64:(c0 + 4) * 64 + 64])]
            if name == "up0":
                w = a["w_up_sw"].rearrange("(g k p) n -> g p k n", g=2, p=64)
                v = raw[:, :, :].rearrange("p (k c) n -> p k (c n)", k=4)
                return [(v[64 * g:64 * g + 64], w[g, :, :, c0:c0 + ncols]) for g in range(2)]
            src = {"mem": "w_mem_kv", "w_in": "w_in", "up1": "w_up_mx", "up2": "w_up_hg", "w_o": "w_o",
                   "ffn_in": "w_ffn_in", "ffn_out": "w_ffn_out"}[name]
            w = a[src].rearrange("(k p) n -> p k n", p=P)[:, k0:k0 + nk, c0:c0 + ncols]
            if ncols == 2 * P:
                return [(raw[:, :, :].rearrange("p (k c) n -> p k (c n)", k=4), w)]
            return [(raw[:, 0:nk, :], w)]

        raw_count, raw_full = [0, 0, 0], {}
        for u in range(len(UNITS)):
            raw_count[u % 3] += 16 * len(unit_source(u))
            raw_full[u] = raw_count[u % 3]

        def unit_tiles(u):
            return UNITS[u][2] * UNITS[u][4] // P

        def hg_cols(n):
            return (P * n, P, LEVELS) if n < NBLK else (SEQ, NB * NS, SAMPLE_LEVELS)

        def lo_of(u):
            return P if u[:2] == ("w", 0) else 0

        SILU = ("hq", "hg", "fg")
        gate_used_no = {key: i + 1 for i, key in enumerate(k for k in ORDER if k[0][:2] == "up")}

        def sig_dst(key):
            kind, idx, half = key
            cols = slice(half * TH, half * TH + TH)
            if kind in ("hq", "hg", "hf"):
                return {"hq": HQ, "hg": HG, "hf": HB}[kind][:, idx, cols]
            return SG[2 * (idx % 2) + half][:]

        def level_view(ap, m):
            return ap.rearrange("p (b m) -> p b m", m=2 * m)

        block = ctx.enter_context(nc.Block())

        @block.tensor
        def _(pe):
            uses = [0] * 8

            def take(bank, *what):
                if uses[bank]:
                    pe.wait_ge(bank_free[bank], uses[bank])
                uses[bank] += 1
                if what:
                    bank_use[what] = (bank, uses[bank])
                return BANK[bank]

            def main(key):
                kind, idx, half = key
                bank = take(main_bank(key))
                if kind == "mem":
                    saved(pe, "memx", 1, 0)
                    saved(pe, "memx", 1, 1)
                elif kind[:2] == "up":
                    pe.wait_ge(branch_split, 4 * int(kind[2]) + 4)
                elif kind == "o":
                    pe.wait_ge(mix_split, KT)
                elif kind == "y":
                    pe.wait_ge(hidden_done, 2 * FT_ - 1 + half)
                elif kind[0] == "f":
                    pe.wait_ge(ln_lo, KT * (half + 1))
                else:
                    pe.wait_ge(x_lo_done, 5 if half else 3)
                parts = OUTS[key]
                n = MEM if kind == "mem" else TH
                for i, (u, tile, k) in enumerate(parts):
                    if first_use[u] == (key, i):
                        pe.wait_ge(w_hi, u + 1)
                        pe.wait_ge(w_lo, u + 1)
                    hi, lo = moving(key, k)
                    wh, wl = WH[u % 2][:, tile, :], WL[u % 2][:, tile, :]
                    pe.matmul(bank[:, 0:n], wh, lo, start=(i == 0), stop=False)
                    pe.matmul(bank[:, 0:n], wl, hi, start=False, stop=False)
                    mm = pe.matmul(bank[:, 0:n], wh, hi, start=False, stop=(i == len(parts) - 1))
                    if last_use[u] == (key, i) and u in inner_no:
                        mm.then_inc(w_used, 1)
                mm.then_inc(out_ready, 1)

            n_ring = [0]

            def ring_tile():
                i = n_ring[0]
                pe.wait_ge(ring_in[i % 4], 16 * (i // 4 + 1))
                n_ring[0] += 1
                return RING[i % 4]

            def scores(u):
                kind, no = u[0], att_no[u]
                if kind == "w":
                    n, g = u[1:]
                    lo = lo_of(u)
                    for kv in range(2):
                        bank = take(S0_ + kv, "scores", no, kv)
                        for jj in range(2):
                            mm = pe.matmul(bank[:, 256 * jj + lo:256 * jj + 256],
                                           SQ[64 * kv:64 * kv + 64, 2 * g + jj, P * n:P * n + P],
                                           SK[64 * kv:64 * kv + 64, P * (n - 1) + lo:P * (n + 1)],
                                           start=True, stop=True)
                elif kind == "ws":
                    out_saved(pe, ("sk", 0, 1))
                    saved(pe, "cacheT", 0)
                    saved(pe, "cacheT", 1)
                    pe.wait_ge(sample_q, 1)
                    banks = [take(S0_, "scores", no, 0), take(S1_, "scores", no, 1)]
                    for kv in range(2):
                        for b in range(NB):
                            r, c = b // 2, 2 * (b % 2) + kv
                            dst = banks[r // 2][32 * c:32 * c + 32, 192 * (r % 2):192 * (r % 2) + 192]
                            q = QSB[64 * kv:64 * kv + 64, b, :]
                            pe.matmul(dst[:, 0:WIN], q, KTS[64 * kv:64 * kv + 64, b, :], start=True, stop=True)
                            mm = pe.matmul(dst[:, WIN:192], q, SK[64 * kv:64 * kv + 64, SEQ:T],
                                           start=True, stop=True)
                elif kind == "mp":
                    n = u[1]
                    out_saved(pe, ("mq", 3, 1))
                    for s in range(4):
                        if s % 2 == 0:
                            bank = take(S0_ + s // 2, "scores", no, s // 2)
                        mm = pe.matmul(bank[:, 256 * (s % 2):256 * (s % 2) + 256], MQ[:, s, P * n:P * n + P],
                                       MKT[:, s, :], start=True, stop=True)
                else:
                    pe.wait_ge(qm_ready, NB)
                    bank = take(S0_, "scores", no, 0)
                    for bl in range(4):
                        b = 4 * u[1] + bl
                        keys = ring_tile()
                        for s in range(2):
                            tb = take(T0_ + s, "memK", b, s)
                            for hh in range(2):
                                for c in range(2):
                                    h = 2 * s + hh
                                    mm = pe.transpose(tb[:, 256 * hh + P * c:256 * hh + P * c + P],
                                                      keys[:, c, P * h:P * h + P], IDENT[:])
                        mm.then_inc(memK_turned, 1)
                        for s in range(2):
                            saved(pe, "memK", b, s)
                        for h in range(4):
                            mm = pe.matmul(bank[32 * h:32 * h + 32, 0:256], QM[:, b, h, :], MKB[:, h, :],
                                           start=(bl == 0), stop=(bl == 3), skip_group_check=True)
                        if bl < 3:
                            mm.then_inc(mkb_used, 1)
                mm.then_inc(scores_ready, 1)

            def turn_probs(u):
                kind, no = u[0], att_no[u]
                probs = XP[:, no % 2]
                pe.wait_ge(p_ready, no + 1)
                if kind == "ws":
                    b0, b1 = take(T0_, "pT", no, 0), take(T1_, "pT", no, 1)
                    for r in range(4):
                        pe.transpose(b0[:, P * r:P * r + P], probs[:, r, 0:P], IDENT[:])
                        mm = pe.transpose(b1[0:64, P * r:P * r + P], probs[:, r, P:192], IDENT[:])
                elif kind == "ms":
                    b0 = take(T0_, "pT", no, 0)
                    for c in range(2):
                        mm = pe.transpose(b0[:, P * c:P * c + P], probs[:, 0, P * c:P * c + P], IDENT[:])
                else:
                    for s in range(4):
                        if s % 2 == 0:
                            bank = take(T0_ + s // 2, "pT", no, s // 2)
                        for c in range(lo_of(u) // P, 2):
                            col = 256 * (s % 2) + P * c
                            mm = pe.transpose(bank[:, col:col + P], probs[:, s, P * c:P * c + P], IDENT[:])
                mm.then_inc(pT_ready, 1)

            def values(u):
                kind, no = u[0], att_no[u]
                saved(pe, "pT", no, 0)
                if kind != "ms":
                    saved(pe, "pT", no, 1)
                ptf = PT[:].rearrange("p a c t -> p (a c t)")
                bank = take(V_, "pv", no)
                if kind == "w":
                    n, g = u[1:]
                    c0 = lo_of(u) // P
                    for kv in range(2):
                        for c in range(c0, 2):
                            mm = pe.matmul(bank[64 * kv:64 * kv + 64, 0:256], SV[:, n - 1 + c, 64 * kv:64 * kv + 64],
                                           PT[:, 2 * kv:2 * kv + 2, c, :], start=(c == c0), stop=(c == 1))
                elif kind == "ws":
                    for kv in range(2):
                        for b in range(NB):
                            r, c = b // 2, 2 * (b % 2) + kv
                            dst = bank[64 * kv:64 * kv + 64, 32 * b:32 * b + 32]
                            col = P * r + 32 * c
                            pe.matmul(dst, VC[:, b, 64 * kv:64 * kv + 64], ptf[:, col:col + 32],
                                      start=True, stop=False)
                            mm = pe.matmul(dst, SV[0:64, NBLK, 64 * kv:64 * kv + 64],
                                           ptf[0:64, 512 + col:512 + col + 32], start=False, stop=True)
                elif kind == "mp":
                    for h in range(4):
                        for c in range(2):
                            mm = pe.matmul(bank[:, P * h:P * h + P], MV[:, c, P * h:P * h + P], PT[:, h, c, :],
                                           start=(c == 0), stop=(c == 1))
                else:
                    for bl in range(4):
                        vals = ring_tile()
                        for h in range(4):
                            for c in range(2):
                                col = 32 * h + 8 * bl
                                mm = pe.matmul(bank[:, col:col + 8], vals[:, c, P * h:P * h + P],
                                               ptf[:, P * c + col:P * c + col + 8],
                                               start=(c == 0), stop=(c == 1))
                        if bl < 3:
                            mm.then_inc(ring_used, 1)
                mm.then_inc(pv_ready, 1)

            def hgrn_pairs(u):
                _, n, h = u
                no = hg_no[u]
                t0, w, levels = hg_cols(n)
                cols = slice(t0, t0 + w)
                nl = len(levels)
                pe.wait_ge(ekq_ready, no + 1)
                for i in range(nl + 1):
                    if i % 4 == 0:
                        bank = take(S0_ + i // 4, "a", no, i // 4)
                    k, q = (EK[:, i, 0:w], EQ[:, i, 0:w]) if i < nl else (HK[:, h, cols], HQ[:, h, cols])
                    mm = pe.matmul(bank[0:w, P * (i % 4):P * (i % 4) + w], k, q, start=True, stop=True)
                mm.then_inc(a_ready, 1)
                bank = take(T0_, "kT", no)
                pe.transpose(bank[0:w, 0:P], EK[:, 7, 0:w], IDENT[:]).then_inc(kT_ready, 1)

            def hgrn_out(u):
                _, n, h = u
                no = hg_no[u]
                _, w, _ = hg_cols(n)
                v = HV[0:w, n, P * h:P * h + P]
                pe.wait_ge(a_sum, no + 1)
                saved(pe, "kT", no)
                if n < NBLK:
                    if n:
                        saved(pe, "state", no - 4)
                    bank = take(V_, "ho", no)
                    pe.matmul(bank[:, 0:P], v, ASB[:], start=True, stop=(n == 0))
                    if n:
                        pe.matmul(bank[:, 0:P], STATE[:, h, :], QW[no % 2][:], start=False, stop=True)
                    sbank = take(T1_, "state", no)
                    mm = pe.matmul(sbank[:, 0:P], KTM[no % 2][:], v, start=True, stop=True)
                else:
                    pe.wait_ge(state_in, 16 * (h + 1))
                    pe.wait_ge(vb_ready, h + 1)
                    bank = take(V_, "ho", no)
                    pe.matmul(bank[:, 0:w], v, ASB[0:w, 0:w], start=True, stop=False, skip_group_check=True)
                    for b in range(NB):
                        pe.matmul(bank[:, NS * b:NS * b + NS], SIN[:, b, :], QW[no % 2][:, NS * b:NS * b + NS],
                                  start=False, stop=(b == NB - 1), skip_group_check=True)
                    for i in range(2):
                        sbank = take(T0_ + i, "state", no, i)
                        mm = pe.matmul(sbank[:, :], KTM[no % 2][0:w, :], VB[:, 4 * i:4 * i + 4, :],
                                       start=True, stop=True)
                mm.then_inc(ho_ready, 1)

            for s in SCHEDULE:
                what, rest = s[0], s[1:]
                if what == "out":
                    main(rest)
                elif what == "setup":
                    pe.wait_ge(const_in, 32)
                    pe.wait_ge(vec_in, 128)
                    pe.transpose(take(V_, "vec")[:, 0:57], VR[0:57, :], IDENT[0:57, 0:57]).then_inc(vecT_ready, 1)
                elif what == "memx":
                    t = rest[0]
                    pe.wait_ge(memx_in[t], 16)
                    for i in range(2):
                        bank = take(T0_ + i, "memx", t, i)
                        for k in range(4):
                            mm = pe.transpose(bank[:, P * k:P * k + P],
                                              MX[t][:, P * (4 * i + k):P * (4 * i + k) + P], IDENT[:])
                    mm.then_inc(memT_ready, 1)
                elif what == "ln0":
                    t = rest[0]
                    n = TOKENS[t][1]
                    pe.wait_ge(x_scaled, t + 1)
                    for i in range(2):
                        bank = take(T0_ + i, "xT", t, i)
                        for k in range(4):
                            mm = pe.transpose(bank[:, P * k:P * k + n],
                                              XS[t][0:n, P * (4 * i + k):P * (4 * i + k) + P],
                                              IDENT[0:n, 0:n])
                    mm.then_inc(xT_ready, 1)
                elif what == "turn_mem":
                    idx = rest[0]
                    out_saved(pe, ("mem", idx, 0))
                    src = MKT[:, idx, :] if idx < 4 else FT[0][:, 0:MEM]
                    bank = take(V_, "turn_mem", idx)
                    for c in range(2):
                        mm = pe.transpose(bank[:, P * c:P * c + P], src[:, P * c:P * c + P], IDENT[:])
                    mm.then_inc(turn_ready, 1)
                elif what == "turn":
                    kind, idx = rest
                    out_saved(pe, (kind, idx, 0))
                    out_saved(pe, (kind, idx, 1))
                    b0, b1 = take(T0_, "turn", kind, idx, 0), take(T1_, "turn", kind, idx, 1)
                    src = SK if kind == "sk" else FT[idx % 2]
                    for t, (t0, n) in enumerate(TOKENS):
                        if kind == "sk" and t < NBLK - 1:
                            continue
                        dst = b0[0:n, P * t:P * t + P] if t < NBLK else b1[0:n, 0:P]
                        mm = pe.transpose(dst, src[:, t0:t0 + n], IDENT[:])
                    mm.then_inc(turn_ready, 1)
                elif what == "wk":
                    pe.wait_ge(cache_in, 32)
                    for i in range(2):
                        bank = take(T0_ + i, "cacheT", i)
                        for k in range(4):
                            mm = pe.transpose(bank[:, P * k:P * k + P], KC[:, 4 * i + k, :], IDENT[:])
                    mm.then_inc(cacheT_ready, 1)
                elif what == "A":
                    (hgrn_pairs if rest[0] == "h" else scores)(rest)
                elif what == "B" and rest[0] != "h":
                    turn_probs(rest)
                elif what == "C":
                    (hgrn_out if rest[0] == "h" else values)(rest)
                elif what == "rms_sum":
                    h = rest[0]
                    for half in range(2):
                        pe.wait_ge(rms_sq, 2 * h + half + 1)
                        bank = take(V_, "rms", h, half)
                        pe.matmul(bank[:, 0:TH], ONES[:], RSQ[:, half, :], start=True,
                                  stop=True).then_inc(rms_sum, 1)
                elif what == "mean":
                    ln, half, c = rest
                    pe.wait_ge(y_ready, 16 * (ln - 1) + 8 * half + c + 1)
                    bank = take(V_, "mean", ln, half) if c == 0 else BANK[V_]
                    mm = pe.matmul(bank[:, 0:TH], ONES[:], Y[:, c, half * TH:half * TH + TH],
                                   start=(c == 0), stop=(c == KT - 1))
                    if c == KT - 1:
                        mm.then_inc(mean_ready, 1)
                elif what == "var":
                    ln, half = rest
                    bank = take(T0_, "var", ln, half)
                    for c in range(KT):
                        pe.wait_ge(squared, 16 * (ln - 1) + 8 * half + c + 1)
                        mm = pe.matmul(bank[:, 0:TH], ONES[:], SQR[:, c, :], start=(c == 0), stop=(c == KT - 1))
                    mm.then_inc(var_ready, 1)
                elif what == "norm" and rest[0] == 2:
                    half = rest[1]
                    for i, (t0, n) in enumerate(OUT_CHUNKS[half]):
                        for j in range(2):
                            pe.wait_ge(ln_hi, 16 + 8 * half + 4 * j + 4)
                            bank = take(S0_ + j, "outT", 3 * half + i, j)
                            for k in range(4):
                                mm = pe.transpose(bank[0:n, P * k:P * k + P], Y[:, 4 * j + k, t0:t0 + n], IDENT[:])
                        mm.then_inc(outT_ready, 1)

        @block.sync
        def _(sp):
            for u in range(len(UNITS)):
                if u >= 3:
                    sp.wait_ge(w_lo, u - 2)
                for dst, src in unit_source(u):
                    sp.dma_start(dst, src).then_inc(raw_in[u % 3], 16)

        @block.gpsimd
        def _(pool):
            def load(sem_, dst, src):
                pool.dma_start(dst, src).then_inc(sem_, 16)

            load(const_in, IDENT[:], a["c_ident"])
            load(const_in, SMALL[:], a["c_small"])
            for i in range(2):
                load(memx_in[i], MX[i][:], a["mem_prompt"][P * i:P * i + P, :])
            for i in range(5):
                src = a["x_sample"] if i == NBLK else a["x_prompt"][P * i:P * i + P, :]
                load(xs_in[i], XS[i][0:TOKENS[i][1], :], src)
            for i, n in enumerate(("ln0_w", "ln0_b", "ln1_w", "ln1_b", "ln2_w", "ln2_b")):
                load(vec_in, VR[8 * i:8 * i + 8, :], a[n].rearrange("(k p) -> k p", p=P))
            load(vec_in, VR[48:56, :], a["hg_lb"].rearrange("l (k p) -> (l k) p", p=P))
            load(vec_in, VR[56:57, :], a["hg_norm_w"])
            load(sink_in, SINK[:], a["sink_rows"])
            load(attc_in, NEGD[:], a["c_negd"])
            load(attc_in, NEGS[:], a["c_negs"])
            load(cache_in, KC[:], a["cache_k"].rearrange("b s f -> s b f"))
            load(cache_in, VC[:], a["cache_v"].rearrange("b s f -> s b f"))
            load(mask_in, MASKS[:], a["c_masks"])
            load(cache_moved, outs_["k_win_s"][:, 0:WIN - NS, :], a["cache_k"][:, NS:WIN, :])
            load(cache_moved, outs_["v_win_s"][:, 0:WIN - NS, :], a["cache_v"][:, NS:WIN, :])

            def load_ring(i):
                if 4 <= i < 12:
                    pool.wait_ge(memK_turned, i - 3)
                elif 12 <= i < 15:
                    pool.wait_ge(ring_used, i - 11)
                elif i == 15:
                    pool.wait_ge(pv_ready, att_no["ms", 0] + 1)
                src = a["mem_k_s"] if i < 8 else a["mem_v_s"]
                load(ring_in[i % 4], RING[i % 4][:], src[i % 8].rearrange("(c p) n -> p c n", p=P))

            for i in range(4):
                load_ring(i)
            for j in range(4):
                out_saved(pool, ("sq", j, 1))
            pool.tensor_copy(QSB[:].rearrange("p b (j i) -> p b j i", j=4),
                             SQ[:, :, SEQ:T].rearrange("p j (b i) -> p b j i", b=NB)).then_inc(sample_q, 1)
            for idx in range(8):
                saved(pool, "turn_mem", idx)
            for name, buf in (("mem_k_p", MKTM), ("mem_v_p", MV)):
                load(kv_stored, outs_[name].rearrange("(c p) n -> p c n", p=P), buf[:])
            saved(pool, "turn", "sk", 0, 0)
            saved(pool, "turn", "sk", 0, 1)
            load(kv_stored, outs_["k_win_p"], SKTM[:, 0, :])
            load(kv_stored, outs_["k_win_s"][:, WIN - NS:WIN, :], SKTM[0:64, 1, :])
            saved(pool, "turn", "sv", 0, 0)
            saved(pool, "turn", "sv", 0, 1)
            load(kv_stored, outs_["v_win_p"], SV[:, 3, :])
            load(kv_stored, outs_["v_win_s"][:, WIN - NS:WIN, :], SV[0:64, NBLK, :])
            pool.wait_ge(kv_stored, 96)
            pool.memset(QM[:], 0.0).then_inc(pool_step, 1)
            pool.wait_ge(pool_step, 1)
            for h in range(4):
                out_saved(pool, ("mq", h, 1))
            for b in range(NB):
                o8 = NS * (b % 4)
                pool.tensor_copy(QM[:, b, :, o8:o8 + NS], MQ[:, :, SEQ + NS * b:SEQ + NS * b + NS])\
                    .then_inc(qm_ready, 1)
            for i in range(4, 16):
                load_ring(i)
            pool.wait_ge(pv_ready, n_att)
            for h in range(4):
                no = hg_no["h", NBLK, h]
                load(state_in, SIN[:], a["state_in"][:, h].rearrange("b d e -> d b e"))
                if h == 0:
                    for hh in range(4):
                        saved(pool, "state", hg_no["h", NBLK - 1, hh])
                    load(prompt_state_out, outs_["state_p"].rearrange("h d e -> d h e"), STATE[:])
                pool.wait_ge(ho_ready, no + 1)
                saved(pool, "state", no, 0)
                saved(pool, "state", no, 1)
                load(state_out, outs_["state_s"][:, h].rearrange("b d e -> d b e"), SOUT[:])
            i = 0
            for half in range(2):
                for t0, n in OUT_CHUNKS[half]:
                    saved(pool, "outT", i, 0)
                    saved(pool, "outT", i, 1)
                    dst = outs_["y_p"][t0:t0 + n, :] if t0 < SEQ else outs_["y_s"]
                    load(out_dma[i % 2], dst, OUTT[i % 2][0:n, :])
                    i += 1
            pool.wait_ge(cache_moved, 32)
            pool.wait_ge(kv_stored, 96)
            pool.wait_ge(prompt_state_out, 16)
            pool.wait_ge(state_out, 64)
            for s in out_dma:
                pool.wait_ge(s, 48)

        @block.scalar
        def _(act):
            steps = [0]
            ex_use = [0, 0]
            n_tanh = {}
            n_turn = [0]

            def wait_gate_free(key):
                kind, idx, half = key
                if kind == "fg":
                    if idx >= 2:
                        out_saved(act, ("fu", idx - 2, half))
                        act.wait_ge(hidden_done, 2 * (idx - 2) + half + 1)
                elif idx >= 2:
                    act.wait_ge(gate_used, gate_used_no["up" + kind[4], idx - 2, half])
                elif kind != "gate0":
                    act.wait_ge(gate_used, gate_used_no["up" + str(int(kind[4]) - 1), KT - 2 + idx, half])

            def step(ins):
                steps[0] += 1
                ins.then_inc(act_step, 1)
                act.wait_ge(act_step, steps[0])

            def copy(dst, src):
                return act.activation(dst, src, ACT.Copy)

            def main(key):
                kind, idx, half = key
                no = OUT_NO[key]
                b = main_bank(key)
                bank = BANK[b][:, 0:TH]
                cols = slice(half * TH, half * TH + TH)
                if kind == "mem":
                    act.wait_ge(out_ready, no + 1)
                    dst = MKT[:, idx, :] if idx < 4 else FT[0][:, 0:MEM]
                    copy(dst, BANK[b][:, 0:MEM]).then_inc(bank_free[b], 1)
                elif kind in ("sq", "mq", "sk", "sv", "hi"):
                    act.wait_ge(out_ready, no + 1)
                    dst = {"sq": SQ, "mq": MQ}[kind][:, idx, cols] if kind in ("sq", "mq") else \
                        (SK[:, cols] if kind == "sk" else FT[idx % 2][:, cols])
                    copy(dst, bank).then_inc(bank_free[b], 1)
                elif kind == "hf":
                    act.wait_ge(out_ready, no + 1)
                    if ex_use[half]:
                        act.wait_ge(ex_free[half], ex_use[half])
                    ex_use[half] += 1
                    act.activation(EX[half][:], bank, ACT.Exp, scale=-1.0).then_inc(bank_free[b], 1)
                elif kind in SILU or kind[:4] == "gate":
                    act.wait_ge(out_ready, no + 1)
                    n_tanh[kind] = n_tanh.get(kind, 0) + 1
                    if kind == "fg" and idx == 0:
                        act.wait_ge(ln_lo, 2 * KT)
                    if kind in ("fg", "gate0", "gate1", "gate2"):
                        wait_gate_free(key)
                    act.activation(sig_dst(key), bank, ACT.Tanh, scale=0.5)\
                        .then_inc(silu_tanh if kind in SILU else bank_free[b], 1)

            def softmax_exp(u):
                kind, no = u[0], att_no[u]
                st = ST[:, no % 2]
                if kind == "ms":
                    for bl in range(4):
                        b = 4 * u[1] + bl
                        act.wait_ge(memK_turned, b + 1)
                        if bl:
                            act.wait_ge(mkb_used, 3 * u[1] + bl)
                        elif u[1]:
                            act.wait_ge(scores_ready, no)
                        for s in range(2):
                            copy(MKB[:, 2 * s:2 * s + 2, :].rearrange("p h t -> p (h t)"), BANK[T0_ + s][:, :])\
                                .then_inc(bank_free[T0_ + s], 1)
                act.wait_ge(max_ready, no + 1)
                lo, w = lo_of(u), {"ws": 192}.get(kind, 256)
                if kind[0] == "w":
                    act.activation(st[:, 16:20], st[:, 8:12], ACT.Exp, scale=0.125)
                    for s in range(4):
                        x = XP[:, no % 2, s, lo:w]
                        ins = act.activation(x, x, ACT.Exp, bias=st[:, 4 + s:5 + s], scale=0.125,
                                             accum_out=st[:, 12 + s:13 + s])
                    ins.then_inc(p_exp, 1)
                else:
                    for s in range(4 if kind == "mp" else 1):
                        src = BANK[S0_ + s // 2][:, 256 * (s % 2):256 * (s % 2) + 256]
                        ins = act.activation(XP[:, no % 2, s, :], src, ACT.Exp, bias=st[:, 4 + s:5 + s],
                                             scale=P ** -0.5, accum_out=st[:, 12 + s:13 + s])
                        if s % 2 or kind == "ms":
                            ins.then_inc(bank_free[S0_ + s // 2], 1)

            def save_probs_T(u):
                kind, no = u[0], att_no[u]
                act.wait_ge(pT_ready, no + 1)
                if no:
                    act.wait_ge(pv_ready, no)
                ptf = PT[:].rearrange("p a c t -> p (a c t)")
                if kind == "ws":
                    copy(ptf[:, 0:512], BANK[T0_][:, :]).then_inc(bank_free[T0_], 1)
                    copy(ptf[0:64, 512:1024], BANK[T1_][0:64, :]).then_inc(bank_free[T1_], 1)
                elif kind == "ms":
                    copy(ptf[:, 0:256], BANK[T0_][:, 0:256]).then_inc(bank_free[T0_], 1)
                else:
                    c0 = lo_of(u) // P
                    for i in range(2):
                        src = BANK[T0_ + i][:, :].rearrange("p (a c t) -> p a c t", a=2, c=2)
                        copy(PT[:, 2 * i:2 * i + 2, c0:2, :], src[:, :, c0:2, :]).then_inc(bank_free[T0_ + i], 1)

            def save_values(u):
                kind, no = u[0], att_no[u]
                act.wait_ge(pv_ready, no + 1)
                bank = BANK[V_]
                if kind == "w":
                    n, g = u[1:]
                    ins = copy(SQ[:, 2 * g:2 * g + 2, P * n:P * n + P],
                               bank[:, 0:256].rearrange("p (j t) -> p j t", j=2))
                elif kind == "ws":
                    ins = copy(SQ[:, :, SEQ:T].rearrange("p j (b i) -> p b j i", b=NB),
                               bank[:, 0:256].rearrange("p (b j i) -> p b j i", b=NB, j=4))
                elif kind == "mp":
                    n = u[1]
                    ins = copy(MQ[:, :, P * n:P * n + P], bank[:, :].rearrange("p (h t) -> p h t", h=4))
                else:
                    c0 = SEQ + 32 * u[1]
                    ins = copy(MQ[:, :, c0:c0 + 32], bank[:, 0:P].rearrange("p (h t) -> p h t", h=4))
                ins.then_inc(bank_free[V_], 1)

            def hgrn_decays(u):
                _, n, h = u
                no = hg_no[u]
                t0, w, levels = hg_cols(n)
                nl = len(levels)
                act.wait_ge(d_ready, no + 1)
                if no == 0:
                    act.wait_ge(kv_stored, 96)
                act.activation(QE[:, 0:w], HB[:, h, t0:t0 + w], ACT.Exp)
                if n < NBLK:
                    act.activation(EBL[:, no % 4, 0:1], HB[:, h, t0 + P - 1:t0 + P], ACT.Exp)
                else:
                    act.activation(EBL[:, no % 4, :], HB[:, h, t0 + NS - 1:t0 + w:NS], ACT.Exp)
                parts = [E[:, :, :]] if n < NBLK else [E[:, 0:nl, 0:w], E[:, 7:8, 0:w]]
                for part in parts:
                    step(act.activation(part, part, ACT.Abs))
                for i, part in enumerate(parts):
                    ins = act.activation(part, part, ACT.Exp, scale=-1.0)
                ins.then_inc(e_ready, 1)
                act.wait_ge(kT_ready, no + 1)
                copy(KTM[no % 2][0:w, :], BANK[T0_][0:w, 0:P]).then_inc(bank_free[T0_], 1)

            def split(u):
                act.wait_ge(raw_in[u % 3], raw_full[u])
                if u >= 2:
                    unit_used(act, u - 2)
                n = unit_tiles(u)
                copy(WH[u % 2][:, 0:n, :], RAW[u % 3][:, 0:n, :]).then_inc(w_hi, 1)

            for s in SCHEDULE:
                what, rest = s[0], s[1:]
                if what == "out":
                    main(rest)
                elif what == "split":
                    split(rest[0])
                elif what == "setup":
                    act.wait_ge(vecT_ready, 1)
                    copy(VEC[:, 0:57], BANK[V_][:, 0:57]).then_inc(bank_free[V_], 1)
                    act.wait_ge(lb_shifted, 1)
                    act.activation(LBT[:, 0:8], LBT[:, 0:8], ACT.Exp).then_inc(lb_exp, 1)
                elif what == "memx":
                    t = rest[0]
                    act.wait_ge(memT_ready, t + 1)
                    for i in range(2):
                        copy(MH[:, 4 * i:4 * i + 4, P * t:P * t + P],
                             BANK[T0_ + i][:, :].rearrange("p (k t) -> p k t", k=4)).then_inc(mem_hi_done, 1)
                elif what == "stats0":
                    act.wait_ge(x_var, 1)
                    step(act.activation(BNR[:], BNV[:, :, 1], ACT.Ln, bias=EPS[:, 0:1]))
                    act.activation(BNR[:], BNR[:], ACT.Exp, scale=-0.5).then_inc(x_rstd, 1)
                elif what == "ln0":
                    t = rest[0]
                    t0, n = TOKENS[t]
                    saved(act, "xT", t, 0)
                    saved(act, "xT", t, 1)
                    copy(XH[:, :, t0:t0 + n], XT[:, :, 0:n]).then_inc(x_hi_done, 1)
                elif what == "turn_mem":
                    idx = rest[0]
                    n_turn[0] += 1
                    act.wait_ge(turn_ready, n_turn[0])
                    dst = (MKTM if idx < 4 else MV)[:, :, P * (idx % 4):P * (idx % 4) + P]
                    copy(dst, BANK[V_][:, 0:MEM].rearrange("p (c n) -> p c n", c=2)).then_inc(bank_free[V_], 1)
                elif what == "turn":
                    kind, idx = rest
                    n_turn[0] += 1
                    act.wait_ge(turn_ready, n_turn[0])
                    b0, b1 = BANK[T0_], BANK[T1_]
                    if kind == "sk":
                        copy(SKTM[:, 0, :], b0[:, 384:512]).then_inc(bank_free[T0_], 1)
                        copy(SKTM[0:64, 1, :], b1[0:64, 0:P]).then_inc(bank_free[T1_], 1)
                    else:
                        full = SV[:, 0:4, :] if kind == "sv" else HV[:, 0:4, P * idx:P * idx + P]
                        tail = SV[0:64, 4, :] if kind == "sv" else HV[0:64, 4, P * idx:P * idx + P]
                        copy(full, b0[:, :].rearrange("p (t n) -> p t n", t=4)).then_inc(bank_free[T0_], 1)
                        copy(tail, b1[0:64, 0:P]).then_inc(bank_free[T1_], 1)
                elif what == "wk":
                    act.wait_ge(cacheT_ready, 1)
                    for i in range(2):
                        copy(KTS[:, 4 * i:4 * i + 4, :].rearrange("p b t -> p (b t)"), BANK[T0_ + i][:, :])\
                            .then_inc(bank_free[T0_ + i], 1)
                elif what == "scan":
                    j = rest[0]
                    act.wait_ge(f_ready, 2 * j + 2)
                    act.activation(HB[:, j, :], HB[:, j, :], ACT.Ln).then_inc(logf_done, 1)
                elif what == "A":
                    (hgrn_decays if rest[0] == "h" else softmax_exp)(rest)
                elif what == "B" and rest[0] != "h":
                    save_probs_T(rest)
                elif what == "C":
                    if rest[0] == "h":
                        _, n, h = rest
                        t0, w, _ = hg_cols(n)
                        act.wait_ge(ho_ready, hg_no[rest] + 1)
                        copy(HQ[:, h, t0:t0 + w], BANK[V_][:, 0:w]).then_inc(bank_free[V_], 1)
                    else:
                        save_values(rest)
                elif what == "rms_sum":
                    h = rest[0]
                    for half in range(2):
                        act.wait_ge(rms_sum, 2 * h + half + 1)
                        copy(RRS[:, 2 * h + half, :], BANK[V_][:, 0:TH]).then_inc(bank_free[V_], 1)
                elif what == "rms":
                    h = rest[0]
                    if h == 0:
                        saved(act, "rms", 3, 1)
                        for i in range(0, 8, 2):
                            ins = act.activation(RRS[:, i:i + 2, :], RRS[:, i:i + 2, :], ACT.Ln, bias=EPS[:, 1:2],
                                                 scale=float(D // P))
                        step(ins)
                    act.activation(RRS[:, 2 * h:2 * h + 2, :], RRS[:, 2 * h:2 * h + 2, :], ACT.Exp, scale=-0.5)\
                        .then_inc(rms_rstd, 1)
                elif what == "var":
                    ln, half = rest
                    if ln > 1 or half:
                        act.wait_ge(var_ready, 2 * (ln - 1) + half)
                    for c in range(KT):
                        if c < KT - 1:
                            act.wait_ge(centered, 14 * (ln - 1) + 7 * half + c + 1)
                        else:
                            saved(act, "mean", ln, half)
                        act.activation(SQR[:, c, :], Y[:, c, half * TH:half * TH + TH], ACT.Square)\
                            .then_inc(squared, 1)
                    act.wait_ge(var_ready, 2 * (ln - 1) + half + 1)
                    act.activation(SG[half][:], BANK[T0_][:, 0:TH], ACT.Ln, bias=EPS[:, 0:1])\
                        .then_inc(bank_free[T0_], 1)
                    saved(act, "var", ln, half)
                    act.activation(SG[half][:], SG[half][:], ACT.Exp, scale=-0.5).then_inc(ln_rstd, 1)
                elif what == "norm":
                    ln, half = rest
                    cols = slice(half * TH, half * TH + TH)
                    for c in range(KT):
                        act.wait_ge(ln_scaled, 16 * (ln - 1) + 8 * half + c + 1)
                        dst = XH[:, c, cols] if ln == 1 else Y[:, c, cols]
                        act.activation(dst, Y[:, c, cols], ACT.Identity, bias=vec[f"ln{ln}_b"][:, c:c + 1])\
                            .then_inc(ln_hi, 1)
                    if ln == 2:
                        for i, (t0, n) in enumerate(OUT_CHUNKS[half]):
                            no = 3 * half + i
                            act.wait_ge(outT_ready, no + 1)
                            if no >= 2:
                                act.wait_ge(out_dma[no % 2], 16 * (no // 2))
                            copy(OUTT[no % 2][0:n, 0:512], BANK[S0_][0:n, :]).then_inc(bank_free[S0_], 1)

        @block.vector
        def _(dve):
            steps = [0]
            ex_use = [0, 0]
            n_silu = [0]

            def step(ins):
                steps[0] += 1
                ins.then_inc(dve_step, 1)
                dve.wait_ge(dve_step, steps[0])

            def main(key):
                kind, idx, half = key
                b = main_bank(key)
                bank = BANK[b][:, 0:TH]
                cols = slice(half * TH, half * TH + TH)
                if kind == "hf":
                    out_saved(dve, key)
                    dst = HB[:, idx, cols]
                    step(dve.tensor_scalar(EX[half][:], EX[half][:], 1.0, None, ALU.add))
                    dve.reciprocal(dst, EX[half][:]).then_inc(ex_free[half], 1)
                    ex_use[half] += 1
                    dve.wait_ge(ex_free[half], ex_use[half])
                    step(dve.tensor_scalar(dst, dst, LB[:, 4 + idx:5 + idx], LB[:, idx:idx + 1],
                                           ALU.mult, ALU.add))
                    dve.tensor_scalar(HK[:, idx, cols], dst, -1.0, 1.0, ALU.mult, ALU.add).then_inc(f_ready, 1)
                elif kind in SILU:
                    n_silu[0] += 1
                    dve.wait_ge(silu_tanh, n_silu[0])
                    dst = sig_dst(key)
                    dve.scalar_tensor_tensor(out=dst, in0=dst, scalar=1.0, in1=bank, op0=ALU.add, op1=ALU.mult)\
                        .then_inc(bank_free[b], 1)
                    if kind == "hq":
                        out_saved(dve, key)
                        step(dve.tensor_scalar(dst, dst, 0.5, None, ALU.mult))
                elif kind[:2] == "up":
                    dve.wait_ge(out_ready, OUT_NO[key] + 1)
                    gate = SG[2 * (idx % 2) + half][:]
                    out_saved(dve, ("gate" + kind[2], idx, half))
                    dst = MIX[:, idx, cols]
                    if kind == "up0":
                        dst_ = dst
                    else:
                        dst_ = gate
                    dve.scalar_tensor_tensor(out=dst_, in0=gate, scalar=1.0, in1=bank, op0=ALU.add, op1=ALU.mult)\
                        .then_inc(bank_free[b], 1)
                    out_saved(dve, key)
                    if kind == "up0":
                        dve.engine_nop().then_inc(gate_used, 1)
                    else:
                        dve.tensor_tensor(dst, dst, gate, ALU.add).then_inc(gate_used, 1)
                elif kind == "fu":
                    dve.wait_ge(out_ready, OUT_NO[key] + 1)
                    gate = SG[2 * (idx % 2) + half][:]
                    out_saved(dve, ("fg", idx, half))
                    dve.scalar_tensor_tensor(out=gate, in0=gate, scalar=0.5, in1=bank, op0=ALU.mult, op1=ALU.mult)\
                        .then_inc(bank_free[b], 1)
                    out_saved(dve, key)
                    step(dve.tensor_copy(GH[:, idx, cols], gate))
                    dve.tensor_tensor(GL[:, idx, cols], gate, f32(GH[:, idx, cols]), ALU.subtract)\
                        .then_inc(hidden_done, 1)
                elif kind in ("o", "y"):
                    dve.wait_ge(out_ready, OUT_NO[key] + 1)
                    if key == ("o", 0, 0):
                        dve.wait_ge(state_out, 64)
                        dve.wait_ge(prompt_state_out, 16)
                    y = Y[:, idx, cols]
                    dve.scalar_tensor_tensor(out=y, in0=f32(XH[:, idx, cols]), scalar=ALPHA, in1=bank,
                                             op0=ALU.mult, op1=ALU.add).then_inc(bank_free[b], 1)
                    out_saved(dve, key)
                    dve.scalar_tensor_tensor(out=y, in0=f32(XL[:, idx, cols]), scalar=ALPHA, in1=y,
                                             op0=ALU.mult, op1=ALU.add).then_inc(y_ready, 1)

            def softmax_max(u):
                kind, no = u[0], att_no[u]
                st = ST[:, no % 2]
                x = XP[:, no % 2]
                dve.wait_ge(scores_ready, no + 1)
                if no >= 2:
                    dve.wait_ge(pT_ready, no - 1)
                if kind[0] == "w":
                    lo, w = lo_of(u), {"ws": 192}.get(kind, 256)
                    for s in range(4):
                        kv, jj = s // 2, s % 2
                        if kind == "w":
                            bias, slope = NEGD[:, lo:w], 8.0 * 2.0 ** -(2 * u[2] + jj + 4 * kv + 1)
                            src = BANK[S0_ + kv][:, 256 * jj + lo:256 * jj + 256]
                        else:
                            bias, slope = NEGS[:, s, :], SMALL[:, 0:1]
                            src = BANK[S0_ + kv][:, 192 * jj:192 * jj + 192]
                        ins = dve.scalar_tensor_tensor(out=x[:, s, lo:w], in0=bias, scalar=slope, in1=src,
                                                       op0=ALU.mult, op1=ALU.add)
                        if jj:
                            ins.then_inc(bank_free[S0_ + kv], 1)
                    saved(dve, "scores", no, 0)
                    saved(dve, "scores", no, 1)
                    step(dve.tensor_reduce(st[:, 0:4], x[:, :, lo:w], AX.X, ALU.max))
                    sink = SINK[:, 4 * u[2]:4 * u[2] + 4] if kind == "w" else SINK[:, 8:9].to_broadcast([P, 4])
                    step(dve.tensor_tensor(st[:, 0:4], st[:, 0:4], sink, ALU.max))
                    dve.tensor_tensor(st[:, 8:12], sink, st[:, 0:4], ALU.subtract)
                    dve.tensor_scalar(st[:, 4:8], st[:, 0:4], -0.125, None, ALU.mult).then_inc(max_ready, 1)
                else:
                    nbank = 2 if kind == "mp" else 1
                    for i in range(nbank):
                        src = BANK[S0_ + i][:, :].rearrange("p (s k) -> p s k", s=2)[:, 0:nbank]
                        ins = dve.tensor_reduce(st[:, 2 * i:2 * i + nbank], src, AX.X, ALU.max)
                    step(ins)
                    ns = nbank * nbank
                    dve.tensor_scalar(st[:, 4:4 + ns], st[:, 0:ns], -(P ** -0.5), None, ALU.mult)\
                        .then_inc(max_ready, 1)

            def softmax_divide(u):
                kind, no = u[0], att_no[u]
                st = ST[:, no % 2]
                ns = 1 if kind == "ms" else 4
                lo, w = lo_of(u), {"ws": 192}.get(kind, 256)
                if kind[0] == "w":
                    dve.wait_ge(p_exp, n_window_exps[u])
                    step(dve.tensor_tensor(st[:, 20:24], st[:, 12:16], st[:, 16:20], ALU.add))
                    step(dve.reciprocal(st[:, 24:28], st[:, 20:24]))
                else:
                    saved(dve, "scores", no, 0)
                    if kind == "mp":
                        saved(dve, "scores", no, 1)
                    step(dve.reciprocal(st[:, 24:24 + ns], st[:, 12:12 + ns]))
                x = XP[:, no % 2, 0:ns, lo:w]
                dve.tensor_tensor(x, x, bcast(st[:, 24:24 + ns], w - lo), ALU.mult).then_inc(p_ready, 1)

            window_units = [u for u in att_units if u[0][0] == "w"]
            n_window_exps = {u: i + 1 for i, u in enumerate(window_units)}

            def hgrn_prepare(u):
                _, n, h = u
                no = hg_no[u]
                t0, w, levels = hg_cols(n)
                nl = len(levels)
                b = HB[:, h, t0:t0 + w]
                if no == 0:
                    dve.wait_ge(pv_ready, n_att)
                    dve.wait_ge(kv_stored, 96)
                    dve.wait_ge(mask_in, 16)
                    for hh in range(4):
                        saved(dve, "turn", "hi", hh, 0)
                for i, m in enumerate(levels):
                    v = level_view(b, m)
                    dve.tensor_tensor(level_view(E[:, i, 0:w], m), v,
                                      v[:, :, m - 1:m].to_broadcast([P, w // (2 * m), 2 * m]), ALU.subtract)
                c = w if n < NBLK else NS
                v = b.rearrange("p (b m) -> p b m", m=c)
                dve.tensor_tensor(E[:, 7, 0:w].rearrange("p (b m) -> p b m", m=c), v,
                                  v[:, :, c - 1:c].to_broadcast([P, w // c, c]), ALU.subtract).then_inc(d_ready, 1)
                k, q = HK[:, h, t0:t0 + w], HQ[:, h, t0:t0 + w]
                dve.wait_ge(e_ready, no + 1)
                if no:
                    dve.wait_ge(kT_ready, no)
                if n < NBLK:
                    dve.tensor_tensor(EK[:, :, :], E[:, :, :], over(k, 8), ALU.mult)
                else:
                    dve.tensor_tensor(EK[:, 0:nl, 0:w], E[:, 0:nl, 0:w], over(k, nl), ALU.mult)
                    dve.tensor_tensor(EK[:, 7, 0:w], E[:, 7, 0:w], k, ALU.mult)
                dve.tensor_tensor(QW[no % 2][:, 0:w], QE[:, 0:w], q, ALU.mult)
                dve.tensor_tensor(EQ[:, 0:nl, 0:w], E[:, 0:nl, 0:w], over(q, nl), ALU.mult).then_inc(ekq_ready, 1)

            def hgrn_mask(u):
                _, n, h = u
                no = hg_no[u]
                _, w, levels = hg_cols(n)
                nl = len(levels)
                dve.wait_ge(a_ready, no + 1)
                if n < NBLK:
                    for i in range(2):
                        src = BANK[S0_ + i][:, :].rearrange("p (l t) -> p l t", l=4)
                        dve.tensor_tensor(AM[:, 4 * i:4 * i + 4, :], src, MASKS[:, 4 * i:4 * i + 4, :], ALU.mult)\
                            .then_inc(bank_free[S0_ + i], 1)
                        saved(dve, "a", no, i)
                else:
                    src = BANK[S0_][:, :].rearrange("p (l t) -> p l t", l=4)
                    dve.tensor_tensor(AM[0:w, 0:4, 0:w], src[0:w, :, 0:w], MASKS[0:w, 4:8, 0:w], ALU.mult)\
                        .then_inc(bank_free[S0_], 1)
                    saved(dve, "a", no, 0)
                    if h:
                        dve.wait_ge(ho_ready, no)
                    dve.tensor_tensor(VB[:, :, :], over(HV[0:w, n, P * h:P * h + P], NB),
                                      bcast(SMALL[0:w, 1:9], P), ALU.mult).then_inc(vb_ready, 1)
                if no:
                    dve.wait_ge(ho_ready, no)
                dve.tensor_reduce(ASB[0:w, 0:w], AM[0:w, 0:nl + 1, 0:w].rearrange("p l t -> p t l"), AX.X, ALU.add)\
                    .then_inc(a_sum, 1)

            def hgrn_state(u):
                _, n, h = u
                no = hg_no[u]
                dve.wait_ge(ho_ready, no + 1)
                if n == 0:
                    dve.tensor_copy(STATE[:, h, :], BANK[T1_][:, 0:P]).then_inc(bank_free[T1_], 1)
                elif n < NBLK:
                    dve.scalar_tensor_tensor(out=STATE[:, h, :], in0=STATE[:, h, :], scalar=EBL[:, no % 4, 0:1],
                                             in1=BANK[T1_][:, 0:P], op0=ALU.mult, op1=ALU.add)\
                        .then_inc(bank_free[T1_], 1)
                else:
                    if h:
                        dve.wait_ge(state_out, 16 * h)
                    step(dve.tensor_tensor(SOUT[:], SIN[:], bcast(EBL[:, no % 4, :], P), ALU.mult))
                    for i in range(2):
                        o = SOUT[:, 4 * i:4 * i + 4, :]
                        dve.tensor_tensor(o, o, BANK[T0_ + i][:, :].rearrange("p (b e) -> p b e", b=4), ALU.add)\
                            .then_inc(bank_free[T0_ + i], 1)

            def split(u):
                dve.wait_ge(w_hi, u + 1)
                n = unit_tiles(u)
                dve.tensor_tensor(WL[u % 2][:, 0:n, :], RAW[u % 3][:, 0:n, :], f32(WH[u % 2][:, 0:n, :]),
                                  ALU.subtract).then_inc(w_lo, 1)

            for s in SCHEDULE:
                what, rest = s[0], s[1:]
                if what == "out":
                    main(rest)
                elif what == "split":
                    split(rest[0])
                elif what == "setup":
                    dve.memset(ONES[:], 1.0 / D)
                    dve.memset(EPS[:, 0:1], LN_EPS)
                    dve.memset(EPS[:, 1:2], RMS_EPS)
                    step(dve.memset(RST[:], 1.0))
                    dve.memset(RST[:, 0:SEQ:P], 0.0)
                    dve.memset(RST[:, SEQ:T:NS], 0.0)
                    dve.wait_ge(sink_in, 16)
                    step(dve.tensor_scalar(SINK[:], SINK[:], 8.0, None, ALU.mult))
                    saved(dve, "vec")
                    lb = vec["hg_lb"]
                    step(dve.tensor_tensor(LBT[:, 8:12], lb[:, 0:4], lb[:, 4:8], ALU.max))
                    dve.tensor_tensor(LBT[:, 0:4], lb[:, 0:4], LBT[:, 8:12], ALU.subtract)
                    dve.tensor_tensor(LBT[:, 4:8], lb[:, 4:8], LBT[:, 8:12], ALU.subtract).then_inc(lb_shifted, 1)
                    dve.wait_ge(lb_exp, 1)
                    step(dve.tensor_tensor(LBT[:, 8:12], LBT[:, 0:4], LBT[:, 4:8], ALU.add))
                    step(dve.reciprocal(LBT[:, 8:12], LBT[:, 8:12]))
                    step(dve.tensor_tensor(LB[:, 0:4], LBT[:, 0:4], LBT[:, 8:12], ALU.mult))
                    step(dve.tensor_scalar(LB[:, 4:8], LB[:, 0:4], -1.0, 1.0, ALU.mult, ALU.add))
                elif what == "memx":
                    t = rest[0]
                    for i in range(2):
                        dve.wait_ge(mem_hi_done, 2 * t + i + 1)
                        sl = (slice(None), slice(4 * i, 4 * i + 4), slice(P * t, P * t + P))
                        dve.tensor_tensor(ML[sl], BANK[T0_ + i][:, :].rearrange("p (k t) -> p k t", k=4),
                                          f32(MH[sl]), ALU.subtract).then_inc(bank_free[T0_ + i], 1)
                elif what == "stats0":
                    step(dve.memset(BNV[:], 1.0))
                    for t, (_, n) in enumerate(TOKENS):
                        dve.wait_ge(xs_in[t], 16)
                        for i in range(2):
                            ins = dve.bn_stats(BNS[0:n, t, 6 * i:6 * i + 6], XS[t][0:n, 512 * i:512 * i + 512])
                        step(ins)
                        ins = dve.bn_aggr(BNV[0:n, t, :], BNS[0:n, t, :])
                    ins.then_inc(x_var, 1)
                    dve.wait_ge(x_rstd, 1)
                elif what == "ln0":
                    t = rest[0]
                    t0, n = TOKENS[t]
                    x = XS[t][0:n, :]
                    dve.tensor_scalar(x, x, BNV[0:n, t, 0:1], BNR[0:n, t:t + 1], ALU.subtract, ALU.mult)\
                        .then_inc(x_scaled, 1)
                    dve.wait_ge(xT_ready, t + 1)
                    for k in range(KT):
                        ins = dve.tensor_scalar(XT[:, k, 0:n], BANK[T0_ + k // 4][:, P * (k % 4):P * (k % 4) + n],
                                                vec["ln0_w"][:, k:k + 1], vec["ln0_b"][:, k:k + 1],
                                                ALU.mult, ALU.add)
                        if k % 4 == 3:
                            ins.then_inc(bank_free[T0_ + k // 4], 1)
                    dve.wait_ge(x_hi_done, t + 1)
                    dve.tensor_tensor(XL[:, :, t0:t0 + n], XT[:, :, 0:n], f32(XH[:, :, t0:t0 + n]), ALU.subtract)\
                        .then_inc(x_lo_done, 1)
                    if t == NBLK:
                        dve.wait_ge(attc_in, 32)
                elif what == "scan":
                    j = rest[0]
                    dve.wait_ge(logf_done, j + 1)
                    step(dve.tensor_tensor_scan(HB[:, j, :], RST[:], HB[:, j, :], 0.0, ALU.mult, ALU.add))
                elif what == "A":
                    (hgrn_prepare if rest[0] == "h" else softmax_max)(rest)
                elif what == "N":
                    (hgrn_mask if rest[0] == "h" else softmax_divide)(rest)
                elif what == "C" and rest[0] == "h":
                    hgrn_state(rest)
                elif what == "rms_sum":
                    h = rest[0]
                    if h == 0:
                        for hh in range(4):
                            saved(dve, "ho", hg_no["h", NBLK, hh])
                        dve.wait_ge(kT_ready, len(hg_units))
                    else:
                        dve.wait_ge(rms_sum, 2 * h)
                    for half in range(2):
                        o = HQ[:, h, half * TH:half * TH + TH]
                        dve.tensor_tensor(RSQ[:, half, :], o, o, ALU.mult).then_inc(rms_sq, 1)
                elif what == "rms":
                    h = rest[0]
                    dve.wait_ge(rms_rstd, h + 1)
                    o = HQ[:, h, :]
                    step(dve.scalar_tensor_tensor(out=o, in0=o, scalar=NORMW,
                                                  in1=RRS[:, 2 * h:2 * h + 2, :].rearrange("p a t -> p (a t)"),
                                                  op0=ALU.mult, op1=ALU.mult))
                    step(dve.scalar_tensor_tensor(out=o, in0=o, scalar=0.5, in1=HG[:, h, :],
                                                  op0=ALU.mult, op1=ALU.mult))
                elif what == "branch":
                    br, j = rest
                    if j == 0:
                        if br == 0:
                            saved(dve, "pv", n_att - 1)
                        else:
                            dve.wait_ge(out_ready, OUT_NO[f"up{br - 1}", KT - 1, 1] + 1)
                    src = (SQ, MQ, HQ)[br][:, j, :]
                    step(dve.tensor_copy(OSH[:, j, :], src))
                    dve.tensor_tensor(OSL[:, j, :], src, f32(OSH[:, j, :]), ALU.subtract)\
                        .then_inc(branch_split, 1)
                elif what == "mix":
                    c = rest[0]
                    if True:
                        dve.wait_ge(gate_used, gate_used_no["up2", c, 1])
                    step(dve.tensor_scalar(MIXH[:, c, :], MIX[:, c, :], 0.5, None, ALU.mult))
                    dve.scalar_tensor_tensor(out=MIXL[:, c, :], in0=MIX[:, c, :], scalar=0.5,
                                             in1=f32(MIXH[:, c, :]), op0=ALU.mult, op1=ALU.subtract)\
                        .then_inc(mix_split, 1)
                elif what == "var":
                    ln, half = rest
                    dve.wait_ge(mean_ready, 2 * (ln - 1) + half + 1)
                    for c in range(KT):
                        y = Y[:, c, half * TH:half * TH + TH]
                        dve.tensor_tensor(y, y, BANK[V_][:, 0:TH], ALU.subtract)\
                            .then_inc(centered if c < KT - 1 else bank_free[V_], 1)
                elif what == "norm":
                    ln, half = rest
                    cols = slice(half * TH, half * TH + TH)
                    dve.wait_ge(ln_rstd, 2 * (ln - 1) + half + 1)
                    saved(dve, "mean", ln, half)
                    for c in range(KT):
                        y = Y[:, c, cols]
                        dve.scalar_tensor_tensor(out=y, in0=y, scalar=vec[f"ln{ln}_w"][:, c:c + 1],
                                                 in1=SG[half][:], op0=ALU.mult, op1=ALU.mult)\
                            .then_inc(ln_scaled, 1)
                    if ln == 1:
                        for c in range(KT):
                            dve.wait_ge(ln_hi, 8 * half + c + 1)
                            dve.scalar_tensor_tensor(out=XL[:, c, cols], in0=Y[:, c, cols],
                                                     scalar=vec["ln1_b"][:, c:c + 1], in1=f32(XH[:, c, cols]),
                                                     op0=ALU.add, op1=ALU.subtract).then_inc(ln_lo, 1)
                    else:
                        for i, (t0, n) in enumerate(OUT_CHUNKS[half]):
                            no = 3 * half + i
                            dve.wait_ge(outT_ready, no + 1)
                            if no >= 2:
                                dve.wait_ge(out_dma[no % 2], 16 * (no // 2))
                            dve.tensor_copy(OUTT[no % 2][0:n, 512:1024], BANK[S1_][0:n, :])\
                                .then_inc(bank_free[S1_], 1)


def kernel(x_prompt, x_sample, cache_k_win, cache_v_win, state_hgrn, cache_mem_k, cache_mem_v, mem_prompt,
           ln0_w, ln0_b, w_in, w_up_sw, w_up_hg, w_up_mx, sw_sinks, hg_lower_bound, hg_norm_w, w_mem_kv,
           w_o, ln1_w, ln1_b, w_ffn_in, w_ffn_out, ln2_w, ln2_b):
    import concourse.bacc as bacc
    from concourse.bass_utils import run_bass_kernel_spmd

    sinks = np.asarray(sw_sinks)[0]
    order = [2 * g + jj + 4 * kv for g in range(2) for kv in range(2) for jj in range(2)]
    row = np.arange(P)
    rows = np.concatenate([np.broadcast_to(sinks[order], (P, 8)),
                           sinks[(row // 8) % 4 + 4 * ((row // 32) % 2)][:, None]], axis=1)
    data = {
        "x_prompt": np.asarray(x_prompt)[0], "x_sample": np.asarray(x_sample).reshape(NB * NS, D),
        "cache_k": np.asarray(cache_k_win)[0].reshape(NB, WIN, P),
        "cache_v": np.asarray(cache_v_win)[0].reshape(NB, WIN, P),
        "state_in": np.asarray(state_hgrn)[0],
        "mem_k_s": np.asarray(cache_mem_k)[0].reshape(NB, MEM, 512),
        "mem_v_s": np.asarray(cache_mem_v)[0].reshape(NB, MEM, 512),
        "mem_prompt": np.asarray(mem_prompt)[0],
        "ln0_w": ln0_w, "ln0_b": ln0_b, "w_in": np.asarray(w_in)[0], "w_up_sw": np.asarray(w_up_sw)[0],
        "w_up_hg": np.asarray(w_up_hg)[0], "w_up_mx": np.asarray(w_up_mx)[0], "sink_rows": rows,
        "hg_lb": hg_lower_bound, "hg_norm_w": hg_norm_w, "w_mem_kv": np.asarray(w_mem_kv)[0],
        "w_o": np.asarray(w_o)[0], "ln1_w": np.asarray(ln1_w)[0], "ln1_b": np.asarray(ln1_b)[0],
        "w_ffn_in": np.asarray(w_ffn_in)[0], "w_ffn_out": np.asarray(w_ffn_out)[0],
        "ln2_w": np.asarray(ln2_w)[0], "ln2_b": np.asarray(ln2_b)[0],
        **shape_constants(),
    }
    shapes = {
        "y_p": (SEQ, D), "y_s": (NB * NS, D), "k_win_p": (WIN, P), "v_win_p": (WIN, P), "state_p": (4, P, P),
        "mem_k_p": (MEM, 512), "mem_v_p": (MEM, 512), "k_win_s": (NB, WIN, P), "v_win_s": (NB, WIN, P),
        "state_s": (NB, 4, P, P),
    }
    nc = bacc.Bacc("TRN2", target_bir_lowering=False, num_devices=1)
    arrays, ins, outs = {}, {}, {}
    for name, value in data.items():
        value = np.ascontiguousarray(value)
        arrays[f"in_{name}"] = value
        ins[name] = nc.dram_tensor(f"in_{name}", value.shape, mybir.dt.from_np(value.dtype),
                                   kind="ExternalInput").ap()
    for name, shape in shapes.items():
        outs[name] = nc.dram_tensor(f"out_{name}", shape, F32, kind="ExternalOutput").ap()
    build_decoder_layer(nc, ins, outs)
    r = run_bass_kernel_spmd(nc, [arrays], core_ids=[0]).results[0]
    got = {name: r[f"out_{name}"] for name in shapes}
    return (got["y_p"][None], got["y_s"].reshape(NB, NS, D),
            got["k_win_p"].reshape(1, 1, WIN, 2, 64), got["v_win_p"].reshape(1, 1, WIN, 2, 64),
            got["state_p"].reshape(1, 1, 4, P, P),
            got["mem_k_p"].reshape(1, 1, MEM, 4, P), got["mem_v_p"].reshape(1, 1, MEM, 4, P),
            got["k_win_s"].reshape(1, NB, WIN, 2, 64), got["v_win_s"].reshape(1, NB, WIN, 2, 64),
            got["state_s"][None])
```

```python
from contextlib import ExitStack

import numpy as np

import concourse.bass as bass
from concourse import mybir

F32 = mybir.dt.float32
F32R = mybir.dt.float32r
BF16 = mybir.dt.bfloat16
ALU = mybir.AluOpType
ACT = mybir.ActivationFunctionType
AX = mybir.AxisListType

P = 128
D = 1024
KT = D // P
SEQ, NB, NS = 512, 8, 8
T = SEQ + NB * NS
TH = T // 2
WIN, MEM = 128, 256
NBLK = SEQ // P
FF = 2816
FT_ = FF // P
LN_EPS, RMS_EPS = 1e-5, 1e-6
ALPHA = 2.0 ** 0.25
LEVELS = [64, 32, 16, 8, 4, 2, 1]
SAMPLE_LEVELS = [4, 2, 1]
MASKED = -3.0e37
GATE_OF = (0, 2, 1)
TOKENS = [(P * t, P) for t in range(NBLK)] + [(SEQ, NB * NS)]

C_SK, C_SV, C_HQ, C_HF, C_HI, C_HG, C_MQ, C_GATE = 512, 640, 768, 1280, 1792, 2304, 2816, 3328


def shape_constants():
    i = np.arange(P)[:, None]
    j = np.arange(2 * P)[None, :]
    dist = i + P - j
    negd = np.where((dist >= 0) & (dist < WIN), -dist, MASKED).astype(np.float32)
    row = np.arange(P)
    c, jj, ii = row // 32, (row // 8) % 4, row % 8
    negs = np.full((P, 4, WIN + NB * NS), MASKED, np.float32)
    for r in range(4):
        b = 2 * r + c // 2
        past = ii[:, None] + WIN - np.arange(WIN)[None, :]
        negs[:, r, :WIN] = np.where(past < WIN, -past, MASKED)
        tok = np.arange(NB * NS)[None, :]
        own = (tok // NS == b[:, None]) & (tok % NS <= ii[:, None])
        negs[:, r, WIN:] = np.where(own, -(ii[:, None] - tok % NS), MASKED)
    head = jj + 4 * (c % 2)
    slope8 = (8.0 * 2.0 ** -(head + 1.0)).astype(np.float32)[:, None]
    s = np.arange(P)[:, None]
    t = np.arange(P)[None, :]
    masks = [(s // (2 * m) == t // (2 * m)) & (s % (2 * m) < m) & (t % (2 * m) >= m) for m in LEVELS] + [s == t]
    masks = np.stack(masks, 1).astype(np.float32)
    own8 = (np.arange(P)[:, None] // NS == np.arange(NB)[None, :]).astype(np.float32)
    return {
        "c_negd": negd, "c_negs": negs, "c_masks": masks,
        "c_small": np.concatenate([slope8, own8], 1).astype(np.float32),
        "c_ident": np.eye(P, dtype=np.float32),
    }


def halves_order(tail):
    return [(c, half) for c in range(tail) for half in range(2)] + \
        [(c, 0) for c in range(tail, KT)] + [(c, 1) for c in range(KT - 1, tail - 1, -1)]


O_TAIL, Y_TAIL = 3, 5
Y_PAIRED = [*range(Y_TAIL), KT - 1]


def ffn_order(j):
    if j == 0:
        return [("fg", 0, 0), ("fu", 0, 0), ("fg", 1, 0), ("fg", 0, 1), ("fu", 0, 1), ("fg", 1, 1)]
    if j == 1:
        return [("fu", 1, 0), ("fu", 1, 1)]
    return [(kind, j, half) for kind in ("fg", "fu") for half in range(2)]


def weight_units():
    units, outs = [], {}

    def unit(name, k0, nk, c0, nc_):
        units.append((name, k0, nk, c0, nc_))
        return len(units) - 1

    def full(kind, idx, name, c0):
        u = unit(name, 0, KT, c0, P)
        for half in range(2):
            outs[kind, idx, half] = [(u, k, k) for k in range(KT)]

    order = []

    def plan(keys):
        order.extend(keys)

    for idx in range(8):
        u = unit("mem", 0, KT, idx * P, P)
        outs["mem", idx, 0] = [(u, k, k) for k in range(KT)]
        plan([("mem", idx, 0)])
    proj = [("sq", j, None) for j in range(4)] + [("sk", 0, C_SK), ("sv", 0, C_SV)]
    for kind, c0 in (("mq", C_MQ), ("hq", C_HQ), ("hf", C_HF), ("hi", C_HI), ("hg", C_HG)):
        proj += [(kind, h, c0 + h * P) for h in range(4)]
    for kind, idx, c0 in proj:
        full(kind, idx, "sq" if kind == "sq" else "w_in", idx if kind == "sq" else c0)
        plan([(kind, idx, 0), (kind, idx, 1)])
    for br in range(3):
        for c in range(0, KT, 2):
            for cc in (c, c + 1):
                full(f"gate{br}", cc, "w_in", C_GATE + GATE_OF[br] * D + cc * P)
                plan([(f"gate{br}", cc, 0), (f"gate{br}", cc, 1)])
            u = unit(f"up{br}", 0, 4, c * P, 2 * P)
            for cc in (c, c + 1):
                for half in range(2):
                    outs[f"up{br}", cc, half] = [(u, 2 * k + cc - c, k) for k in range(4)]
                    plan([(f"up{br}", cc, half)])
    last = None
    for c, half in halves_order(O_TAIL):
        if c != last:
            u, last = unit("w_o", 0, KT, c * P, P), c
        outs["o", c, half] = [(u, k, k) for k in range(KT)]
        plan([("o", c, half)])
    for j in range(FT_):
        for kind, c0 in (("fg", j * P), ("fu", FF + j * P)):
            full(kind, j, "ffn_in", c0)
        plan(ffn_order(j))
    for c, half in halves_order(Y_TAIL):
        if c in Y_PAIRED and half:
            outs["y", c, 1] = parts
            plan([("y", c, 1)])
            continue
        parts = []
        for k0 in range(0, FT_, 8):
            nk = min(8, FT_ - k0)
            u = unit("ffn_out", k0, nk, c * P, P)
            parts += [(u, k, k0 + k) for k in range(nk)]
        outs["y", c, half] = parts
        plan([("y", c, half)])
    return units, outs, order


UNITS, OUTS, ORDER = weight_units()


def schedule():
    steps = [("init",), ("split_hi", 0), ("split_lo", 0), ("split_hi", 1), ("split_lo", 1)]
    seen = set()
    number = {}

    def out(key, late=None, extras=()):
        left, extras = [], list(extras)
        for u, _, _ in OUTS[key]:
            if u not in seen:
                seen.add(u)
                if u + 2 < len(UNITS):
                    (left if late == "all" else steps).append(("split_hi", u + 2))
                    (left if late else steps).append(("split_lo", u + 2))
                steps.extend(extras)
                extras = []
        steps.extend(extras)
        number[key] = len(number)
        steps.append(("out",) + key)
        return left

    att = [("ws",)] + [("w", n, g) for n in range(NBLK) for g in range(2)] + [("mp", n) for n in range(NBLK)]
    att += [("ms", 0), ("ms", 1)]
    hg = [None, None]
    for i, u in enumerate([("h", n, h) for n in range(NBLK + 1) for h in range(4)]):
        hg.append(u)
        if i % 5 == 4:
            hg.append(None)
    state = {"side": [], "pos": 0}

    def part(name, i):
        if 0 <= i < len(state["side"]) and state["side"][i] is not None:
            steps.append((name,) + state["side"][i])

    def slot(keys):
        s, left = state["pos"], []
        hgrn = state["side"] is hg
        if hgrn:
            if keys and OUTS[keys[0]][0][0] not in seen:
                u = OUTS[keys[0]][0][0]
                seen.add(u)
                steps.append(("split_hi", u + 2))
                left = [("split_lo", u + 2)]
            part("K", s)
            part("N", s - 1)
            part("D", s + 1)
        if keys:
            left += out(keys[0], late="lo")
        if hgrn:
            part("P", s + 1)
        part("C", s - 2)
        if not hgrn:
            part("N", s - 1)
        for key in keys[1:]:
            out(key)
        memory_sample = s < len(state["side"]) and state["side"][s] and state["side"][s][0] == "ms"
        for name, i in (("B", s - 1), ("Q", s), ("A", s)) if memory_sample else (("Q", s), ("B", s - 1), ("A", s)):
            part(name, i)
        steps.extend(left)
        state["pos"] += 1

    steps += [("memx", 0), ("x_load",), ("memx", 1)]
    for idx in range(8):
        out(("mem", idx, 0))
        steps += {1: [("stat", 0), ("stat", 1), ("stat", 2)],
                  2: [("stat", 3), ("stat", 4), ("setup",)],
                  3: [("rstd0",), ("scale0", 0), ("scale0", 1)]}.get(idx, [])
        steps.append(("turn_mem", idx))
        if idx >= 4:
            steps += [("ln0", idx - 4), ("scale0", idx - 2)] if idx < 7 else [("ln0", 3), ("ln0", 4)]
    for kind, n in (("sq", 4), ("sk", 1), ("sv", 1)):
        for j in range(n):
            out((kind, j, 0))
            out((kind, j, 1))
            if kind in ("sk", "sv"):
                steps.append(("turn", kind, j))
    steps.append(("wk",))
    state["side"], state["pos"] = att, 0
    for kind in ("mq", "hq", "hf", "hi", "hg"):
        for j in range(4):
            slot([(kind, j, 0), (kind, j, 1)])
            if kind == "hf" and j == 3:
                steps += [("scan", i) for i in range(4)]
            if kind == "hi":
                steps.append(("turn", kind, j))
    while state["pos"] < len(att) + 2:
        slot([])
    state["side"], state["pos"] = hg, 0
    for br in range(3):
        for c in range(0, KT, 2):
            for kind in (f"gate{br}", f"up{br}"):
                for cc in (c, c + 1):
                    if kind[:4] == "gate" and cc == (0 if br == 0 else 1):
                        steps += [("branch", br, j) for j in range(4)]
                    slot([(kind, cc, 0), (kind, cc, 1)])
                    after = state["pos"] - len(hg) - 2
                    if 0 <= after < 4:
                        steps.append(("rms_sum", after))
                    if after == 3:
                        steps += [("rms", h) for h in range(4)]
                    if kind == "up2":
                        steps.append(("mix", cc))

    pending = []

    def summed():
        while pending:
            steps.append(pending.pop(0))

    def mean(ln, tail, half, c):
        return ("mean", ln, half, c, c == 0, c == (tail if half else KT - 1))

    for c, half in halves_order(O_TAIL):
        out(("o", c, half))
        summed()
        pending.append(mean(1, O_TAIL, half, c))
        steps += {(KT - 1, 1): [("center", 1, 0)], (KT - 2, 1): [("var", 1, 0)],
                  (KT - 3, 1): [("norm", 1, 0)]}.get((c, half), [])
    summed()
    steps.append(("center", 1, 1))
    first = ffn_order(0)
    out(first[0])
    steps += [("var", 1, 1), ("norm", 1, 1)]
    late = [out(first[1], late="all"), out(first[2], late="all")]
    out(first[3])
    steps += late[0]
    out(first[4])
    steps += late[1]
    out(first[5])
    for j in range(1, FT_):
        for key in ffn_order(j):
            out(key)
    for c, half in halves_order(Y_TAIL):
        extras = {(KT - 2, 1): [("center", 2, 0)], (KT - 3, 1): [("var", 2, 0), ("norm", 2, 0)]}
        out(("y", c, half), extras=extras.get((c, half), ()))
        if not (c in Y_PAIRED and half):
            summed()
        pending.append(mean(2, Y_TAIL, half, c))
        if (c, half) == (KT - 1, 1):
            summed()
    summed()
    steps += [("center", 2, 1), ("store", 0), ("var", 2, 1), ("norm", 2, 1), ("store", 1)]
    return steps, number


SCHEDULE, OUT_NO = schedule()
MAIN_BANKS = 3
NRAW, NHI = 4, 3
S0_, S1_, T0_, T1_, V_ = 3, 4, 5, 6, 7
MEAN_BANK = (V_, T1_)
Y_NO = {}
for _s in SCHEDULE:
    if _s[0] == "out" and _s[1] in ("o", "y"):
        Y_NO[1 + (_s[1] == "y"), _s[3], _s[2]] = len(Y_NO) + 1

OUT_CHUNKS = {0: [(0, 128), (128, 128), (256, 32)], 1: [(288, 128), (416, 96), (512, 64)]}


def build_decoder_layer(nc, a, outs_):
    ctx = ExitStack()
    with ctx:
        place = {"at": 16512}

        def sb(name, shape, dt, offset=None):
            size = int(np.prod(shape[1:])) * mybir.dt.size(dt)
            if offset is None:
                offset = place["at"]
                place["at"] += -(-size // 32) * 32
            return nc.alloc_sbuf_tensor_at(name, list(shape), dt, offset=offset)

        def sem(name):
            return ctx.enter_context(nc.semaphore(name))

        XH = sb("x_hi", [P, KT, T], F32R)
        XL = sb("x_lo", [P, KT, T], F32R)
        raw0 = place["at"]
        RAW = [sb(f"w_raw{i}", [P, 8, P], F32) for i in range(NRAW)]
        WL = [sb(f"w_lo{i}", [P, 8, P], F32R, raw0 + 4096 * i) for i in range(NRAW)]
        WH = [sb(f"w_hi{i}", [P, 8, P], F32R) for i in range(NHI)]
        IDENT = sb("ident", [P, P], F32)
        ONES = sb("ones", [P, P], F32)
        VEC = sb("vectors", [P, 64], F32)
        SMALL = sb("small", [P, 9], F32)
        SINK = sb("sinks8", [P, 9], F32)
        LB = sb("lower_bound", [P, 8], F32)
        LBT = sb("lower_tmp", [P, 12], F32)
        EPS = sb("eps", [P, 2], F32)
        ST = sb("softmax_stats", [P, 2, 28], F32)
        BNS = sb("bn", [P, 5, 12], F32)
        BNV = sb("bn_mean_var", [P, 5, 2], F32)
        BNR = sb("bn_rstd", [P, 5], F32)
        EBL = sb("exp_b_last", [P, 4, NB], F32)
        EX = [sb(f"exp{i}", [P, TH], F32) for i in range(2)]
        sg0 = place["at"]
        SG = [sb(f"gate{i}", [P, TH], F32) for i in range(4)]
        FT = [sb(f"to_turn{i}", [P, T], F32, sg0 + 4 * T * i) for i in range(2)]
        arena = place["at"]
        MIX = sb("mix", [P, KT, T], F32)
        OSH = sb("branch_hi", [P, 4, T], F32R)
        OSL = sb("branch_lo", [P, 4, T], F32R)
        o = arena
        XP = sb("probs", [P, 2, 4, 2 * P], F32, o); o += 8192
        PT = sb("probs_T", [P, 4, 2, P], F32, o); o += 4096
        NEGD = sb("negd", [P, 2 * P], F32, o); o += 1024
        NEGS = sb("negs", [P, 4, WIN + NB * NS], F32, o); o += 3072
        RING = [sb(f"mem_ring{i}", [P, 2, 512], F32, o + 4096 * i) for i in range(4)]; o += 16384
        QM = sb("q_masked", [P, NB, 4, 32], F32, o)
        MKTM = sb("mem_k_tokens", [P, 2, 512], F32, o)
        proj0 = place["at"]
        SQ = sb("sq", [P, 4, T], F32)
        MQ = sb("mq", [P, 4, T], F32)
        HQ = sb("hq", [P, 4, T], F32)
        HB = sb("hb", [P, 4, T], F32)
        HK = sb("hk", [P, 4, T], F32)
        HV = sb("hv", [P, NBLK + 1, 512], F32)
        HG = sb("hg", [P, 4, T], F32)
        skv = place["at"]
        SK = sb("sk", [P, T], F32)
        SV = sb("sv", [P, NBLK + 1, P], F32)
        mkv = place["at"]
        MKT = sb("mem_kT", [P, 4, MEM], F32)
        MV = sb("mem_v", [P, 2, 512], F32)
        hq0 = proj0 + 2 * 4 * T * 4
        MX = [sb(f"mem_x{i}", [P, D], F32, hq0 + 4096 * i) for i in range(2)]
        MH = sb("mem_hi", [P, KT, MEM], F32R, hq0 + 8192)
        ML = sb("mem_lo", [P, KT, MEM], F32R, hq0 + 16384)
        hv0 = hq0 + 3 * 4 * T * 4
        XS = [sb(f"x_tokens{i}", [P, D], F32, arena + 4096 * i if i < 3 else hv0 + 4096 * (i - 3))
              for i in range(5)]
        hg0 = hv0 + (NBLK + 1) * 512 * 4
        XT = [sb(f"x_normed{i}", [P, KT, P], F32, hg0 + 4096 * i) for i in range(2)]
        VR = sb("vector_rows", [64, P], F32, hg0 + 8192)
        E = [sb(f"decay{i}", [P, 8, P], F32, proj0 + 4096 * i) for i in range(2)]
        ASB = [sb(f"a_sum{i}", [P, P], F32, proj0 + 8192 + 512 * i) for i in range(2)]
        hs = place["at"]
        AM = sb("a_masked", [P, 8, P], F32)
        EK = sb("decay_k", [P, 8, P], F32)
        EQ = sb("decay_q", [P, 8, P], F32)
        QE = sb("exp_b", [P, P], F32)
        QW = [sb(f"q_exp_b{i}", [P, P], F32) for i in range(3)]
        KTM = [sb(f"k_tokens{i}", [P, P], F32) for i in range(2)]
        RRS = sb("rms_rstd", [P, 8, TH], F32, hs)
        RSQ = sb("rms_squares", [P, 2, TH], F32, hs + 8 * TH * 4)
        MASKS = sb("masks", [P, 8, P], F32)
        RST = sb("reset", [P, T], BF16)
        STATE = sb("state", [P, 4, P], F32)
        KC = sb("win_k", [P, NB, P], F32, hs)
        VC = sb("win_v", [P, NB, P], F32, hs + 4096)
        KTS = sb("win_kT", [P, NB, P], F32, hs + 8192)
        MKB = [sb(f"mem_kT_batch{i}", [P, 4, MEM], F32, hs + 4096 * i) for i in range(2)]
        SKTM = sb("sk_tokens", [P, 2, P], F32, hs + 12288)
        QSB = sb("sample_q", [P, NB, 32], F32, hs + 13312)
        SIN = sb("sample_state", [P, NB, P], F32, mkv)
        SOUT = sb("sample_state_new", [P, NB, P], F32, mkv + 4096)
        VB = sb("v_by_batch", [64, NB, P], F32, skv)
        assert place["at"] <= 229368, place["at"]
        MIXH = sb("mix_hi", [P, KT, T], F32R, proj0)
        MIXL = sb("mix_lo", [P, KT, T], F32R, proj0 + KT * T * 4)
        GH = sb("hidden_hi", [P, FT_, T], F32R, arena)
        GL = sb("hidden_lo", [P, FT_, T], F32R, arena + FT_ * T * 4)
        o = arena + 2 * FT_ * T * 4
        Y = sb("pre_norm", [P, KT, T], F32, o); o += KT * T * 4
        SQR = sb("squares", [P, KT, TH], F32, o); o += KT * TH * 4
        OUTT = [sb(f"out_tokens{i}", [P, D], F32, o + 4096 * i) for i in range(2)]
        assert o + 8192 <= 229368

        BANK = [ctx.enter_context(nc.psum_tensor(f"bank{i}", [P, 512], F32)) for i in range(8)]

        raw_in = [sem(f"raw_in{i}") for i in range(NRAW)]
        w_hi, w_lo, w_used, out_ready = sem("w_hi"), sem("w_lo"), sem("w_used"), sem("out_ready")
        bank_free = [sem(f"bank_free{i}") for i in range(8)]
        dve_step, act_step, pool_step = sem("dve_step"), sem("act_step"), sem("pool_step")
        silu_tanh, gate_used, ex_free = sem("silu_tanh"), sem("gate_used"), [sem(f"ex_free{i}") for i in range(2)]
        ident_in, vec_in, sink_in, attc_in, mask_in = (
            sem(n) for n in ("ident_in", "vec_in", "sink_in", "attc_in", "mask_in"))
        memx_in = [sem(f"memx_in{i}") for i in range(2)]
        xs_in = [sem(f"xs_in{i}") for i in range(5)]
        vecT_ready, setup_done, lb_shifted, lb_exp = (
            sem(n) for n in ("vecT_ready", "setup_done", "lb_shifted", "lb_exp"))
        x_var, x_rstd, x_scaled, xT_ready, x_lo_done = (
            sem(n) for n in ("x_var", "x_rstd", "x_scaled", "xT_ready", "x_lo_done"))
        memT_ready, mem_hi_done, turn_ready = sem("memT_ready"), sem("mem_hi_done"), sem("turn_ready")
        f_ready, logf_done = sem("f_ready"), sem("logf_done")
        cache_in, cacheT_ready, sample_q = sem("cache_in"), sem("cacheT_ready"), sem("sample_q")
        ring_in = [sem(f"ring_in{i}") for i in range(4)]
        ring_used, memK_turned, mkb_used, qm_ready = (
            sem(n) for n in ("ring_used", "memK_turned", "mkb_used", "qm_ready"))
        scores_ready, max_ready, p_exp, p_ready, pT_ready, pv_ready = (
            sem(n) for n in ("scores_ready", "max_ready", "p_exp", "p_ready", "pT_ready", "pv_ready"))
        d_ready, e_ready, ekq_ready, a_ready, a_sum, kT_ready, ho_ready = (
            sem(n) for n in ("d_ready", "e_ready", "ekq_ready", "a_ready", "a_sum", "kT_ready", "ho_ready"))
        state_in, vb_ready, state_out, kv_stored = (
            sem(n) for n in ("state_in", "vb_ready", "state_out", "kv_stored"))
        rms_sq, rms_sum, rms_rstd, branch_split = (
            sem(n) for n in ("rms_sq", "rms_sum", "rms_rstd", "branch_split"))
        mix_split, y_ready, mean_ready, centered, squared, var_ready, ln_rstd = (
            sem(n) for n in ("mix_split", "y_ready", "mean_ready", "centered", "squared", "var_ready", "ln_rstd"))
        hidden_done, ln_scaled, ln_hi, ln_lo, outT_ready = (
            sem(n) for n in ("hidden_done", "ln_scaled", "ln_hi", "ln_lo", "outT_ready"))
        out_dma = [sem(f"out_dma{i}") for i in range(2)]
        cache_moved, prompt_state_out = sem("cache_moved"), sem("prompt_state_out")

        vec = {n: VEC[:, 8 * i:8 * i + 8] for i, n in
               enumerate(("ln0_w", "ln0_b", "ln1_w", "ln1_b", "ln2_w", "ln2_b", "hg_lb"))}
        NORMW = VEC[:, 56:57]
        att_units = [s[1:] for s in SCHEDULE if s[0] == "A" and s[1] != "h"]
        att_no = {u: i for i, u in enumerate(att_units)}
        n_att = len(att_units)
        hg_units = [s[1:] for s in SCHEDULE if s[0] == "A" and s[1] == "h"]
        hg_no = {u: i for i, u in enumerate(hg_units)}

        first_use, last_use = {}, {}
        for key in ORDER:
            for n, (u, _, _) in enumerate(OUTS[key]):
                first_use.setdefault(u, (key, n))
                last_use[u] = (key, n)
        inner_uses = [u for u in range(len(UNITS)) if last_use[u][1] < len(OUTS[last_use[u][0]]) - 1]
        inner_no = {u: i + 1 for i, u in enumerate(inner_uses)}

        def unit_used(eng, u):
            if u in inner_no:
                eng.wait_ge(w_used, inner_no[u])
            else:
                eng.wait_ge(out_ready, OUT_NO[last_use[u][0]] + 1)

        def main_bank(key):
            return OUT_NO[key] % MAIN_BANKS

        def out_saved(eng, key):
            eng.wait_ge(bank_free[main_bank(key)], OUT_NO[key] // MAIN_BANKS + 1)

        bank_use = {}

        def saved(eng, *what):
            bank, count = bank_use[what]
            eng.wait_ge(bank_free[bank], count)

        def moving(key, k):
            kind, _, half = key
            cols = slice(half * TH, half * TH + TH)
            if kind == "mem":
                return MH[:, k, :], ML[:, k, :]
            if kind[:2] == "up":
                return OSH[:, k, cols], OSL[:, k, cols]
            if kind == "o":
                return MIXH[:, k, cols], MIXL[:, k, cols]
            if kind == "y":
                return GH[:, k, cols], GL[:, k, cols]
            return XH[:, k, cols], XL[:, k, cols]

        def bcast(ap, n):
            return ap.unsqueeze(2).to_broadcast([ap.shape[0], ap.shape[1], n])

        def over(ap, n):
            return ap.unsqueeze(1).to_broadcast([ap.shape[0], n, ap.shape[1]])

        def f32(ap):
            return ap.bitcast(F32)

        def unit_source(u):
            name, k0, nk, c0, ncols = UNITS[u]
            raw = RAW[u % NRAW]
            if name == "sq":
                w = a["w_in"].rearrange("(k p) n -> p k n", p=P)
                return [(raw[:, :, 0:64], w[:, :, c0 * 64:c0 * 64 + 64]),
                        (raw[:, :, 64:128], w[:, :, (c0 + 4) * 64:(c0 + 4) * 64 + 64])]
            if name == "up0":
                w = a["w_up_sw"].rearrange("(g k p) n -> g p k n", g=2, p=64)
                v = raw[:, :, :].rearrange("p (k c) n -> p k (c n)", k=4)
                return [(v[64 * g:64 * g + 64], w[g, :, :, c0:c0 + ncols]) for g in range(2)]
            src = {"mem": "w_mem_kv", "w_in": "w_in", "up1": "w_up_mx", "up2": "w_up_hg", "w_o": "w_o",
                   "ffn_in": "w_ffn_in", "ffn_out": "w_ffn_out"}[name]
            w = a[src].rearrange("(k p) n -> p k n", p=P)[:, k0:k0 + nk, c0:c0 + ncols]
            if ncols == 2 * P:
                return [(raw[:, :, :].rearrange("p (k c) n -> p k (c n)", k=4), w)]
            return [(raw[:, 0:nk, :], w)]

        raw_count, raw_full = [0] * NRAW, {}
        for u in range(len(UNITS)):
            raw_count[u % NRAW] += 16 * len(unit_source(u))
            raw_full[u] = raw_count[u % NRAW]

        def unit_tiles(u):
            return UNITS[u][2] * UNITS[u][4] // P

        def hg_cols(n):
            return (P * n, P, LEVELS) if n < NBLK else (SEQ, NB * NS, SAMPLE_LEVELS)

        def lo_of(u):
            return P if u[:2] == ("w", 0) else 0

        def keys_free(eng, b):
            eng.wait_ge(memK_turned, b + 1)
            if b >= 2:
                last = b - 2
                if last % 4 < 3:
                    eng.wait_ge(mkb_used, 3 * (last // 4) + last % 4 + 1)
                else:
                    eng.wait_ge(scores_ready, att_no["ms", last // 4] + 1)

        SILU = ("hq", "hg", "fg")
        gate_used_no = {key: i + 1 for i, key in enumerate(k for k in ORDER if k[0][:2] == "up")}

        def sig_dst(key):
            kind, idx, half = key
            cols = slice(half * TH, half * TH + TH)
            if kind in ("hq", "hg", "hf"):
                return {"hq": HQ, "hg": HG, "hf": HB}[kind][:, idx, cols]
            return SG[2 * (idx % 2) + half][:]

        def level_view(ap, m):
            return ap.rearrange("p (b m) -> p b m", m=2 * m)

        block = ctx.enter_context(nc.Block())

        @block.tensor
        def _(pe):
            uses = [0] * 8

            def take(bank, *what):
                if uses[bank]:
                    pe.wait_ge(bank_free[bank], uses[bank])
                uses[bank] += 1
                if what:
                    bank_use[what] = (bank, uses[bank])
                return BANK[bank]

            def main(key):
                kind, idx, half = key
                if kind == "y" and idx in Y_PAIRED:
                    if half == 0:
                        main_pair(idx)
                    return
                bank = take(main_bank(key))
                if kind == "mem":
                    saved(pe, "memx", 1, 0)
                    saved(pe, "memx", 1, 1)
                elif kind[:2] == "up":
                    pe.wait_ge(branch_split, 4 * int(kind[2]) + 4)
                elif kind == "o":
                    pe.wait_ge(mix_split, KT)
                elif kind[0] == "f":
                    pe.wait_ge(ln_lo, KT * (half + 1))
                else:
                    pe.wait_ge(x_lo_done, 5 if half else 3)
                parts = OUTS[key]
                n = MEM if kind == "mem" else TH
                for i, (u, tile, k) in enumerate(parts):
                    if first_use[u] == (key, i):
                        pe.wait_ge(w_hi, u + 1)
                        pe.wait_ge(w_lo, u + 1)
                    hi, lo = moving(key, k)
                    wh, wl = WH[u % NHI][:, tile, :], WL[u % NRAW][:, tile, :]
                    pe.matmul(bank[:, 0:n], wh, lo, start=(i == 0), stop=False)
                    pe.matmul(bank[:, 0:n], wl, hi, start=False, stop=False)
                    mm = pe.matmul(bank[:, 0:n], wh, hi, start=False, stop=(i == len(parts) - 1))
                    if last_use[u] == (key, i) and u in inner_no:
                        mm.then_inc(w_used, 1)
                mm.then_inc(out_ready, 1)

            def main_pair(c):
                keys = ("y", c, 0), ("y", c, 1)
                banks = [take(main_bank(key)) for key in keys]
                parts = OUTS[keys[0]]
                pe.wait_ge(hidden_done, 2 * FT_)
                for unit in dict.fromkeys(u for u, _, _ in parts):
                    pe.wait_ge(w_hi, unit + 1)
                    pe.wait_ge(w_lo, unit + 1)
                    for half in range(2):
                        bank = banks[half]
                        for i, (u, tile, k) in enumerate(parts):
                            if u != unit:
                                continue
                            hi, lo = moving(keys[half], k)
                            wh, wl = WH[u % NHI][:, tile, :], WL[u % NRAW][:, tile, :]
                            pe.matmul(bank[:, 0:TH], wh, lo, start=(i == 0), stop=False)
                            pe.matmul(bank[:, 0:TH], wl, hi, start=False, stop=False)
                            mm = pe.matmul(bank[:, 0:TH], wh, hi, start=False, stop=(i == len(parts) - 1))
                            if last_use[u] == (keys[half], i) and u in inner_no:
                                mm.then_inc(w_used, 1)
                        if unit == parts[-1][0]:
                            mm.then_inc(out_ready, 1)

            n_ring = [0]

            def ring_tile():
                i = n_ring[0]
                pe.wait_ge(ring_in[i % 4], 16 * (i // 4 + 1))
                n_ring[0] += 1
                return RING[i % 4]

            def turn_keys(b):
                keys = ring_tile()
                for s in range(2):
                    bank = take(T0_ + s, "memK", b, s)
                    for hh in range(2):
                        for c in range(2):
                            h = 2 * s + hh
                            mm = pe.transpose(bank[:, 256 * hh + P * c:256 * hh + P * c + P],
                                              keys[:, c, P * h:P * h + P], IDENT[:])
                mm.then_inc(memK_turned, 1)

            def scores(u):
                kind, no = u[0], att_no[u]
                if kind == "w":
                    n, g = u[1:]
                    lo = lo_of(u)
                    for kv in range(2):
                        bank = take(S0_ + kv, "scores", no, kv)
                        for jj in range(2):
                            mm = pe.matmul(bank[:, 256 * jj + lo:256 * jj + 256],
                                           SQ[64 * kv:64 * kv + 64, 2 * g + jj, P * n:P * n + P],
                                           SK[64 * kv:64 * kv + 64, P * (n - 1) + lo:P * (n + 1)],
                                           start=True, stop=True)
                elif kind == "ws":
                    out_saved(pe, ("sk", 0, 1))
                    saved(pe, "cacheT", 0)
                    saved(pe, "cacheT", 1)
                    pe.wait_ge(sample_q, 1)
                    banks = [take(S0_, "scores", no, 0), take(S1_, "scores", no, 1)]
                    for kv in range(2):
                        for b in range(NB):
                            r, c = b // 2, 2 * (b % 2) + kv
                            dst = banks[r // 2][32 * c:32 * c + 32, 192 * (r % 2):192 * (r % 2) + 192]
                            q = QSB[64 * kv:64 * kv + 64, b, :]
                            pe.matmul(dst[:, 0:WIN], q, KTS[64 * kv:64 * kv + 64, b, :], start=True, stop=True)
                            mm = pe.matmul(dst[:, WIN:192], q, SK[64 * kv:64 * kv + 64, SEQ:T],
                                           start=True, stop=True)
                elif kind == "mp":
                    n = u[1]
                    out_saved(pe, ("mq", 3, 1))
                    for s in range(4):
                        if s % 2 == 0:
                            bank = take(S0_ + s // 2, "scores", no, s // 2)
                        mm = pe.matmul(bank[:, 256 * (s % 2):256 * (s % 2) + 256], MQ[:, s, P * n:P * n + P],
                                       MKT[:, s, :], start=True, stop=True)
                else:
                    pe.wait_ge(qm_ready, NB)
                    bank = take(S0_, "scores", no, 0)
                    turn_keys(4 * u[1])
                    for bl in range(4):
                        b = 4 * u[1] + bl
                        if bl < 3:
                            turn_keys(b + 1)
                        for s in range(2):
                            saved(pe, "memK", b, s)
                        for h in range(4):
                            mm = pe.matmul(bank[32 * h:32 * h + 32, 0:256], QM[:, b, h, :], MKB[b % 2][:, h, :],
                                           start=(bl == 0), stop=(bl == 3), skip_group_check=True)
                        if bl < 3:
                            mm.then_inc(mkb_used, 1)
                mm.then_inc(scores_ready, 1)

            def turn_probs(u):
                kind, no = u[0], att_no[u]
                probs = XP[:, no % 2]
                pe.wait_ge(p_ready, no + 1)
                if kind == "ws":
                    b0, b1 = take(T0_, "pT", no, 0), take(T1_, "pT", no, 1)
                    for r in range(4):
                        pe.transpose(b0[:, P * r:P * r + P], probs[:, r, 0:P], IDENT[:])
                        mm = pe.transpose(b1[0:64, P * r:P * r + P], probs[:, r, P:192], IDENT[:])
                elif kind == "ms":
                    b0 = take(T0_, "pT", no, 0)
                    for c in range(2):
                        mm = pe.transpose(b0[:, P * c:P * c + P], probs[:, 0, P * c:P * c + P], IDENT[:])
                else:
                    for s in range(4):
                        if s % 2 == 0:
                            bank = take(T0_ + s // 2, "pT", no, s // 2)
                        for c in range(lo_of(u) // P, 2):
                            col = 256 * (s % 2) + P * c
                            mm = pe.transpose(bank[:, col:col + P], probs[:, s, P * c:P * c + P], IDENT[:])
                mm.then_inc(pT_ready, 1)

            def values(u):
                kind, no = u[0], att_no[u]
                saved(pe, "pT", no, 0)
                if kind != "ms":
                    saved(pe, "pT", no, 1)
                ptf = PT[:].rearrange("p a c t -> p (a c t)")
                bank = take(V_, "pv", no)
                if kind == "w":
                    n, g = u[1:]
                    c0 = lo_of(u) // P
                    for kv in range(2):
                        for c in range(c0, 2):
                            mm = pe.matmul(bank[64 * kv:64 * kv + 64, 0:256], SV[:, n - 1 + c, 64 * kv:64 * kv + 64],
                                           PT[:, 2 * kv:2 * kv + 2, c, :], start=(c == c0), stop=(c == 1))
                elif kind == "ws":
                    for kv in range(2):
                        for b in range(NB):
                            r, c = b // 2, 2 * (b % 2) + kv
                            dst = bank[64 * kv:64 * kv + 64, 32 * b:32 * b + 32]
                            col = P * r + 32 * c
                            pe.matmul(dst, VC[:, b, 64 * kv:64 * kv + 64], ptf[:, col:col + 32],
                                      start=True, stop=False)
                            mm = pe.matmul(dst, SV[0:64, NBLK, 64 * kv:64 * kv + 64],
                                           ptf[0:64, 512 + col:512 + col + 32], start=False, stop=True)
                elif kind == "mp":
                    for h in range(4):
                        for c in range(2):
                            mm = pe.matmul(bank[:, P * h:P * h + P], MV[:, c, P * h:P * h + P], PT[:, h, c, :],
                                           start=(c == 0), stop=(c == 1))
                else:
                    for bl in range(4):
                        vals = ring_tile()
                        for h in range(4):
                            for c in range(2):
                                col = 32 * h + 8 * bl
                                mm = pe.matmul(bank[:, col:col + 8], vals[:, c, P * h:P * h + P],
                                               ptf[:, P * c + col:P * c + col + 8],
                                               start=(c == 0), stop=(c == 1))
                        if bl < 3:
                            mm.then_inc(ring_used, 1)
                mm.then_inc(pv_ready, 1)

            def hgrn_pairs(u):
                _, n, h = u
                no = hg_no[u]
                t0, w, levels = hg_cols(n)
                cols = slice(t0, t0 + w)
                nl = len(levels)
                pe.wait_ge(ekq_ready, no + 1)
                for i in range(nl + 1):
                    if i % 4 == 0:
                        bank = take(S0_ + i // 4, "a", no, i // 4)
                    k, q = (EK[:, i, 0:w], EQ[:, i, 0:w]) if i < nl else (HK[:, h, cols], HQ[:, h, cols])
                    mm = pe.matmul(bank[0:w, P * (i % 4):P * (i % 4) + w], k, q, start=True, stop=True)
                mm.then_inc(a_ready, 1)
                bank = take(T0_, "kT", no)
                pe.transpose(bank[0:w, 0:P], EK[:, 7, 0:w], IDENT[:]).then_inc(kT_ready, 1)

            def hgrn_out(u):
                _, n, h = u
                no = hg_no[u]
                _, w, _ = hg_cols(n)
                v = HV[0:w, n, P * h:P * h + P]
                pe.wait_ge(a_sum, no + 1)
                saved(pe, "kT", no)
                if n < NBLK:
                    if n:
                        saved(pe, "state", no - 4)
                    bank = take(V_, "ho", no)
                    pe.matmul(bank[:, 0:P], v, ASB[no % 2][:], start=True, stop=(n == 0))
                    if n:
                        pe.matmul(bank[:, 0:P], STATE[:, h, :], QW[no % 3][:], start=False, stop=True)
                    sbank = take(T1_, "state", no)
                    mm = pe.matmul(sbank[:, 0:P], KTM[no % 2][:], v, start=True, stop=True)
                else:
                    pe.wait_ge(state_in, 16 * (h + 1))
                    pe.wait_ge(vb_ready, h + 1)
                    bank = take(V_, "ho", no)
                    pe.matmul(bank[:, 0:w], v, ASB[no % 2][0:w, 0:w], start=True, stop=False, skip_group_check=True)
                    for b in range(NB):
                        pe.matmul(bank[:, NS * b:NS * b + NS], SIN[:, b, :], QW[no % 3][:, NS * b:NS * b + NS],
                                  start=False, stop=(b == NB - 1), skip_group_check=True)
                    for i in range(2):
                        sbank = take(T0_ + i, "state", no, i)
                        mm = pe.matmul(sbank[:, :], KTM[no % 2][0:w, :], VB[:, 4 * i:4 * i + 4, :],
                                       start=True, stop=True)
                mm.then_inc(ho_ready, 1)

            for s in SCHEDULE:
                what, rest = s[0], s[1:]
                if what == "out":
                    main(rest)
                elif what == "setup":
                    pe.wait_ge(vec_in, 128)
                    pe.transpose(take(V_, "vec")[:, 0:57], VR[0:57, :], IDENT[0:57, 0:57]).then_inc(vecT_ready, 1)
                elif what == "memx":
                    t = rest[0]
                    if t == 0:
                        pe.wait_ge(ident_in, 16)
                    pe.wait_ge(memx_in[t], 16)
                    for i in range(2):
                        bank = take(T0_ + i, "memx", t, i)
                        for k in range(4):
                            mm = pe.transpose(bank[:, P * k:P * k + P],
                                              MX[t][:, P * (4 * i + k):P * (4 * i + k) + P], IDENT[:])
                    mm.then_inc(memT_ready, 1)
                elif what == "ln0":
                    t = rest[0]
                    n = TOKENS[t][1]
                    pe.wait_ge(x_scaled, t + 1)
                    for i in range(2):
                        bank = take(T0_ + i, "xT", t, i)
                        for k in range(4):
                            mm = pe.transpose(bank[:, P * k:P * k + n],
                                              XS[t][0:n, P * (4 * i + k):P * (4 * i + k) + P],
                                              IDENT[0:n, 0:n])
                    mm.then_inc(xT_ready, 1)
                elif what == "turn_mem":
                    idx = rest[0]
                    out_saved(pe, ("mem", idx, 0))
                    src = MKT[:, idx, :] if idx < 4 else FT[0][:, 0:MEM]
                    bank = take(V_, "turn_mem", idx)
                    for c in range(2):
                        mm = pe.transpose(bank[:, P * c:P * c + P], src[:, P * c:P * c + P], IDENT[:])
                    mm.then_inc(turn_ready, 1)
                elif what == "turn":
                    kind, idx = rest
                    out_saved(pe, (kind, idx, 0))
                    out_saved(pe, (kind, idx, 1))
                    b0, b1 = take(T0_, "turn", kind, idx, 0), take(T1_, "turn", kind, idx, 1)
                    src = SK if kind == "sk" else FT[idx % 2]
                    for t, (t0, n) in enumerate(TOKENS):
                        if kind == "sk" and t < NBLK - 1:
                            continue
                        dst = b0[0:n, P * t:P * t + P] if t < NBLK else b1[0:n, 0:P]
                        mm = pe.transpose(dst, src[:, t0:t0 + n], IDENT[:])
                    mm.then_inc(turn_ready, 1)
                elif what == "wk":
                    pe.wait_ge(cache_in, 32)
                    for i in range(2):
                        bank = take(T0_ + i, "cacheT", i)
                        for k in range(4):
                            mm = pe.transpose(bank[:, P * k:P * k + P], KC[:, 4 * i + k, :], IDENT[:])
                    mm.then_inc(cacheT_ready, 1)
                elif what == "Q":
                    (hgrn_pairs if rest[0] == "h" else scores)(rest)
                elif what == "B" and rest[0] != "h":
                    turn_probs(rest)
                elif what == "C":
                    (hgrn_out if rest[0] == "h" else values)(rest)
                elif what == "rms_sum":
                    h = rest[0]
                    for half in range(2):
                        pe.wait_ge(rms_sq, 2 * h + half + 1)
                        bank = take(V_, "rms", h, half)
                        pe.matmul(bank[:, 0:TH], ONES[:], RSQ[:, half, :], start=True,
                                  stop=True).then_inc(rms_sum, 1)
                elif what == "mean":
                    ln, half, c, first, last = rest
                    pe.wait_ge(y_ready, Y_NO[ln, half, c])
                    mb = MEAN_BANK[half]
                    bank = take(mb, "mean", ln, half) if first else BANK[mb]
                    mm = pe.matmul(bank[:, 0:TH], ONES[:], Y[:, c, half * TH:half * TH + TH],
                                   start=first, stop=last)
                    if last:
                        mm.then_inc(mean_ready, 1)
                elif what == "var":
                    ln, half = rest
                    bank = take(T0_, "var", ln, half)
                    for c in range(KT):
                        pe.wait_ge(squared, 16 * (ln - 1) + 8 * half + c + 1)
                        mm = pe.matmul(bank[:, 0:TH], ONES[:], SQR[:, c, :], start=(c == 0), stop=(c == KT - 1))
                    mm.then_inc(var_ready, 1)
                elif what == "store":
                    half = rest[0]
                    for i, (t0, n) in enumerate(OUT_CHUNKS[half]):
                        for j in range(2):
                            pe.wait_ge(ln_hi, 16 + 8 * half + 4 * j + 4)
                            bank = take(S0_ + j, "outT", 3 * half + i, j)
                            for k in range(4):
                                mm = pe.transpose(bank[0:n, P * k:P * k + P], Y[:, 4 * j + k, t0:t0 + n], IDENT[:])
                        mm.then_inc(outT_ready, 1)

        @block.sync
        def _(sp):
            sp.dma_start(IDENT[:], a["c_ident"]).then_inc(ident_in, 16)
            for i in range(2):
                sp.dma_start(MX[i][:], a["mem_prompt"][P * i:P * i + P, :]).then_inc(memx_in[i], 16)
            for u in range(len(UNITS)):
                if u >= NRAW:
                    unit_used(sp, u - NRAW)
                for dst, src in unit_source(u):
                    sp.dma_start(dst, src).then_inc(raw_in[u % NRAW], 16)
            i = 0
            for half in range(2):
                for t0, n in OUT_CHUNKS[half]:
                    saved(sp, "outT", i, 0)
                    saved(sp, "outT", i, 1)
                    dst = outs_["y_p"][t0:t0 + n, :] if t0 < SEQ else outs_["y_s"]
                    sp.dma_start(dst, OUTT[i % 2][0:n, :]).then_inc(out_dma[i % 2], 16)
                    i += 1
            for s in out_dma:
                sp.wait_ge(s, 48)

        @block.gpsimd
        def _(pool):
            def load(sem_, dst, src):
                pool.dma_start(dst, src).then_inc(sem_, 16)

            for i, n in enumerate(("ln0_w", "ln0_b", "ln1_w", "ln1_b", "ln2_w", "ln2_b")):
                load(vec_in, VR[8 * i:8 * i + 8, :], a[n].rearrange("(k p) -> k p", p=P))
            load(vec_in, VR[48:56, :], a["hg_lb"].rearrange("l (k p) -> (l k) p", p=P))
            load(vec_in, VR[56:57, :], a["hg_norm_w"])
            load(sink_in, SINK[:], a["sink_rows"])
            load(attc_in, SMALL[:], a["c_small"])
            load(attc_in, NEGD[:], a["c_negd"])
            load(attc_in, NEGS[:], a["c_negs"])
            load(cache_in, KC[:], a["cache_k"].rearrange("b s f -> s b f"))
            load(cache_in, VC[:], a["cache_v"].rearrange("b s f -> s b f"))
            load(mask_in, MASKS[:], a["c_masks"])
            load(cache_moved, outs_["k_win_s"][:, 0:WIN - NS, :], a["cache_k"][:, NS:WIN, :])
            load(cache_moved, outs_["v_win_s"][:, 0:WIN - NS, :], a["cache_v"][:, NS:WIN, :])

            def load_ring(i):
                if 4 <= i < 12:
                    pool.wait_ge(memK_turned, i - 3)
                elif 12 <= i < 15:
                    pool.wait_ge(ring_used, i - 11)
                elif i == 15:
                    pool.wait_ge(pv_ready, att_no["ms", 0] + 1)
                src = a["mem_k_s"] if i < 8 else a["mem_v_s"]
                load(ring_in[i % 4], RING[i % 4][:], src[i % 8].rearrange("(c p) n -> p c n", p=P))

            for i in range(4):
                load_ring(i)
            for j in range(4):
                out_saved(pool, ("sq", j, 1))
            pool.tensor_copy(QSB[:].rearrange("p b (j i) -> p b j i", j=4),
                             SQ[:, :, SEQ:T].rearrange("p j (b i) -> p b j i", b=NB)).then_inc(sample_q, 1)
            for idx in range(8):
                saved(pool, "turn_mem", idx)
            for name, buf in (("mem_k_p", MKTM), ("mem_v_p", MV)):
                load(kv_stored, outs_[name].rearrange("(c p) n -> p c n", p=P), buf[:])
            saved(pool, "turn", "sk", 0, 0)
            saved(pool, "turn", "sk", 0, 1)
            load(kv_stored, outs_["k_win_p"], SKTM[:, 0, :])
            load(kv_stored, outs_["k_win_s"][:, WIN - NS:WIN, :], SKTM[0:64, 1, :])
            saved(pool, "turn", "sv", 0, 0)
            saved(pool, "turn", "sv", 0, 1)
            load(kv_stored, outs_["v_win_p"], SV[:, 3, :])
            load(kv_stored, outs_["v_win_s"][:, WIN - NS:WIN, :], SV[0:64, NBLK, :])
            pool.wait_ge(kv_stored, 96)
            pool.memset(QM[:], 0.0).then_inc(pool_step, 1)
            pool.wait_ge(pool_step, 1)
            for h in range(4):
                out_saved(pool, ("mq", h, 1))
            for b in range(NB):
                o8 = NS * (b % 4)
                pool.tensor_copy(QM[:, b, :, o8:o8 + NS], MQ[:, :, SEQ + NS * b:SEQ + NS * b + NS])\
                    .then_inc(qm_ready, 1)
            for i in range(4, 16):
                load_ring(i)
            pool.wait_ge(pv_ready, n_att)
            for h in range(4):
                no = hg_no["h", NBLK, h]
                load(state_in, SIN[:], a["state_in"][:, h].rearrange("b d e -> d b e"))
                if h == 0:
                    for hh in range(4):
                        saved(pool, "state", hg_no["h", NBLK - 1, hh])
                    load(prompt_state_out, outs_["state_p"].rearrange("h d e -> d h e"), STATE[:])
                pool.wait_ge(ho_ready, no + 1)
                saved(pool, "state", no, 0)
                saved(pool, "state", no, 1)
                load(state_out, outs_["state_s"][:, h].rearrange("b d e -> d b e"), SOUT[:])
            pool.wait_ge(cache_moved, 32)
            pool.wait_ge(kv_stored, 96)
            pool.wait_ge(prompt_state_out, 16)
            pool.wait_ge(state_out, 64)

        @block.scalar
        def _(act):
            steps = [0]
            ex_use = [0, 0]
            n_turn = [0]

            def wait_gate_free(key):
                kind, idx, half = key
                if kind == "fg":
                    if idx >= 2:
                        out_saved(act, ("fu", idx - 2, half))
                        act.wait_ge(hidden_done, 2 * (idx - 2) + half + 1)
                elif idx >= 2:
                    act.wait_ge(gate_used, gate_used_no["up" + kind[4], idx - 2, half])
                elif kind != "gate0":
                    act.wait_ge(gate_used, gate_used_no["up" + str(int(kind[4]) - 1), KT - 2 + idx, half])

            def step(ins):
                steps[0] += 1
                ins.then_inc(act_step, 1)
                act.wait_ge(act_step, steps[0])

            def copy(dst, src):
                return act.activation(dst, src, ACT.Copy)

            def main(key):
                kind, idx, half = key
                no = OUT_NO[key]
                b = main_bank(key)
                bank = BANK[b][:, 0:TH]
                cols = slice(half * TH, half * TH + TH)
                if kind == "mem":
                    act.wait_ge(out_ready, no + 1)
                    dst = MKT[:, idx, :] if idx < 4 else FT[0][:, 0:MEM]
                    copy(dst, BANK[b][:, 0:MEM]).then_inc(bank_free[b], 1)
                elif kind in ("sq", "mq", "sk", "sv", "hi"):
                    act.wait_ge(out_ready, no + 1)
                    dst = {"sq": SQ, "mq": MQ}[kind][:, idx, cols] if kind in ("sq", "mq") else \
                        (SK[:, cols] if kind == "sk" else FT[idx % 2][:, cols])
                    copy(dst, bank).then_inc(bank_free[b], 1)
                elif kind == "hf":
                    act.wait_ge(out_ready, no + 1)
                    if ex_use[half]:
                        act.wait_ge(ex_free[half], ex_use[half])
                    ex_use[half] += 1
                    act.activation(EX[half][:], bank, ACT.Exp, scale=-1.0).then_inc(bank_free[b], 1)
                elif kind in SILU or kind[:4] == "gate":
                    act.wait_ge(out_ready, no + 1)
                    if kind == "fg" and idx == 0:
                        act.wait_ge(ln_lo, KT * (half + 1))
                    if kind in ("fg", "gate0", "gate1", "gate2"):
                        wait_gate_free(key)
                    act.activation(sig_dst(key), bank, ACT.Tanh, scale=0.5)\
                        .then_inc(silu_tanh if kind in SILU else bank_free[b], 1)

            def softmax_exp(u):
                kind, no = u[0], att_no[u]
                st = ST[:, no % 2]
                if kind == "ms":
                    for bl in range(4):
                        keys_free(act, 4 * u[1] + bl)
                        copy(MKB[bl % 2][:, 0:2, :].rearrange("p h t -> p (h t)"), BANK[T0_][:, :])\
                            .then_inc(bank_free[T0_], 1)
                act.wait_ge(max_ready, no + 1)
                lo, w = lo_of(u), {"ws": 192}.get(kind, 256)
                if kind[0] == "w":
                    act.activation(st[:, 16:20], st[:, 8:12], ACT.Exp, scale=0.125)
                    for s in range(4):
                        x = XP[:, no % 2, s, lo:w]
                        ins = act.activation(x, x, ACT.Exp, bias=st[:, 4 + s:5 + s], scale=0.125,
                                             accum_out=st[:, 12 + s:13 + s])
                    ins.then_inc(p_exp, 1)
                else:
                    for s in range(4 if kind == "mp" else 1):
                        src = BANK[S0_ + s // 2][:, 256 * (s % 2):256 * (s % 2) + 256]
                        ins = act.activation(XP[:, no % 2, s, :], src, ACT.Exp, bias=st[:, 4 + s:5 + s],
                                             scale=P ** -0.5, accum_out=st[:, 12 + s:13 + s])
                        if s % 2 or kind == "ms":
                            ins.then_inc(bank_free[S0_ + s // 2], 1)

            def save_probs_T(u):
                kind, no = u[0], att_no[u]
                act.wait_ge(pT_ready, no + 1)
                if no:
                    act.wait_ge(pv_ready, no)
                ptf = PT[:].rearrange("p a c t -> p (a c t)")
                if kind == "ws":
                    copy(ptf[:, 0:512], BANK[T0_][:, :]).then_inc(bank_free[T0_], 1)
                    copy(ptf[0:64, 512:1024], BANK[T1_][0:64, :]).then_inc(bank_free[T1_], 1)
                elif kind == "ms":
                    copy(ptf[:, 0:256], BANK[T0_][:, 0:256]).then_inc(bank_free[T0_], 1)
                else:
                    c0 = lo_of(u) // P
                    for i in range(2):
                        src = BANK[T0_ + i][:, :].rearrange("p (a c t) -> p a c t", a=2, c=2)
                        copy(PT[:, 2 * i:2 * i + 2, c0:2, :], src[:, :, c0:2, :]).then_inc(bank_free[T0_ + i], 1)

            def save_values(u):
                kind, no = u[0], att_no[u]
                act.wait_ge(pv_ready, no + 1)
                bank = BANK[V_]
                if kind == "w":
                    n, g = u[1:]
                    ins = copy(SQ[:, 2 * g:2 * g + 2, P * n:P * n + P],
                               bank[:, 0:256].rearrange("p (j t) -> p j t", j=2))
                elif kind == "ws":
                    ins = copy(SQ[:, :, SEQ:T].rearrange("p j (b i) -> p b j i", b=NB),
                               bank[:, 0:256].rearrange("p (b j i) -> p b j i", b=NB, j=4))
                elif kind == "mp":
                    n = u[1]
                    ins = copy(MQ[:, :, P * n:P * n + P], bank[:, :].rearrange("p (h t) -> p h t", h=4))
                else:
                    c0 = SEQ + 32 * u[1]
                    ins = copy(MQ[:, :, c0:c0 + 32], bank[:, 0:P].rearrange("p (h t) -> p h t", h=4))
                ins.then_inc(bank_free[V_], 1)

            def hgrn_decays(u):
                _, n, h = u
                no = hg_no[u]
                t0, w, levels = hg_cols(n)
                nl = len(levels)
                act.wait_ge(d_ready, no + 1)
                if no == 0:
                    act.wait_ge(kv_stored, 96)
                act.activation(QE[:, 0:w], HB[:, h, t0:t0 + w], ACT.Exp)
                if n < NBLK:
                    act.activation(EBL[:, no % 4, 0:1], HB[:, h, t0 + P - 1:t0 + P], ACT.Exp)
                else:
                    act.activation(EBL[:, no % 4, :], HB[:, h, t0 + NS - 1:t0 + w:NS], ACT.Exp)
                e = E[no % 2]
                parts = [e[:, :, :]] if n < NBLK else [e[:, 0:nl, 0:w], e[:, 7:8, 0:w]]
                for part in parts:
                    step(act.activation(part, part, ACT.Abs))
                for i, part in enumerate(parts):
                    ins = act.activation(part, part, ACT.Exp, scale=-1.0)
                ins.then_inc(e_ready, 1)

            def save_decayed_keys(u):
                no = hg_no[u]
                w = hg_cols(u[1])[1]
                act.wait_ge(kT_ready, no + 1)
                copy(KTM[no % 2][0:w, :], BANK[T0_][0:w, 0:P]).then_inc(bank_free[T0_], 1)

            def split(u):
                act.wait_ge(raw_in[u % NRAW], raw_full[u])
                if u >= NHI:
                    unit_used(act, u - NHI)
                n = unit_tiles(u)
                copy(WH[u % NHI][:, 0:n, :], RAW[u % NRAW][:, 0:n, :]).then_inc(w_hi, 1)

            for s in SCHEDULE:
                what, rest = s[0], s[1:]
                if what == "out":
                    main(rest)
                elif what == "split_hi":
                    split(rest[0])
                elif what == "setup":
                    act.wait_ge(vecT_ready, 1)
                    copy(VEC[:, 0:57], BANK[V_][:, 0:57]).then_inc(bank_free[V_], 1)
                    saved(act, "vec")
                    act.wait_ge(lb_shifted, 1)
                    act.activation(LBT[:, 0:8], LBT[:, 0:8], ACT.Exp).then_inc(lb_exp, 1)
                elif what == "memx":
                    t = rest[0]
                    act.wait_ge(memT_ready, t + 1)
                    for i in range(2):
                        copy(MH[:, 4 * i:4 * i + 4, P * t:P * t + P],
                             BANK[T0_ + i][:, :].rearrange("p (k t) -> p k t", k=4)).then_inc(mem_hi_done, 1)
                elif what == "x_load":
                    for i in range(5):
                        src = a["x_sample"] if i == NBLK else a["x_prompt"][P * i:P * i + P, :]
                        act.dma_start(XS[i][0:TOKENS[i][1], :], src).then_inc(xs_in[i], 16)
                elif what == "rstd0":
                    act.wait_ge(x_var, 1)
                    step(act.activation(BNR[:], BNV[:, :, 1], ACT.Ln, bias=EPS[:, 0:1]))
                    act.activation(BNR[:], BNR[:], ACT.Exp, scale=-0.5).then_inc(x_rstd, 1)
                elif what == "ln0":
                    t = rest[0]
                    t0, n = TOKENS[t]
                    act.wait_ge(xT_ready, t + 1)
                    if t >= 2:
                        act.wait_ge(x_lo_done, t - 1)
                    for k in range(KT):
                        ins = act.activation(XT[t % 2][:, k, 0:n],
                                             BANK[T0_ + k // 4][:, P * (k % 4):P * (k % 4) + n], ACT.Identity,
                                             scale=vec["ln0_w"][:, k:k + 1], bias=vec["ln0_b"][:, k:k + 1])
                        if k % 4 == 3:
                            ins.then_inc(bank_free[T0_ + k // 4], 1)
                elif what == "turn_mem":
                    idx = rest[0]
                    n_turn[0] += 1
                    act.wait_ge(turn_ready, n_turn[0])
                    dst = (MKTM if idx < 4 else MV)[:, :, P * (idx % 4):P * (idx % 4) + P]
                    copy(dst, BANK[V_][:, 0:MEM].rearrange("p (c n) -> p c n", c=2)).then_inc(bank_free[V_], 1)
                elif what == "turn":
                    kind, idx = rest
                    n_turn[0] += 1
                    act.wait_ge(turn_ready, n_turn[0])
                    b0, b1 = BANK[T0_], BANK[T1_]
                    if kind == "sk":
                        copy(SKTM[:, 0, :], b0[:, 384:512]).then_inc(bank_free[T0_], 1)
                        copy(SKTM[0:64, 1, :], b1[0:64, 0:P]).then_inc(bank_free[T1_], 1)
                    else:
                        full = SV[:, 0:4, :] if kind == "sv" else HV[:, 0:4, P * idx:P * idx + P]
                        tail = SV[0:64, 4, :] if kind == "sv" else HV[0:64, 4, P * idx:P * idx + P]
                        copy(full, b0[:, :].rearrange("p (t n) -> p t n", t=4)).then_inc(bank_free[T0_], 1)
                        copy(tail, b1[0:64, 0:P]).then_inc(bank_free[T1_], 1)
                elif what == "wk":
                    act.wait_ge(cacheT_ready, 1)
                    for i in range(2):
                        copy(KTS[:, 4 * i:4 * i + 4, :].rearrange("p b t -> p (b t)"), BANK[T0_ + i][:, :])\
                            .then_inc(bank_free[T0_ + i], 1)
                elif what == "scan":
                    j = rest[0]
                    act.wait_ge(f_ready, 2 * j + 2)
                    act.activation(HB[:, j, :], HB[:, j, :], ACT.Ln).then_inc(logf_done, 1)
                elif what == "P" and rest[0] == "h":
                    hgrn_decays(rest)
                elif what == "A":
                    (save_decayed_keys if rest[0] == "h" else softmax_exp)(rest)
                elif what == "B" and rest[0] != "h":
                    save_probs_T(rest)
                elif what == "C":
                    if rest[0] == "h":
                        _, n, h = rest
                        t0, w, _ = hg_cols(n)
                        act.wait_ge(ho_ready, hg_no[rest] + 1)
                        copy(HQ[:, h, t0:t0 + w], BANK[V_][:, 0:w]).then_inc(bank_free[V_], 1)
                    else:
                        save_values(rest)
                elif what == "rms_sum":
                    h = rest[0]
                    for half in range(2):
                        act.wait_ge(rms_sum, 2 * h + half + 1)
                        copy(RRS[:, 2 * h + half, :], BANK[V_][:, 0:TH]).then_inc(bank_free[V_], 1)
                elif what == "rms":
                    h = rest[0]
                    if h == 0:
                        saved(act, "rms", 3, 1)
                        for i in range(0, 8, 2):
                            ins = act.activation(RRS[:, i:i + 2, :], RRS[:, i:i + 2, :], ACT.Ln, bias=EPS[:, 1:2],
                                                 scale=float(D // P))
                        step(ins)
                    act.activation(RRS[:, 2 * h:2 * h + 2, :], RRS[:, 2 * h:2 * h + 2, :], ACT.Exp, scale=-0.5)\
                        .then_inc(rms_rstd, 1)
                elif what == "center":
                    ln, half = rest
                    if ln > 1 or half:
                        act.wait_ge(var_ready, 2 * (ln - 1) + half)
                    for c in range(KT):
                        if c < KT - 1:
                            act.wait_ge(centered, 14 * (ln - 1) + 7 * half + c + 1)
                        else:
                            saved(act, "mean", ln, half)
                        act.activation(SQR[:, c, :], Y[:, c, half * TH:half * TH + TH], ACT.Square)\
                            .then_inc(squared, 1)
                elif what == "var":
                    ln, half = rest
                    act.wait_ge(var_ready, 2 * (ln - 1) + half + 1)
                    act.activation(SG[half][:], BANK[T0_][:, 0:TH], ACT.Ln, bias=EPS[:, 0:1])\
                        .then_inc(bank_free[T0_], 1)
                    saved(act, "var", ln, half)
                    act.activation(SG[half][:], SG[half][:], ACT.Exp, scale=-0.5).then_inc(ln_rstd, 1)
                elif what == "norm":
                    ln, half = rest
                    cols = slice(half * TH, half * TH + TH)
                    for c in range(KT):
                        act.wait_ge(ln_scaled, 16 * (ln - 1) + 8 * half + c + 1)
                        dst = XH[:, c, cols] if ln == 1 else Y[:, c, cols]
                        act.activation(dst, Y[:, c, cols], ACT.Identity, bias=vec[f"ln{ln}_b"][:, c:c + 1])\
                            .then_inc(ln_hi, 1)
                elif what == "store":
                    half = rest[0]
                    for i, (t0, n) in enumerate(OUT_CHUNKS[half]):
                        no = 3 * half + i
                        act.wait_ge(outT_ready, no + 1)
                        if no >= 2:
                            act.wait_ge(out_dma[no % 2], 16 * (no // 2))
                        copy(OUTT[no % 2][0:n, 0:512], BANK[S0_][0:n, :]).then_inc(bank_free[S0_], 1)

        @block.vector
        def _(dve):
            steps = [0]
            ex_use = [0, 0]
            n_silu = [0]

            def step(ins):
                steps[0] += 1
                ins.then_inc(dve_step, 1)
                dve.wait_ge(dve_step, steps[0])

            def main(key):
                kind, idx, half = key
                b = main_bank(key)
                bank = BANK[b][:, 0:TH]
                cols = slice(half * TH, half * TH + TH)
                if kind == "hf":
                    out_saved(dve, key)
                    dst = HB[:, idx, cols]
                    step(dve.tensor_scalar(EX[half][:], EX[half][:], 1.0, None, ALU.add))
                    dve.reciprocal(dst, EX[half][:]).then_inc(ex_free[half], 1)
                    ex_use[half] += 1
                    dve.wait_ge(ex_free[half], ex_use[half])
                    step(dve.tensor_scalar(dst, dst, LB[:, 4 + idx:5 + idx], LB[:, idx:idx + 1],
                                           ALU.mult, ALU.add))
                    dve.tensor_scalar(HK[:, idx, cols], dst, -1.0, 1.0, ALU.mult, ALU.add).then_inc(f_ready, 1)
                elif kind in SILU:
                    n_silu[0] += 1
                    dve.wait_ge(silu_tanh, n_silu[0])
                    dst = sig_dst(key)
                    dve.scalar_tensor_tensor(out=dst, in0=dst, scalar=1.0, in1=bank, op0=ALU.add, op1=ALU.mult)\
                        .then_inc(bank_free[b], 1)
                    if kind == "hq":
                        out_saved(dve, key)
                        step(dve.tensor_scalar(dst, dst, 0.5, None, ALU.mult))
                elif kind[:2] == "up":
                    dve.wait_ge(out_ready, OUT_NO[key] + 1)
                    gate = SG[2 * (idx % 2) + half][:]
                    out_saved(dve, ("gate" + kind[2], idx, half))
                    mix = MIX[:, idx, cols]
                    dst = mix if kind == "up0" else gate
                    dve.scalar_tensor_tensor(out=dst, in0=gate, scalar=1.0, in1=bank, op0=ALU.add, op1=ALU.mult)\
                        .then_inc(bank_free[b], 1)
                    out_saved(dve, key)
                    if kind == "up0":
                        dve.engine_nop().then_inc(gate_used, 1)
                    else:
                        dve.tensor_tensor(mix, mix, gate, ALU.add).then_inc(gate_used, 1)
                elif kind == "fu":
                    dve.wait_ge(out_ready, OUT_NO[key] + 1)
                    gate = SG[2 * (idx % 2) + half][:]
                    out_saved(dve, ("fg", idx, half))
                    dve.scalar_tensor_tensor(out=gate, in0=gate, scalar=0.5, in1=bank, op0=ALU.mult, op1=ALU.mult)\
                        .then_inc(bank_free[b], 1)
                    out_saved(dve, key)
                    step(dve.tensor_copy(GH[:, idx, cols], gate))
                    dve.tensor_tensor(GL[:, idx, cols], gate, f32(GH[:, idx, cols]), ALU.subtract)\
                        .then_inc(hidden_done, 1)
                elif kind in ("o", "y"):
                    dve.wait_ge(out_ready, OUT_NO[key] + 1)
                    if key == ("o", 0, 0):
                        dve.wait_ge(state_out, 64)
                        dve.wait_ge(prompt_state_out, 16)
                    y = Y[:, idx, cols]
                    dve.scalar_tensor_tensor(out=y, in0=f32(XH[:, idx, cols]), scalar=ALPHA, in1=bank,
                                             op0=ALU.mult, op1=ALU.add).then_inc(bank_free[b], 1)
                    out_saved(dve, key)
                    dve.scalar_tensor_tensor(out=y, in0=f32(XL[:, idx, cols]), scalar=ALPHA, in1=y,
                                             op0=ALU.mult, op1=ALU.add).then_inc(y_ready, 1)

            def softmax_max(u):
                kind, no = u[0], att_no[u]
                st = ST[:, no % 2]
                x = XP[:, no % 2]
                if kind == "ms":
                    for bl in range(4):
                        keys_free(dve, 4 * u[1] + bl)
                        dve.tensor_copy(MKB[bl % 2][:, 2:4, :].rearrange("p h t -> p (h t)"), BANK[T1_][:, :])\
                            .then_inc(bank_free[T1_], 1)
                dve.wait_ge(scores_ready, no + 1)
                if no >= 2:
                    dve.wait_ge(pT_ready, no - 1)
                if kind[0] == "w":
                    lo, w = lo_of(u), {"ws": 192}.get(kind, 256)
                    for s in range(4):
                        kv, jj = s // 2, s % 2
                        if kind == "w":
                            bias, slope = NEGD[:, lo:w], 8.0 * 2.0 ** -(2 * u[2] + jj + 4 * kv + 1)
                            src = BANK[S0_ + kv][:, 256 * jj + lo:256 * jj + 256]
                        else:
                            bias, slope = NEGS[:, s, :], SMALL[:, 0:1]
                            src = BANK[S0_ + kv][:, 192 * jj:192 * jj + 192]
                        ins = dve.scalar_tensor_tensor(out=x[:, s, lo:w], in0=bias, scalar=slope, in1=src,
                                                       op0=ALU.mult, op1=ALU.add)
                        if jj:
                            ins.then_inc(bank_free[S0_ + kv], 1)
                    saved(dve, "scores", no, 0)
                    saved(dve, "scores", no, 1)
                    step(dve.tensor_reduce(st[:, 0:4], x[:, :, lo:w], AX.X, ALU.max))
                    sink = SINK[:, 4 * u[2]:4 * u[2] + 4] if kind == "w" else SINK[:, 8:9].to_broadcast([P, 4])
                    step(dve.tensor_tensor(st[:, 0:4], st[:, 0:4], sink, ALU.max))
                    dve.tensor_tensor(st[:, 8:12], sink, st[:, 0:4], ALU.subtract)
                    dve.tensor_scalar(st[:, 4:8], st[:, 0:4], -0.125, None, ALU.mult).then_inc(max_ready, 1)
                else:
                    nbank = 2 if kind == "mp" else 1
                    for i in range(nbank):
                        src = BANK[S0_ + i][:, :].rearrange("p (s k) -> p s k", s=2)[:, 0:nbank]
                        ins = dve.tensor_reduce(st[:, 2 * i:2 * i + nbank], src, AX.X, ALU.max)
                    step(ins)
                    ns = nbank * nbank
                    dve.tensor_scalar(st[:, 4:4 + ns], st[:, 0:ns], -(P ** -0.5), None, ALU.mult)\
                        .then_inc(max_ready, 1)

            def softmax_divide(u):
                kind, no = u[0], att_no[u]
                st = ST[:, no % 2]
                ns = 1 if kind == "ms" else 4
                lo, w = lo_of(u), {"ws": 192}.get(kind, 256)
                if kind[0] == "w":
                    dve.wait_ge(p_exp, n_window_exps[u])
                    step(dve.tensor_tensor(st[:, 20:24], st[:, 12:16], st[:, 16:20], ALU.add))
                    step(dve.reciprocal(st[:, 24:28], st[:, 20:24]))
                else:
                    saved(dve, "scores", no, 0)
                    if kind == "mp":
                        saved(dve, "scores", no, 1)
                    step(dve.reciprocal(st[:, 24:24 + ns], st[:, 12:12 + ns]))
                x = XP[:, no % 2, 0:ns, lo:w]
                dve.tensor_tensor(x, x, bcast(st[:, 24:24 + ns], w - lo), ALU.mult).then_inc(p_ready, 1)

            window_units = [u for u in att_units if u[0][0] == "w"]
            n_window_exps = {u: i + 1 for i, u in enumerate(window_units)}

            def hgrn_distances(u):
                _, n, h = u
                t0, w, levels = hg_cols(n)
                no = hg_no[u]
                e = E[no % 2]
                if no >= 2:
                    dve.wait_ge(ekq_ready, no - 1)
                b = HB[:, h, t0:t0 + w]
                for i, m in enumerate(levels):
                    v = level_view(b, m)
                    dve.tensor_tensor(level_view(e[:, i, 0:w], m), v,
                                      v[:, :, m - 1:m].to_broadcast([P, w // (2 * m), 2 * m]), ALU.subtract)
                c = w if n < NBLK else NS
                v = b.rearrange("p (b m) -> p b m", m=c)
                dve.tensor_tensor(e[:, 7, 0:w].rearrange("p (b m) -> p b m", m=c), v,
                                  v[:, :, c - 1:c].to_broadcast([P, w // c, c]), ALU.subtract).then_inc(d_ready, 1)

            def hgrn_decayed(u):
                _, n, h = u
                no = hg_no[u]
                t0, w, levels = hg_cols(n)
                nl = len(levels)
                e = E[no % 2]
                if no == 0:
                    dve.wait_ge(pv_ready, n_att)
                    dve.wait_ge(kv_stored, 96)
                    dve.wait_ge(mask_in, 16)
                    for hh in range(4):
                        saved(dve, "turn", "hi", hh, 0)
                k, q = HK[:, h, t0:t0 + w], HQ[:, h, t0:t0 + w]
                dve.wait_ge(e_ready, no + 1)
                if no:
                    dve.wait_ge(kT_ready, no)
                if n < NBLK:
                    dve.tensor_tensor(EK[:, :, :], e[:, :, :], over(k, 8), ALU.mult)
                else:
                    dve.tensor_tensor(EK[:, 0:nl, 0:w], e[:, 0:nl, 0:w], over(k, nl), ALU.mult)
                    dve.tensor_tensor(EK[:, 7, 0:w], e[:, 7, 0:w], k, ALU.mult)
                dve.tensor_tensor(QW[no % 3][:, 0:w], QE[:, 0:w], q, ALU.mult)
                dve.tensor_tensor(EQ[:, 0:nl, 0:w], e[:, 0:nl, 0:w], over(q, nl), ALU.mult).then_inc(ekq_ready, 1)

            def hgrn_mask(u):
                _, n, h = u
                no = hg_no[u]
                _, w, levels = hg_cols(n)
                nl = len(levels)
                if no:
                    dve.wait_ge(a_sum, no)
                dve.wait_ge(a_ready, no + 1)
                if n < NBLK:
                    for i in range(2):
                        src = BANK[S0_ + i][:, :].rearrange("p (l t) -> p l t", l=4)
                        dve.tensor_tensor(AM[:, 4 * i:4 * i + 4, :], src, MASKS[:, 4 * i:4 * i + 4, :], ALU.mult)\
                            .then_inc(bank_free[S0_ + i], 1)
                        saved(dve, "a", no, i)
                else:
                    src = BANK[S0_][:, :].rearrange("p (l t) -> p l t", l=4)
                    dve.tensor_tensor(AM[0:w, 0:4, 0:w], src[0:w, :, 0:w], MASKS[0:w, 4:8, 0:w], ALU.mult)\
                        .then_inc(bank_free[S0_], 1)
                    saved(dve, "a", no, 0)
                    if h:
                        dve.wait_ge(ho_ready, no)
                    dve.tensor_tensor(VB[:, :, :], over(HV[0:w, n, P * h:P * h + P], NB),
                                      bcast(SMALL[0:w, 1:9], P), ALU.mult).then_inc(vb_ready, 1)
                if no >= 2:
                    dve.wait_ge(ho_ready, no - 1)
                dve.tensor_reduce(ASB[no % 2][0:w, 0:w], AM[0:w, 0:nl + 1, 0:w].rearrange("p l t -> p t l"), AX.X, ALU.add)\
                    .then_inc(a_sum, 1)

            def hgrn_state(u):
                _, n, h = u
                no = hg_no[u]
                dve.wait_ge(ho_ready, no + 1)
                if n == 0:
                    dve.tensor_copy(STATE[:, h, :], BANK[T1_][:, 0:P]).then_inc(bank_free[T1_], 1)
                elif n < NBLK:
                    dve.scalar_tensor_tensor(out=STATE[:, h, :], in0=STATE[:, h, :], scalar=EBL[:, no % 4, 0:1],
                                             in1=BANK[T1_][:, 0:P], op0=ALU.mult, op1=ALU.add)\
                        .then_inc(bank_free[T1_], 1)
                else:
                    if h:
                        dve.wait_ge(state_out, 16 * h)
                    step(dve.tensor_tensor(SOUT[:], SIN[:], bcast(EBL[:, no % 4, :], P), ALU.mult))
                    for i in range(2):
                        o = SOUT[:, 4 * i:4 * i + 4, :]
                        dve.tensor_tensor(o, o, BANK[T0_ + i][:, :].rearrange("p (b e) -> p b e", b=4), ALU.add)\
                            .then_inc(bank_free[T0_ + i], 1)

            def split(u):
                dve.wait_ge(w_hi, u + 1)
                n = unit_tiles(u)
                dve.tensor_tensor(WL[u % NRAW][:, 0:n, :], RAW[u % NRAW][:, 0:n, :], f32(WH[u % NHI][:, 0:n, :]),
                                  ALU.subtract).then_inc(w_lo, 1)

            for s in SCHEDULE:
                what, rest = s[0], s[1:]
                if what == "out":
                    main(rest)
                elif what == "split_lo":
                    split(rest[0])
                elif what == "init":
                    dve.memset(ONES[:], 1.0 / D)
                    dve.memset(EPS[:, 0:1], LN_EPS)
                    dve.memset(EPS[:, 1:2], RMS_EPS)
                    dve.memset(BNV[:], 1.0)
                    step(dve.memset(RST[:], 1.0))
                    dve.memset(RST[:, 0:SEQ:P], 0.0)
                    step(dve.memset(RST[:, SEQ:T:NS], 0.0))
                elif what == "setup":
                    dve.wait_ge(sink_in, 16)
                    step(dve.tensor_scalar(SINK[:], SINK[:], 8.0, None, ALU.mult))
                    saved(dve, "vec")
                    lb = vec["hg_lb"]
                    step(dve.tensor_tensor(LBT[:, 8:12], lb[:, 0:4], lb[:, 4:8], ALU.max))
                    dve.tensor_tensor(LBT[:, 0:4], lb[:, 0:4], LBT[:, 8:12], ALU.subtract)
                    dve.tensor_tensor(LBT[:, 4:8], lb[:, 4:8], LBT[:, 8:12], ALU.subtract).then_inc(lb_shifted, 1)
                    dve.wait_ge(lb_exp, 1)
                    step(dve.tensor_tensor(LBT[:, 8:12], LBT[:, 0:4], LBT[:, 4:8], ALU.add))
                    step(dve.reciprocal(LBT[:, 8:12], LBT[:, 8:12]))
                    step(dve.tensor_tensor(LB[:, 0:4], LBT[:, 0:4], LBT[:, 8:12], ALU.mult))
                    step(dve.tensor_scalar(LB[:, 4:8], LB[:, 0:4], -1.0, 1.0, ALU.mult, ALU.add))
                elif what == "memx":
                    t = rest[0]
                    for i in range(2):
                        dve.wait_ge(mem_hi_done, 2 * t + i + 1)
                        sl = (slice(None), slice(4 * i, 4 * i + 4), slice(P * t, P * t + P))
                        dve.tensor_tensor(ML[sl], BANK[T0_ + i][:, :].rearrange("p (k t) -> p k t", k=4),
                                          f32(MH[sl]), ALU.subtract).then_inc(bank_free[T0_ + i], 1)
                elif what == "stat":
                    t = rest[0]
                    n = TOKENS[t][1]
                    dve.wait_ge(xs_in[t], 16)
                    for i in range(2):
                        ins = dve.bn_stats(BNS[0:n, t, 6 * i:6 * i + 6], XS[t][0:n, 512 * i:512 * i + 512])
                    step(ins)
                    ins = dve.bn_aggr(BNV[0:n, t, :], BNS[0:n, t, :])
                    if t == NBLK:
                        ins.then_inc(x_var, 1)
                elif what == "scale0":
                    t = rest[0]
                    x = XS[t][0:TOKENS[t][1], :]
                    dve.wait_ge(x_rstd, 1)
                    dve.tensor_scalar(x, x, BNV[0:TOKENS[t][1], t, 0:1], BNR[0:TOKENS[t][1], t:t + 1],
                                      ALU.subtract, ALU.mult).then_inc(x_scaled, 1)
                elif what == "ln0":
                    t = rest[0]
                    t0, n = TOKENS[t]
                    saved(dve, "xT", t, 0)
                    saved(dve, "xT", t, 1)
                    step(dve.tensor_copy(XH[:, :, t0:t0 + n], XT[t % 2][:, :, 0:n]))
                    dve.tensor_tensor(XL[:, :, t0:t0 + n], XT[t % 2][:, :, 0:n], f32(XH[:, :, t0:t0 + n]),
                                      ALU.subtract).then_inc(x_lo_done, 1)
                    if t == NBLK:
                        dve.wait_ge(attc_in, 48)
                elif what == "scan":
                    j = rest[0]
                    dve.wait_ge(logf_done, j + 1)
                    step(dve.tensor_tensor_scan(HB[:, j, :], RST[:], HB[:, j, :], 0.0, ALU.mult, ALU.add))
                elif what == "D" and rest[0] == "h":
                    hgrn_distances(rest)
                elif what == "K" and rest[0] == "h":
                    hgrn_decayed(rest)
                elif what == "A" and rest[0] != "h":
                    softmax_max(rest)
                elif what == "N":
                    (hgrn_mask if rest[0] == "h" else softmax_divide)(rest)
                elif what == "C" and rest[0] == "h":
                    hgrn_state(rest)
                elif what == "rms_sum":
                    h = rest[0]
                    if h == 0:
                        for hh in range(4):
                            saved(dve, "ho", hg_no["h", NBLK, hh])
                        dve.wait_ge(kT_ready, len(hg_units))
                    else:
                        dve.wait_ge(rms_sum, 2 * h)
                    for half in range(2):
                        o = HQ[:, h, half * TH:half * TH + TH]
                        dve.tensor_tensor(RSQ[:, half, :], o, o, ALU.mult).then_inc(rms_sq, 1)
                elif what == "rms":
                    h = rest[0]
                    dve.wait_ge(rms_rstd, h + 1)
                    o = HQ[:, h, :]
                    step(dve.scalar_tensor_tensor(out=o, in0=o, scalar=NORMW,
                                                  in1=RRS[:, 2 * h:2 * h + 2, :].rearrange("p a t -> p (a t)"),
                                                  op0=ALU.mult, op1=ALU.mult))
                    step(dve.scalar_tensor_tensor(out=o, in0=o, scalar=0.5, in1=HG[:, h, :],
                                                  op0=ALU.mult, op1=ALU.mult))
                elif what == "branch":
                    br, j = rest
                    if j == 0:
                        if br == 0:
                            saved(dve, "pv", n_att - 1)
                        else:
                            dve.wait_ge(out_ready, OUT_NO[f"up{br - 1}", KT - 1, 1] + 1)
                    src = (SQ, MQ, HQ)[br][:, j, :]
                    step(dve.tensor_copy(OSH[:, j, :], src))
                    dve.tensor_tensor(OSL[:, j, :], src, f32(OSH[:, j, :]), ALU.subtract)\
                        .then_inc(branch_split, 1)
                elif what == "mix":
                    c = rest[0]
                    dve.wait_ge(gate_used, gate_used_no["up2", c, 1])
                    step(dve.tensor_scalar(MIXH[:, c, :], MIX[:, c, :], 0.5, None, ALU.mult))
                    dve.scalar_tensor_tensor(out=MIXL[:, c, :], in0=MIX[:, c, :], scalar=0.5,
                                             in1=f32(MIXH[:, c, :]), op0=ALU.mult, op1=ALU.subtract)\
                        .then_inc(mix_split, 1)
                elif what == "center":
                    ln, half = rest
                    mb = MEAN_BANK[half]
                    dve.wait_ge(mean_ready, 2 * (ln - 1) + half + 1)
                    for c in range(KT):
                        y = Y[:, c, half * TH:half * TH + TH]
                        dve.tensor_tensor(y, y, BANK[mb][:, 0:TH], ALU.subtract)\
                            .then_inc(centered if c < KT - 1 else bank_free[mb], 1)
                elif what == "norm":
                    ln, half = rest
                    cols = slice(half * TH, half * TH + TH)
                    dve.wait_ge(ln_rstd, 2 * (ln - 1) + half + 1)
                    saved(dve, "mean", ln, half)
                    for c in range(KT):
                        y = Y[:, c, cols]
                        dve.scalar_tensor_tensor(out=y, in0=y, scalar=vec[f"ln{ln}_w"][:, c:c + 1],
                                                 in1=SG[half][:], op0=ALU.mult, op1=ALU.mult)\
                            .then_inc(ln_scaled, 1)
                    if ln == 1:
                        for c in range(KT):
                            dve.wait_ge(ln_hi, 8 * half + c + 1)
                            dve.scalar_tensor_tensor(out=XL[:, c, cols], in0=Y[:, c, cols],
                                                     scalar=vec["ln1_b"][:, c:c + 1], in1=f32(XH[:, c, cols]),
                                                     op0=ALU.add, op1=ALU.subtract).then_inc(ln_lo, 1)
                elif what == "store":
                    half = rest[0]
                    for i, (t0, n) in enumerate(OUT_CHUNKS[half]):
                        no = 3 * half + i
                        dve.wait_ge(outT_ready, no + 1)
                        if no >= 2:
                            dve.wait_ge(out_dma[no % 2], 16 * (no // 2))
                        dve.tensor_copy(OUTT[no % 2][0:n, 512:1024], BANK[S1_][0:n, :])\
                            .then_inc(bank_free[S1_], 1)


def kernel(x_prompt, x_sample, cache_k_win, cache_v_win, state_hgrn, cache_mem_k, cache_mem_v, mem_prompt,
           ln0_w, ln0_b, w_in, w_up_sw, w_up_hg, w_up_mx, sw_sinks, hg_lower_bound, hg_norm_w, w_mem_kv,
           w_o, ln1_w, ln1_b, w_ffn_in, w_ffn_out, ln2_w, ln2_b):
    import concourse.bacc as bacc
    from concourse.bass_utils import run_bass_kernel_spmd

    sinks = np.asarray(sw_sinks)[0]
    order = [2 * g + jj + 4 * kv for g in range(2) for kv in range(2) for jj in range(2)]
    row = np.arange(P)
    rows = np.concatenate([np.broadcast_to(sinks[order], (P, 8)),
                           sinks[(row // 8) % 4 + 4 * ((row // 32) % 2)][:, None]], axis=1)
    data = {
        "x_prompt": np.asarray(x_prompt)[0], "x_sample": np.asarray(x_sample).reshape(NB * NS, D),
        "cache_k": np.asarray(cache_k_win)[0].reshape(NB, WIN, P),
        "cache_v": np.asarray(cache_v_win)[0].reshape(NB, WIN, P),
        "state_in": np.asarray(state_hgrn)[0],
        "mem_k_s": np.asarray(cache_mem_k)[0].reshape(NB, MEM, 512),
        "mem_v_s": np.asarray(cache_mem_v)[0].reshape(NB, MEM, 512),
        "mem_prompt": np.asarray(mem_prompt)[0],
        "ln0_w": ln0_w, "ln0_b": ln0_b, "w_in": np.asarray(w_in)[0], "w_up_sw": np.asarray(w_up_sw)[0],
        "w_up_hg": np.asarray(w_up_hg)[0], "w_up_mx": np.asarray(w_up_mx)[0], "sink_rows": rows,
        "hg_lb": hg_lower_bound, "hg_norm_w": hg_norm_w, "w_mem_kv": np.asarray(w_mem_kv)[0],
        "w_o": np.asarray(w_o)[0], "ln1_w": np.asarray(ln1_w)[0], "ln1_b": np.asarray(ln1_b)[0],
        "w_ffn_in": np.asarray(w_ffn_in)[0], "w_ffn_out": np.asarray(w_ffn_out)[0],
        "ln2_w": np.asarray(ln2_w)[0], "ln2_b": np.asarray(ln2_b)[0],
        **shape_constants(),
    }
    shapes = {
        "y_p": (SEQ, D), "y_s": (NB * NS, D), "k_win_p": (WIN, P), "v_win_p": (WIN, P), "state_p": (4, P, P),
        "mem_k_p": (MEM, 512), "mem_v_p": (MEM, 512), "k_win_s": (NB, WIN, P), "v_win_s": (NB, WIN, P),
        "state_s": (NB, 4, P, P),
    }
    nc = bacc.Bacc("TRN2", target_bir_lowering=False, num_devices=1)
    arrays, ins, outs = {}, {}, {}
    for name, value in data.items():
        value = np.ascontiguousarray(value)
        arrays[f"in_{name}"] = value
        ins[name] = nc.dram_tensor(f"in_{name}", value.shape, mybir.dt.from_np(value.dtype),
                                   kind="ExternalInput").ap()
    for name, shape in shapes.items():
        outs[name] = nc.dram_tensor(f"out_{name}", shape, F32, kind="ExternalOutput").ap()
    build_decoder_layer(nc, ins, outs)
    r = run_bass_kernel_spmd(nc, [arrays], core_ids=[0]).results[0]
    got = {name: r[f"out_{name}"] for name in shapes}
    return (got["y_p"][None], got["y_s"].reshape(NB, NS, D),
            got["k_win_p"].reshape(1, 1, WIN, 2, 64), got["v_win_p"].reshape(1, 1, WIN, 2, 64),
            got["state_p"].reshape(1, 1, 4, P, P),
            got["mem_k_p"].reshape(1, 1, MEM, 4, P), got["mem_v_p"].reshape(1, 1, MEM, 4, P),
            got["k_win_s"].reshape(1, NB, WIN, 2, 64), got["v_win_s"].reshape(1, NB, WIN, 2, 64),
            got["state_s"][None])
```

```python
from contextlib import ExitStack

import numpy as np

import concourse.bass as bass
from concourse import mybir

F32 = mybir.dt.float32
F32R = mybir.dt.float32r
BF16 = mybir.dt.bfloat16
ALU = mybir.AluOpType
ACT = mybir.ActivationFunctionType
AX = mybir.AxisListType

P = 128
D = 1024
KT = D // P
SEQ, NB, NS = 512, 8, 8
T = SEQ + NB * NS
TH = T // 2
WIN, MEM = 128, 256
NBLK = SEQ // P
FF = 2816
FT_ = FF // P
LN_EPS, RMS_EPS = 1e-5, 1e-6
ALPHA = 2.0 ** 0.25
LEVELS = [64, 32, 16, 8, 4, 2, 1]
SAMPLE_LEVELS = [4, 2, 1]
MASKED = -3.0e37
GATE_OF = (0, 2, 1)
TOKENS = [(P * t, P) for t in range(NBLK)] + [(SEQ, NB * NS)]

C_SK, C_SV, C_HQ, C_HF, C_HI, C_HG, C_MQ, C_GATE = 512, 640, 768, 1280, 1792, 2304, 2816, 3328


def shape_constants():
    i = np.arange(P)[:, None]
    j = np.arange(2 * P)[None, :]
    dist = i + P - j
    negd = np.where((dist >= 0) & (dist < WIN), -dist, MASKED).astype(np.float32)
    row = np.arange(P)
    c, jj, ii = row // 32, (row // 8) % 4, row % 8
    negs = np.full((P, 4, WIN + NB * NS), MASKED, np.float32)
    for r in range(4):
        b = 2 * r + c // 2
        past = ii[:, None] + WIN - np.arange(WIN)[None, :]
        negs[:, r, :WIN] = np.where(past < WIN, -past, MASKED)
        tok = np.arange(NB * NS)[None, :]
        own = (tok // NS == b[:, None]) & (tok % NS <= ii[:, None])
        negs[:, r, WIN:] = np.where(own, -(ii[:, None] - tok % NS), MASKED)
    head = jj + 4 * (c % 2)
    slope8 = (8.0 * 2.0 ** -(head + 1.0)).astype(np.float32)[:, None]
    s = np.arange(P)[:, None]
    t = np.arange(P)[None, :]
    masks = [(s // (2 * m) == t // (2 * m)) & (s % (2 * m) < m) & (t % (2 * m) >= m) for m in LEVELS] + [s == t]
    masks = np.stack(masks, 1).astype(np.float32)
    own8 = (np.arange(P)[:, None] // NS == np.arange(NB)[None, :]).astype(np.float32)
    return {
        "c_negd": negd, "c_negs": negs, "c_masks": masks,
        "c_small": np.concatenate([slope8, own8], 1).astype(np.float32),
        "c_ident": np.eye(P, dtype=np.float32),
    }


def halves_order(tail):
    return [(c, half) for c in range(tail) for half in range(2)] + \
        [(c, 0) for c in range(tail, KT)] + [(c, 1) for c in range(KT - 1, tail - 1, -1)]


O_TAIL, Y_TAIL = 1, 5
Y_PAIRED = [*range(Y_TAIL), KT - 1]


HEAD_TILES = [(kind, h) for kind in ("mq", "hq", "hi") for h in range(4)] + \
    [("hg", 0), ("hg", 1)] + [("hf", h) for h in range(4)] + [("hg", 2), ("hg", 3)]


def ffn_order(j):
    if j == 0:
        return [("fg", 0, 0), ("fu", 0, 0), ("fg", 1, 0), ("fg", 0, 1), ("fu", 0, 1), ("fg", 1, 1)]
    if j == 1:
        return [("fu", 1, 0), ("fu", 1, 1)]
    return [(kind, j, half) for kind in ("fg", "fu") for half in range(2)]


def weight_units():
    units, outs = [], {}

    def unit(name, k0, nk, c0, nc_):
        units.append((name, k0, nk, c0, nc_))
        return len(units) - 1

    def full(kind, idx, name, c0):
        u = unit(name, 0, KT, c0, P)
        for half in range(2):
            outs[kind, idx, half] = [(u, k, k) for k in range(KT)]

    order = []

    def plan(keys):
        order.extend(keys)

    for idx in range(8):
        u = unit("mem", 0, KT, idx * P, P)
        outs["mem", idx, 0] = [(u, k, k) for k in range(KT)]
        plan([("mem", idx, 0)])
    proj = [("sq", j, None) for j in range(4)] + [("sk", 0, C_SK), ("sv", 0, C_SV)]
    first = {"mq": C_MQ, "hq": C_HQ, "hf": C_HF, "hi": C_HI, "hg": C_HG}
    proj += [(kind, h, first[kind] + h * P) for kind, h in HEAD_TILES]
    for kind, idx, c0 in proj:
        full(kind, idx, "sq" if kind == "sq" else "w_in", idx if kind == "sq" else c0)
    plan([("sq", 0, 0), ("sq", 1, 0), ("sq", 0, 1), ("sq", 1, 1)])
    plan([(kind, idx, half) for kind, idx, _ in proj[2:] for half in range(2)])
    for br in range(3):
        for c in range(0, KT, 2):
            for cc in (c, c + 1):
                full(f"gate{br}", cc, "w_in", C_GATE + GATE_OF[br] * D + cc * P)
                plan([(f"gate{br}", cc, 0), (f"gate{br}", cc, 1)])
            u = unit(f"up{br}", 0, 4, c * P, 2 * P)
            for cc in (c, c + 1):
                for half in range(2):
                    outs[f"up{br}", cc, half] = [(u, 2 * k + cc - c, k) for k in range(4)]
                    plan([(f"up{br}", cc, half)])
    last = None
    for c, half in halves_order(O_TAIL):
        if c != last:
            u, last = unit("w_o", 0, KT, c * P, P), c
        outs["o", c, half] = [(u, k, k) for k in range(KT)]
        plan([("o", c, half)])
    for j in range(FT_):
        for kind, c0 in (("fg", j * P), ("fu", FF + j * P)):
            full(kind, j, "ffn_in", c0)
        plan(ffn_order(j))
    for c, half in halves_order(Y_TAIL):
        if c in Y_PAIRED and half:
            outs["y", c, 1] = parts
            plan([("y", c, 1)])
            continue
        parts = []
        for k0 in range(0, FT_, 8):
            nk = min(8, FT_ - k0)
            u = unit("ffn_out", k0, nk, c * P, P)
            parts += [(u, k, k0 + k) for k in range(nk)]
        outs["y", c, half] = parts
        plan([("y", c, half)])
    return units, outs, order


UNITS, OUTS, ORDER = weight_units()


def schedule():
    steps = [("init",), ("memx", 0), ("x_load",), ("memx", 1)]
    steps += [("split_hi", 0), ("split_lo", 0), ("split_hi", 1), ("split_lo", 1)]
    seen = set()
    number = {}
    beside = {}

    def out(key, late=None, extras=()):
        left, extras = [], list(extras)
        for u, _, _ in OUTS[key]:
            if u not in seen:
                seen.add(u)
                if u + 2 < len(UNITS):
                    (left if late == "all" else steps).append(("split_hi", u + 2))
                    (left if late else steps).append(("split_lo", u + 2))
                steps.extend(extras)
                extras = []
        steps.extend(extras)
        number[key] = len(number)
        steps.append(("out",) + key)
        return left

    att = [("ws",)] + [("w", n, g) for n in range(NBLK) for g in range(2)] + [("mp", n) for n in range(NBLK)]
    att += [("ms", 0), ("ms", 1)]
    hg = [None, None]
    for i, u in enumerate([("h", n, h) for n in range(NBLK + 1) for h in range(4)]):
        hg.append(u)
        if i == 7:
            hg.append(None)
    state = {"side": [], "pos": 0}

    def part(name, i):
        if 0 <= i < len(state["side"]) and state["side"][i] is not None:
            steps.append((name,) + state["side"][i])

    turns = []

    def slot(keys):
        s, left = state["pos"], []
        hgrn = state["side"] is hg
        if hgrn:
            if keys and OUTS[keys[0]][0][0] not in seen:
                u = OUTS[keys[0]][0][0]
                seen.add(u)
                steps.append(("split_hi", u + 2))
                left = [("split_lo", u + 2)]
            part("K", s)
            part("D", s + 1)
            part("N", s - 1)
        old = state["side"][s - 2] if 2 <= s < len(state["side"]) + 2 else None
        if old is not None and old[:2] == ("h", NBLK):
            beside[keys[0]] = old
        if keys:
            left += out(keys[0], late="lo")
            while turns:
                steps.append(turns.pop(0))
        if hgrn:
            part("P", s + 1)
        spread = old is not None and old[0] == "ms"
        if spread:
            beside.update({key: old for key in keys})
        else:
            part("C", s - 2)
        if not hgrn:
            part("N", s - 1)
        for key in keys[1:]:
            out(key)
        if spread:
            part("C", s - 2)
        memory_sample = s < len(state["side"]) and state["side"][s] and state["side"][s][0] == "ms"
        for name, i in (("B", s - 1), ("Q", s), ("A", s)) if memory_sample else (("Q", s), ("B", s - 1), ("A", s)):
            part(name, i)
        steps.extend(left)
        state["pos"] += 1

    for idx in range(8):
        out(("mem", idx, 0))
        if idx:
            steps.append(("turn_mem", idx - 1))
        steps += {1: [("stat", 0), ("stat", 1)], 2: [("stat", 2), ("setup",)],
                  3: [("stat", 3), ("stat", 4), ("rstd0",)] + [("scale0", t) for t in range(NBLK + 1)],
                  4: [("ln0", 0)], 5: [("ln0", 1)], 6: [("ln0", 2)], 7: [("ln0", 3)]}.get(idx, [])
    steps.append(("turn_mem", 7))
    out(("sq", 0, 0))
    steps.append(("ln0", 4))
    left = out(("sq", 1, 0), late="all")
    out(("sq", 0, 1))
    steps += left
    out(("sq", 1, 1))
    for kind, j in (("sq", 2), ("sq", 3), ("sk", 0), ("sv", 0)):
        out((kind, j, 0))
        while turns:
            steps.append(turns.pop(0))
        out((kind, j, 1))
        if kind in ("sk", "sv"):
            turns.append(("turn", kind, j))
    steps.append(("wk",))
    state["side"], state["pos"] = att, 0
    for kind, j in HEAD_TILES:
        slot([(kind, j, 0), (kind, j, 1)])
        if kind == "hi":
            turns.append(("turn", kind, j))
        if (kind, j) == ("hg", 2):
            steps += [("scan", i) for i in range(4)]
    state["side"], state["pos"] = hg, 0
    for br in range(3):
        for c in range(0, KT, 2):
            for kind in (f"gate{br}", f"up{br}"):
                for cc in (c, c + 1):
                    if kind[:4] == "gate" and cc == 0:
                        steps += [("branch", br, j) for j in range(4)]
                    if kind == "up2":
                        for half in range(2):
                            out((kind, cc, half))
                            steps.append(("mix", cc, half))
                        continue
                    after = state["pos"] - len(hg) - 2
                    two = (2 * after, 2 * after + 1) if after in (0, 1) else ()
                    steps += [("rms_squares", h) for h in two]
                    slot([(kind, cc, 0), (kind, cc, 1)])
                    steps += [("rms_sum", h) for h in two]
                    if 2 <= after < 6:
                        steps.append(("rms", after - 2))

    pending = []

    def summed():
        while pending:
            steps.append(pending.pop(0))

    def mean(ln, tail, half, c):
        return ("mean", ln, half, c, c == 0, c == (tail if half else KT - 1))

    extras = {(KT - 5, 1): [("var", 1, 0)], (KT - 6, 1): [("norm", 1, 0)]}
    for c, half in halves_order(O_TAIL):
        out(("o", c, half), extras=extras.get((c, half), ()))
        summed()
        pending.append(mean(1, O_TAIL, half, c))
        if (c, half) == (KT - 1, 1):
            steps += [("center", 1, 0), ("fold", 1)]
    first = ffn_order(0)
    out(first[0])
    summed()
    steps.append(("center", 1, 1))
    late = [out(first[1], late="all")]
    steps += [("var", 1, 1), ("norm", 1, 1)]
    late.append(out(first[2], late="all"))
    out(first[3])
    steps += late[0]
    out(first[4])
    steps += late[1]
    out(first[5])
    for j in range(1, FT_):
        for key in ffn_order(j):
            out(key)
    for c, half in halves_order(Y_TAIL):
        extras = {(KT - 2, 1): [("center", 2, 0), ("fold", 2)], (KT - 3, 1): [("var", 2, 0), ("norm", 2, 0)]}
        out(("y", c, half), extras=extras.get((c, half), ()))
        if not (c in Y_PAIRED and half):
            summed()
        pending.append(mean(2, Y_TAIL, half, c))
        if (c, half) == (KT - 1, 1):
            summed()
    summed()
    steps += [("center", 2, 1), ("store", 0), ("var", 2, 1), ("store", 1), ("store", 2), ("norm", 2, 1)]
    steps += [("store", i) for i in range(3, 6)]
    return steps, number, beside


SCHEDULE, OUT_NO, BESIDE = schedule()
MAIN_BANKS = 3
NRAW, NHI = 4, 3
S0_, S1_, T0_, T1_, V_ = 3, 4, 5, 6, 7
MEAN_BANK = (V_, T1_)
SUM_NO = {}
for _s in SCHEDULE:
    if _s[0] == "mean" and not _s[-1] and _s[-2] is False:
        SUM_NO[_s[1], _s[2]] = max(SUM_NO.values(), default=0) + 1
Y_NO = {}
for _s in SCHEDULE:
    if _s[0] == "out" and _s[1] in ("o", "y"):
        Y_NO[1 + (_s[1] == "y"), _s[3], _s[2]] = len(Y_NO) + 1

OUT_CHUNKS = [(0, 128), (128, 128), (256, 32), (288, 128), (416, 96), (512, 64)]


def build_decoder_layer(nc, a, outs_):
    ctx = ExitStack()
    with ctx:
        place = {"at": 16512}

        def sb(name, shape, dt, offset=None):
            size = int(np.prod(shape[1:])) * mybir.dt.size(dt)
            if offset is None:
                offset = place["at"]
                place["at"] += -(-size // 32) * 32
            return nc.alloc_sbuf_tensor_at(name, list(shape), dt, offset=offset)

        def sem(name):
            return ctx.enter_context(nc.semaphore(name))

        XH = sb("x_hi", [P, KT, T], F32R)
        XL = sb("x_lo", [P, KT, T], F32R)
        raw0 = place["at"]
        RAW = [sb(f"w_raw{i}", [P, 8, P], F32) for i in range(NRAW)]
        WL = [sb(f"w_lo{i}", [P, 8, P], F32R, raw0 + 4096 * i) for i in range(NRAW)]
        WH = [sb(f"w_hi{i}", [P, 8, P], F32R) for i in range(NHI)]
        IDENT = sb("ident", [P, P], F32)
        ONES = sb("ones", [P, P], F32)
        VEC = sb("vectors", [P, 64], F32)
        SMALL = sb("small", [P, 9], F32)
        SINK = sb("sinks8", [P, 9], F32)
        LB = sb("lower_bound", [P, 8], F32)
        LBT = sb("lower_tmp", [P, 12], F32)
        EPS = sb("eps", [P, 2], F32)
        ST = sb("softmax_stats", [P, 2, 28], F32)
        BNS = sb("bn", [P, 5, 12], F32)
        BNV = sb("bn_mean_var", [P, 5, 2], F32)
        BNR = sb("bn_rstd", [P, 5], F32)
        EBL = sb("exp_b_last", [P, 4, NB], F32)
        EX = [sb(f"exp{i}", [P, TH], F32) for i in range(2)]
        sg0 = place["at"]
        SG = [sb(f"gate{i}", [P, TH], F32) for i in range(4)]
        FT = [sb(f"to_turn{i}", [P, T], F32, sg0 + 4 * T * i) for i in range(2)]
        arena = place["at"]
        MIX = sb("mix", [P, KT, T], F32)
        OSH = sb("branch_hi", [P, 4, T], F32R)
        OSL = sb("branch_lo", [P, 4, T], F32R)
        o = arena
        XP = sb("probs", [P, 2, 4, 2 * P], F32, o); o += 8192
        PT = sb("probs_T", [P, 4, 2, P], F32, o); o += 4096
        NEGD = sb("negd", [P, 2 * P], F32, o); o += 1024
        NEGS = sb("negs", [P, 4, WIN + NB * NS], F32, o); o += 3072
        RING = [sb(f"mem_ring{i}", [P, 2, 512], F32, o + 4096 * i) for i in range(4)]; o += 16384
        QM = sb("q_masked", [P, NB, 4, 32], F32, o)
        MKTM = sb("mem_k_tokens", [P, 2, 512], F32, o)
        proj0 = place["at"]
        SQ = sb("sq", [P, 4, T], F32)
        MQ = sb("mq", [P, 4, T], F32)
        HQ = sb("hq", [P, 4, T], F32)
        HB = sb("hb", [P, 4, T], F32)
        HK = sb("hk", [P, 4, T], F32)
        HV = sb("hv", [P, NBLK + 1, 512], F32)
        HG = sb("hg", [P, 4, T], F32)
        skv = place["at"]
        SK = sb("sk", [P, T], F32)
        SV = sb("sv", [P, NBLK + 1, P], F32)
        mkv = place["at"]
        MKT = sb("mem_kT", [P, 4, MEM], F32)
        MV = sb("mem_v", [P, 2, 512], F32)
        hq0 = proj0 + 2 * 4 * T * 4
        MX = [sb(f"mem_x{i}", [P, D], F32, hq0 + 4096 * i) for i in range(2)]
        MH = sb("mem_hi", [P, KT, MEM], F32R, hq0 + 8192)
        ML = sb("mem_lo", [P, KT, MEM], F32R, hq0 + 16384)
        hv0 = hq0 + 3 * 4 * T * 4
        XS = [sb(f"x_tokens{i}", [P, D], F32, arena + 4096 * i if i < 3 else hv0 + 4096 * (i - 3))
              for i in range(5)]
        hg0 = hv0 + (NBLK + 1) * 512 * 4
        XT = [sb(f"x_normed{i}", [P, KT, P], F32, hg0 + 4096 * i) for i in range(2)]
        VR = sb("vector_rows", [64, P], F32, hg0 + 8192)
        E = [sb(f"decay{i}", [P, 8, P], F32, proj0 + 4096 * i) for i in range(2)]
        ASB = [sb(f"a_sum{i}", [P, P], F32, proj0 + 8192 + 512 * i) for i in range(2)]
        hs = place["at"]
        AM = sb("a_masked", [P, 8, P], F32)
        EK = sb("decay_k", [P, 8, P], F32)
        EQ = sb("decay_q", [P, 8, P], F32)
        QE = sb("exp_b", [P, P], F32)
        QW = [sb(f"q_exp_b{i}", [P, P], F32) for i in range(3)]
        KTM = [sb(f"k_tokens{i}", [P, P], F32) for i in range(2)]
        RRS = sb("rms_rstd", [P, 8, TH], F32, hs)
        RSQ = sb("rms_squares", [P, 4, TH], F32, hs + 8 * TH * 4)
        MASKS = sb("masks", [P, 8, P], F32)
        RST = sb("reset", [P, T], BF16)
        STATE = sb("state", [P, 4, P], F32)
        KC = sb("win_k", [P, NB, P], F32, hs)
        VC = sb("win_v", [P, NB, P], F32, hs + 4096)
        KTS = sb("win_kT", [P, NB, P], F32, hs + 8192)
        MKB = [sb(f"mem_kT_batch{i}", [P, 4, MEM], F32, hs + 4096 * i) for i in range(2)]
        SKTM = sb("sk_tokens", [P, 2, P], F32, hs + 12288)
        QSB = sb("sample_q", [P, NB, 32], F32, hs + 13312)
        mq0 = proj0 + 4 * T * 4
        SIN = [sb(f"sample_state{i}", [P, NB, P], F32, o) for i, o in enumerate((mkv, mq0))]
        SOUT = [sb(f"sample_state_new{i}", [P, NB, P], F32, o + 4096) for i, o in enumerate((mkv, mq0))]
        VB = [sb(f"v_by_batch{i}", [64, NB, P], F32, o) for i, o in enumerate((skv, hv0))]
        assert place["at"] <= 229368, place["at"]
        MIXH = sb("mix_hi", [P, KT, T], F32R, proj0)
        MIXL = sb("mix_lo", [P, KT, T], F32R, proj0 + KT * T * 4)
        GH = sb("hidden_hi", [P, FT_, T], F32R, arena)
        GL = sb("hidden_lo", [P, FT_, T], F32R, arena + FT_ * T * 4)
        o = arena + 2 * FT_ * T * 4
        Y = sb("pre_norm", [P, KT, T], F32, o); o += KT * T * 4
        SQR = sb("squares", [P, KT, TH], F32, o); o += KT * TH * 4
        OUTT = [sb(f"out_tokens{i}", [P, D], F32, o + 4096 * i) for i in range(2)]
        assert o + 8192 <= 229368

        BANK = [ctx.enter_context(nc.psum_tensor(f"bank{i}", [P, 512], F32)) for i in range(8)]

        raw_in = [sem(f"raw_in{i}") for i in range(NRAW)]
        w_hi, w_lo, w_lo_pool, w_used, out_ready = sem("w_hi"), sem("w_lo"), sem("w_lo_pool"), sem("w_used"), sem("out_ready")
        bank_free = [sem(f"bank_free{i}") for i in range(8)]
        dve_step, act_step, pool_step = sem("dve_step"), sem("act_step"), sem("pool_step")
        silu_tanh, gate_used, ex_free = sem("silu_tanh"), sem("gate_used"), [sem(f"ex_free{i}") for i in range(2)]
        ident_in, vec_in, sink_in, attc_in, mask_in = (
            sem(n) for n in ("ident_in", "vec_in", "sink_in", "attc_in", "mask_in"))
        memx_in = [sem(f"memx_in{i}") for i in range(2)]
        xs_in = [sem(f"xs_in{i}") for i in range(5)]
        vecT_ready, lb_shifted, lb_exp = (sem(n) for n in ("vecT_ready", "lb_shifted", "lb_exp"))
        x_var, x_rstd, x_scaled, xT_ready, x_lo_done = (
            sem(n) for n in ("x_var", "x_rstd", "x_scaled", "xT_ready", "x_lo_done"))
        memT_ready, mem_hi_done, turn_ready = sem("memT_ready"), sem("mem_hi_done"), sem("turn_ready")
        f_ready, logf_done, b_ready = sem("f_ready"), sem("logf_done"), sem("b_ready")
        cache_in, cacheT_ready, sample_q = sem("cache_in"), sem("cacheT_ready"), sem("sample_q")
        ring_in = [sem(f"ring_in{i}") for i in range(4)]
        ring_used, memK_turned, mkb_used, qm_ready = (
            sem(n) for n in ("ring_used", "memK_turned", "mkb_used", "qm_ready"))
        scores_ready, max_ready, p_exp, p_ready, pT_ready, pv_ready = (
            sem(n) for n in ("scores_ready", "max_ready", "p_exp", "p_ready", "pT_ready", "pv_ready"))
        d_ready, e_ready, ekq_ready, a_ready, a_sum, kT_ready, ho_ready = (
            sem(n) for n in ("d_ready", "e_ready", "ekq_ready", "a_ready", "a_sum", "kT_ready", "ho_ready"))
        vb_ready, state_decayed, kv_stored = (sem(n) for n in ("vb_ready", "state_decayed", "kv_stored"))
        state_in, state_out = ([sem(f"{n}{i}") for i in range(2)] for n in ("state_in", "state_out"))
        rms_sq, rms_sum, rms_rstd, branch_split = (
            sem(n) for n in ("rms_sq", "rms_sum", "rms_rstd", "branch_split"))
        mix_split, y_ready, mean_ready, centered, squared, var_ready, ln_rstd = (
            sem(n) for n in ("mix_split", "y_ready", "mean_ready", "centered", "squared", "var_ready", "ln_rstd"))
        hidden_done, ln_scaled, ln_hi, outT_ready = (
            sem(n) for n in ("hidden_done", "ln_scaled", "ln_hi", "outT_ready"))
        tiles_summed, folded = sem("tiles_summed"), sem("folded")
        ln_lo = [sem(f"ln_lo{i}") for i in range(2)]
        out_dma = [sem(f"out_dma{i}") for i in range(2)]
        cache_moved, prompt_state_out = sem("cache_moved"), sem("prompt_state_out")

        vec = {n: VEC[:, 8 * i:8 * i + 8] for i, n in
               enumerate(("ln0_w", "ln0_b", "ln1_w", "ln1_b", "ln2_w", "ln2_b", "hg_lb"))}
        NORMW = VEC[:, 56:57]
        att_units = [s[1:] for s in SCHEDULE if s[0] == "A" and s[1] != "h"]
        att_no = {u: i for i, u in enumerate(att_units)}
        n_att = len(att_units)
        hg_units = [s[1:] for s in SCHEDULE if s[0] == "A" and s[1] == "h"]
        hg_no = {u: i for i, u in enumerate(hg_units)}

        first_use, last_use = {}, {}
        for key in ORDER:
            for n, (u, _, _) in enumerate(OUTS[key]):
                first_use.setdefault(u, (key, n))
                last_use[u] = (key, n)
        inner_uses = [u for u in range(len(UNITS)) if last_use[u][1] < len(OUTS[last_use[u][0]]) - 1]
        inner_no = {u: i + 1 for i, u in enumerate(inner_uses)}

        def unit_used(eng, u):
            if u in inner_no:
                eng.wait_ge(w_used, inner_no[u])
            else:
                eng.wait_ge(out_ready, OUT_NO[last_use[u][0]] + 1)

        def main_bank(key):
            return OUT_NO[key] % MAIN_BANKS

        def out_saved(eng, key):
            eng.wait_ge(bank_free[main_bank(key)], OUT_NO[key] // MAIN_BANKS + 1)

        bank_use = {}

        def saved(eng, *what):
            bank, count = bank_use[what]
            eng.wait_ge(bank_free[bank], count)

        def moving(key, k):
            kind, _, half = key
            cols = slice(half * TH, half * TH + TH)
            if kind == "mem":
                return MH[:, k, :], ML[:, k, :]
            if kind[:2] == "up":
                return OSH[:, k, cols], OSL[:, k, cols]
            if kind == "o":
                return MIXH[:, k, cols], MIXL[:, k, cols]
            if kind == "y":
                return GH[:, k, cols], GL[:, k, cols]
            return XH[:, k, cols], XL[:, k, cols]

        def bcast(ap, n):
            return ap.unsqueeze(2).to_broadcast([ap.shape[0], ap.shape[1], n])

        def over(ap, n):
            return ap.unsqueeze(1).to_broadcast([ap.shape[0], n, ap.shape[1]])

        def f32(ap):
            return ap.bitcast(F32)

        def unit_source(u):
            name, k0, nk, c0, ncols = UNITS[u]
            raw = RAW[u % NRAW]
            if name == "sq":
                w = a["w_in"].rearrange("(k p) n -> p k n", p=P)
                return [(raw[:, :, 0:64], w[:, :, c0 * 64:c0 * 64 + 64]),
                        (raw[:, :, 64:128], w[:, :, (c0 + 4) * 64:(c0 + 4) * 64 + 64])]
            if name == "up0":
                w = a["w_up_sw"].rearrange("(g k p) n -> g p k n", g=2, p=64)
                v = raw[:, :, :].rearrange("p (k c) n -> p k (c n)", k=4)
                return [(v[64 * g:64 * g + 64], w[g, :, :, c0:c0 + ncols]) for g in range(2)]
            src = {"mem": "w_mem_kv", "w_in": "w_in", "up1": "w_up_mx", "up2": "w_up_hg", "w_o": "w_o",
                   "ffn_in": "w_ffn_in", "ffn_out": "w_ffn_out"}[name]
            w = a[src].rearrange("(k p) n -> p k n", p=P)[:, k0:k0 + nk, c0:c0 + ncols]
            if ncols == 2 * P:
                return [(raw[:, :, :].rearrange("p (k c) n -> p k (c n)", k=4), w)]
            return [(raw[:, 0:nk, :], w)]

        raw_count, raw_full = [0] * NRAW, {}
        for u in range(len(UNITS)):
            raw_count[u % NRAW] += 16 * len(unit_source(u))
            raw_full[u] = raw_count[u % NRAW]

        def unit_tiles(u):
            return UNITS[u][2] * UNITS[u][4] // P

        EARLY_UNITS = range(4, 10)
        POOL_UNITS = [*EARLY_UNITS] + [OUTS[f"gate{br}", c, 0][0][0] for br in range(2) for c in range(KT)]
        VECTOR_UNITS = [u for u in range(len(UNITS)) if u not in POOL_UNITS]

        def split_lo(eng, u):
            eng.wait_ge(w_hi, u + 1)
            n = unit_tiles(u)
            eng.tensor_tensor(WL[u % NRAW][:, 0:n, :], RAW[u % NRAW][:, 0:n, :], f32(WH[u % NHI][:, 0:n, :]),
                              ALU.subtract).then_inc(w_lo_pool if u in POOL_UNITS else w_lo, 1)

        def lo_split(eng, u):
            if u in POOL_UNITS:
                eng.wait_ge(w_lo_pool, POOL_UNITS.index(u) + 1)
            else:
                eng.wait_ge(w_lo, VECTOR_UNITS.index(u) + 1)

        def hg_cols(n):
            return (P * n, P, LEVELS) if n < NBLK else (SEQ, NB * NS, SAMPLE_LEVELS)

        def lo_of(u):
            return P if u[:2] == ("w", 0) else 0

        def keys_free(eng, b):
            eng.wait_ge(memK_turned, b + 1)
            if b >= 2:
                last = b - 2
                if last % 4 < 3:
                    eng.wait_ge(mkb_used, 3 * (last // 4) + last % 4 + 1)
                else:
                    eng.wait_ge(scores_ready, att_no["ms", last // 4] + 1)

        SILU = ("hq", "hg", "fg")
        gate_used_no = {key: i + 1 for i, key in enumerate(k for k in ORDER if k[0][:2] == "up")}

        def sig_dst(key):
            kind, idx, half = key
            cols = slice(half * TH, half * TH + TH)
            if kind in ("hq", "hg", "hf"):
                return {"hq": HQ, "hg": HG, "hf": HB}[kind][:, idx, cols]
            return SG[2 * (idx % 2) + half][:]

        def level_view(ap, m):
            return ap.rearrange("p (b m) -> p b m", m=2 * m)

        block = ctx.enter_context(nc.Block())

        @block.tensor
        def _(pe):
            uses = [0] * 8

            def take(bank, *what):
                if uses[bank]:
                    pe.wait_ge(bank_free[bank], uses[bank])
                uses[bank] += 1
                if what:
                    bank_use[what] = (bank, uses[bank])
                return BANK[bank]

            def main(key):
                kind, idx, half = key
                if kind == "y" and idx in Y_PAIRED:
                    if half == 0:
                        main_pair(idx)
                    return
                bank = take(main_bank(key))
                if kind == "mem":
                    saved(pe, "memx", 1, 0)
                    saved(pe, "memx", 1, 1)
                elif kind[:2] != "up" and kind not in ("o", "fg", "fu", "y"):
                    pe.wait_ge(x_lo_done, 5 if half else 3)
                parts = OUTS[key]
                n = MEM if kind == "mem" else TH
                for i, (u, tile, k) in enumerate(parts):
                    if first_use[u] == (key, i):
                        pe.wait_ge(w_hi, u + 1)
                        lo_split(pe, u)
                    if kind == "fg" and idx == 0:
                        pe.wait_ge(ln_lo[half], k + 1)
                    elif kind[:2] == "up" and idx == 0:
                        pe.wait_ge(branch_split, 4 * int(kind[2]) + k + 1)
                    elif kind == "o" and idx == 0:
                        pe.wait_ge(mix_split, 2 * k + half + 1)
                    hi, lo = moving(key, k)
                    wh, wl = WH[u % NHI][:, tile, :], WL[u % NRAW][:, tile, :]
                    pe.matmul(bank[:, 0:n], wh, lo, start=(i == 0), stop=False)
                    pe.matmul(bank[:, 0:n], wl, hi, start=False, stop=False)
                    mm = pe.matmul(bank[:, 0:n], wh, hi, start=False, stop=(i == len(parts) - 1))
                    if last_use[u] == (key, i) and u in inner_no:
                        mm.then_inc(w_used, 1)
                    if i == len(parts) - 1:
                        mm.then_inc(out_ready, 1)
                    if key in BESIDE:
                        if BESIDE[key][0] == "ms":
                            sample_values(BESIDE[key], KT * half + i)
                        else:
                            sample_state_out(BESIDE[key], i, len(parts))

            def main_pair(c):
                keys = ("y", c, 0), ("y", c, 1)
                banks = [take(main_bank(key)) for key in keys]
                parts = OUTS[keys[0]]
                for unit in dict.fromkeys(u for u, _, _ in parts):
                    pe.wait_ge(w_hi, unit + 1)
                    lo_split(pe, unit)
                    for half in range(2):
                        bank = banks[half]
                        if c == 0:
                            pe.wait_ge(hidden_done, 2 * max(k for u, _, k in parts if u == unit) + half + 1)
                        for i, (u, tile, k) in enumerate(parts):
                            if u != unit:
                                continue
                            hi, lo = moving(keys[half], k)
                            wh, wl = WH[u % NHI][:, tile, :], WL[u % NRAW][:, tile, :]
                            pe.matmul(bank[:, 0:TH], wh, lo, start=(i == 0), stop=False)
                            pe.matmul(bank[:, 0:TH], wl, hi, start=False, stop=False)
                            mm = pe.matmul(bank[:, 0:TH], wh, hi, start=False, stop=(i == len(parts) - 1))
                            if last_use[u] == (keys[half], i) and u in inner_no:
                                mm.then_inc(w_used, 1)
                        if unit == parts[-1][0]:
                            mm.then_inc(out_ready, 1)

            n_ring = [0]

            def ring_tile():
                i = n_ring[0]
                pe.wait_ge(ring_in[i % 4], 16 * (i // 4 + 1))
                n_ring[0] += 1
                return RING[i % 4]

            def turn_keys(b):
                keys = ring_tile()
                for s in range(2):
                    bank = take(T0_ + s, "memK", b, s)
                    for hh in range(2):
                        for c in range(2):
                            h = 2 * s + hh
                            mm = pe.transpose(bank[:, 256 * hh + P * c:256 * hh + P * c + P],
                                              keys[:, c, P * h:P * h + P], IDENT[:])
                mm.then_inc(memK_turned, 1)

            def scores(u):
                kind, no = u[0], att_no[u]
                if kind == "w":
                    n, g = u[1:]
                    lo = lo_of(u)
                    for kv in range(2):
                        bank = take(S0_ + kv, "scores", no, kv)
                        for jj in range(2):
                            mm = pe.matmul(bank[:, 256 * jj + lo:256 * jj + 256],
                                           SQ[64 * kv:64 * kv + 64, 2 * g + jj, P * n:P * n + P],
                                           SK[64 * kv:64 * kv + 64, P * (n - 1) + lo:P * (n + 1)],
                                           start=True, stop=True)
                elif kind == "ws":
                    out_saved(pe, ("sk", 0, 1))
                    saved(pe, "cacheT", 0)
                    saved(pe, "cacheT", 1)
                    pe.wait_ge(sample_q, 1)
                    banks = [take(S0_, "scores", no, 0), take(S1_, "scores", no, 1)]
                    for kv in range(2):
                        for b in range(NB):
                            r, c = b // 2, 2 * (b % 2) + kv
                            dst = banks[r // 2][32 * c:32 * c + 32, 192 * (r % 2):192 * (r % 2) + 192]
                            q = QSB[64 * kv:64 * kv + 64, b, :]
                            pe.matmul(dst[:, 0:WIN], q, KTS[64 * kv:64 * kv + 64, b, :], start=True, stop=True)
                            mm = pe.matmul(dst[:, WIN:192], q, SK[64 * kv:64 * kv + 64, SEQ:T],
                                           start=True, stop=True)
                elif kind == "mp":
                    n = u[1]
                    out_saved(pe, ("mq", 3, 1))
                    for s in range(4):
                        if s % 2 == 0:
                            bank = take(S0_ + s // 2, "scores", no, s // 2)
                        mm = pe.matmul(bank[:, 256 * (s % 2):256 * (s % 2) + 256], MQ[:, s, P * n:P * n + P],
                                       MKT[:, s, :], start=True, stop=True)
                else:
                    pe.wait_ge(qm_ready, NB)
                    bank = take(S0_, "scores", no, 0)
                    turn_keys(4 * u[1])
                    for bl in range(4):
                        b = 4 * u[1] + bl
                        if bl < 3:
                            turn_keys(b + 1)
                        for s in range(2):
                            saved(pe, "memK", b, s)
                        for h in range(4):
                            mm = pe.matmul(bank[32 * h:32 * h + 32, 0:256], QM[:, b, h, :], MKB[b % 2][:, h, :],
                                           start=(bl == 0), stop=(bl == 3), skip_group_check=True)
                        if bl < 3:
                            mm.then_inc(mkb_used, 1)
                mm.then_inc(scores_ready, 1)

            def turn_probs(u):
                kind, no = u[0], att_no[u]
                probs = XP[:, no % 2]
                pe.wait_ge(p_ready, no + 1)
                if kind == "ws":
                    b0, b1 = take(T0_, "pT", no, 0), take(T1_, "pT", no, 1)
                    for r in range(4):
                        pe.transpose(b0[:, P * r:P * r + P], probs[:, r, 0:P], IDENT[:])
                        mm = pe.transpose(b1[0:64, P * r:P * r + P], probs[:, r, P:192], IDENT[:])
                elif kind == "ms":
                    b0 = take(T0_, "pT", no, 0)
                    for c in range(2):
                        mm = pe.transpose(b0[:, P * c:P * c + P], probs[:, 0, P * c:P * c + P], IDENT[:])
                else:
                    for s in range(4):
                        if s % 2 == 0:
                            bank = take(T0_ + s // 2, "pT", no, s // 2)
                        for c in range(lo_of(u) // P, 2):
                            col = 256 * (s % 2) + P * c
                            mm = pe.transpose(bank[:, col:col + P], probs[:, s, P * c:P * c + P], IDENT[:])
                mm.then_inc(pT_ready, 1)

            def values(u):
                kind, no = u[0], att_no[u]
                saved(pe, "pT", no, 0)
                saved(pe, "pT", no, 1)
                ptf = PT[:].rearrange("p a c t -> p (a c t)")
                bank = take(V_, "pv", no)
                if kind == "w":
                    n, g = u[1:]
                    c0 = lo_of(u) // P
                    for kv in range(2):
                        for c in range(c0, 2):
                            mm = pe.matmul(bank[64 * kv:64 * kv + 64, 0:256], SV[:, n - 1 + c, 64 * kv:64 * kv + 64],
                                           PT[:, 2 * kv:2 * kv + 2, c, :], start=(c == c0), stop=(c == 1))
                elif kind == "ws":
                    for kv in range(2):
                        for b in range(NB):
                            r, c = b // 2, 2 * (b % 2) + kv
                            dst = bank[64 * kv:64 * kv + 64, 32 * b:32 * b + 32]
                            col = P * r + 32 * c
                            pe.matmul(dst, VC[:, b, 64 * kv:64 * kv + 64], ptf[:, col:col + 32],
                                      start=True, stop=False)
                            mm = pe.matmul(dst, SV[0:64, NBLK, 64 * kv:64 * kv + 64],
                                           ptf[0:64, 512 + col:512 + col + 32], start=False, stop=True)
                else:
                    for h in range(4):
                        for c in range(2):
                            mm = pe.matmul(bank[:, P * h:P * h + P], MV[:, c, P * h:P * h + P], PT[:, h, c, :],
                                           start=(c == 0), stop=(c == 1))
                mm.then_inc(pv_ready, 1)

            vals = [None]

            def sample_values(u, i):
                no = att_no[u]
                bl, h = i // 4, i % 4
                if i == 0:
                    saved(pe, "pT", no, 0)
                    take(V_, "pv", no)
                if h == 0:
                    vals[0] = ring_tile()
                ptf = PT[:].rearrange("p a c t -> p (a c t)")
                col = 32 * h + 8 * bl
                for c in range(2):
                    mm = pe.matmul(BANK[V_][:, col:col + 8], vals[0][:, c, P * h:P * h + P],
                                   ptf[:, P * c + col:P * c + col + 8], start=(c == 0), stop=(c == 1))
                if h == 3:
                    mm.then_inc(ring_used if bl < 3 else pv_ready, 1)

            def hgrn_pairs(u):
                _, n, h = u
                no = hg_no[u]
                t0, w, levels = hg_cols(n)
                cols = slice(t0, t0 + w)
                nl = len(levels)
                pe.wait_ge(ekq_ready, no + 1)
                for i in range(nl + 1):
                    if i % 4 == 0:
                        bank = take(S0_ + i // 4, "a", no, i // 4)
                    k, q = (EK[:, i, 0:w], EQ[:, i, 0:w]) if i < nl else (HK[:, h, cols], HQ[:, h, cols])
                    mm = pe.matmul(bank[0:w, P * (i % 4):P * (i % 4) + w], k, q, start=True, stop=True)
                mm.then_inc(a_ready, 1)
                bank = take(T0_, "kT", no)
                pe.transpose(bank[0:w, 0:P], EK[:, 7, 0:w], IDENT[:]).then_inc(kT_ready, 1)

            def hgrn_out(u):
                _, n, h = u
                no = hg_no[u]
                _, w, _ = hg_cols(n)
                v = HV[0:w, n, P * h:P * h + P]
                if n < NBLK:
                    pe.wait_ge(a_sum, no + 1)
                    saved(pe, "kT", no)
                    if n:
                        saved(pe, "state", no - 4)
                    bank = take(V_, "ho", no)
                    pe.matmul(bank[:, 0:P], v, ASB[no % 2][:], start=True, stop=(n == 0))
                    if n:
                        pe.matmul(bank[:, 0:P], STATE[:, h, :], QW[no % 3][:], start=False, stop=True)
                    sbank = take(T1_, "state", no)
                    mm = pe.matmul(sbank[:, 0:P], KTM[no % 2][:], v, start=True, stop=True)
                else:
                    pe.wait_ge(vb_ready, h + 1)
                    for i in range(2):
                        sbank = take(T0_ + i, "state", no, i)
                        mm = pe.matmul(sbank[:, :], KTM[no % 2][0:w, :], VB[h % 2][:, 4 * i:4 * i + 4, :],
                                       start=True, stop=True)
                mm.then_inc(ho_ready, 1)

            def sample_state_out(u, i, n_parts):
                _, n, h = u
                no = hg_no[u]
                w = NB * NS
                bank = BANK[V_]
                if i == 0:
                    pe.wait_ge(a_sum, no + 1)
                    saved(pe, "kT", no)
                    pe.wait_ge(state_in[h % 2], 16 * (h // 2 + 1))
                    take(V_, "ho", no)
                    pe.matmul(bank[:, 0:w], HV[0:w, n, P * h:P * h + P], ASB[no % 2][0:w, 0:w], start=True, stop=False,
                              skip_group_check=True)
                for b in range(NB // n_parts * i, NB // n_parts * (i + 1)):
                    pe.matmul(bank[:, NS * b:NS * b + NS], SIN[h % 2][:, b, :], QW[no % 3][:, NS * b:NS * b + NS],
                              start=False, stop=(b == NB - 1), skip_group_check=True)

            for s in SCHEDULE:
                what, rest = s[0], s[1:]
                if what == "out":
                    main(rest)
                elif what == "setup":
                    pe.wait_ge(vec_in, 128)
                    pe.transpose(take(V_, "vec")[:, 0:57], VR[0:57, :], IDENT[0:57, 0:57]).then_inc(vecT_ready, 1)
                elif what == "memx":
                    t = rest[0]
                    if t == 0:
                        pe.wait_ge(ident_in, 16)
                    pe.wait_ge(memx_in[t], 16)
                    for i in range(2):
                        bank = take(T0_ + i, "memx", t, i)
                        for k in range(4):
                            mm = pe.transpose(bank[:, P * k:P * k + P],
                                              MX[t][:, P * (4 * i + k):P * (4 * i + k) + P], IDENT[:])
                    mm.then_inc(memT_ready, 1)
                elif what == "ln0":
                    t = rest[0]
                    n = TOKENS[t][1]
                    pe.wait_ge(x_scaled, t + 1)
                    for i in range(2):
                        bank = take(T0_ + i, "xT", t, i)
                        for k in range(4):
                            mm = pe.transpose(bank[:, P * k:P * k + n],
                                              XS[t][0:n, P * (4 * i + k):P * (4 * i + k) + P],
                                              IDENT[0:n, 0:n])
                    mm.then_inc(xT_ready, 1)
                elif what == "turn_mem":
                    idx = rest[0]
                    out_saved(pe, ("mem", idx, 0))
                    src = MKT[:, idx, :] if idx < 4 else FT[idx % 2][:, 0:MEM]
                    bank = take(V_, "turn_mem", idx)
                    for c in range(2):
                        mm = pe.transpose(bank[:, P * c:P * c + P], src[:, P * c:P * c + P], IDENT[:])
                    mm.then_inc(turn_ready, 1)
                elif what == "turn":
                    kind, idx = rest
                    out_saved(pe, (kind, idx, 0))
                    out_saved(pe, (kind, idx, 1))
                    b0, b1 = take(T0_, "turn", kind, idx, 0), take(T1_, "turn", kind, idx, 1)
                    src = SK if kind == "sk" else FT[idx % 2]
                    for t, (t0, n) in enumerate(TOKENS):
                        if kind == "sk" and t < NBLK - 1:
                            continue
                        dst = b0[0:n, P * t:P * t + P] if t < NBLK else b1[0:n, 0:P]
                        mm = pe.transpose(dst, src[:, t0:t0 + n], IDENT[:])
                    mm.then_inc(turn_ready, 1)
                elif what == "wk":
                    pe.wait_ge(cache_in, 32)
                    for i in range(2):
                        bank = take(T0_ + i, "cacheT", i)
                        for k in range(4):
                            mm = pe.transpose(bank[:, P * k:P * k + P], KC[:, 4 * i + k, :], IDENT[:])
                    mm.then_inc(cacheT_ready, 1)
                elif what == "Q":
                    (hgrn_pairs if rest[0] == "h" else scores)(rest)
                elif what == "B" and rest[0] != "h":
                    turn_probs(rest)
                elif what == "C" and rest[0] != "ms":
                    (hgrn_out if rest[0] == "h" else values)(rest)
                elif what == "rms_sum":
                    h = rest[0]
                    for half in range(2):
                        pe.wait_ge(rms_sq, 2 * h + half + 1)
                        bank = take((V_, T1_)[half], "rms", h, half)
                        pe.matmul(bank[:, 0:TH], ONES[:], RSQ[:, 2 * (h % 2) + half, :], start=True,
                                  stop=True).then_inc(rms_sum, 1)
                elif what == "mean" and rest[-1]:
                    ln, half, c, _, _ = rest
                    bank = take(MEAN_BANK[half], "mean", ln, half)
                    pe.wait_ge(tiles_summed, SUM_NO[ln, half])
                    pe.matmul(bank[:, 0:TH], ONES[:], EX[half][:], start=True, stop=False)
                    pe.wait_ge(y_ready, Y_NO[ln, half, c])
                    pe.matmul(bank[:, 0:TH], ONES[:], Y[:, c, half * TH:half * TH + TH], start=False, stop=True)\
                        .then_inc(mean_ready, 1)
                elif what == "var":
                    ln, half = rest
                    bank = take(T0_, "var", ln, half)
                    if half == 0:
                        pe.wait_ge(folded, ln)
                        mm = pe.matmul(bank[:, 0:TH], ONES[:], SQR[:, 0, :], start=True, stop=True)
                    else:
                        for c in range(KT):
                            pe.wait_ge(squared, 16 * (ln - 1) + 8 + c + 1)
                            mm = pe.matmul(bank[:, 0:TH], ONES[:], SQR[:, c, :], start=(c == 0), stop=(c == KT - 1))
                    mm.then_inc(var_ready, 1)
                elif what == "store":
                    i = rest[0]
                    t0, n = OUT_CHUNKS[i]
                    for j in range(2):
                        pe.wait_ge(ln_hi, 16 + 8 * (i // 3) + 4 * j + 4)
                        bank = take((S0_, T1_)[i % 2] if j else (S1_, V_)[i % 2], "outT", i, j)
                        for k in range(4):
                            mm = pe.transpose(bank[0:n, P * k:P * k + P], Y[:, 4 * j + k, t0:t0 + n], IDENT[:])
                    mm.then_inc(outT_ready, 1)

        @block.sync
        def _(sp):
            sp.dma_start(IDENT[:], a["c_ident"]).then_inc(ident_in, 16)
            for i in range(2):
                sp.dma_start(MX[i][:], a["mem_prompt"][P * i:P * i + P, :]).then_inc(memx_in[i], 16)
            for u in range(len(UNITS)):
                if u >= NRAW:
                    unit_used(sp, u - NRAW)
                for dst, src in unit_source(u):
                    sp.dma_start(dst, src).then_inc(raw_in[u % NRAW], 16)
            for i, (t0, n) in enumerate(OUT_CHUNKS):
                saved(sp, "outT", i, 0)
                saved(sp, "outT", i, 1)
                dst = outs_["y_p"][t0:t0 + n, :] if t0 < SEQ else outs_["y_s"]
                sp.dma_start(dst, OUTT[i % 2][0:n, :]).then_inc(out_dma[i % 2], 16)
            for s in out_dma:
                sp.wait_ge(s, 48)

        @block.gpsimd
        def _(pool):
            def load(sem_, dst, src):
                pool.dma_start(dst, src).then_inc(sem_, 16)

            for i, n in enumerate(("ln0_w", "ln0_b", "ln1_w", "ln1_b", "ln2_w", "ln2_b")):
                load(vec_in, VR[8 * i:8 * i + 8, :], a[n].rearrange("(k p) -> k p", p=P))
            load(vec_in, VR[48:56, :], a["hg_lb"].rearrange("l (k p) -> (l k) p", p=P))
            load(vec_in, VR[56:57, :], a["hg_norm_w"])
            load(sink_in, SINK[:], a["sink_rows"])
            load(attc_in, SMALL[:], a["c_small"])
            load(attc_in, NEGD[:], a["c_negd"])
            load(attc_in, NEGS[:], a["c_negs"])
            for u in EARLY_UNITS:
                split_lo(pool, u)
            load(cache_in, KC[:], a["cache_k"].rearrange("b s f -> s b f"))
            load(cache_in, VC[:], a["cache_v"].rearrange("b s f -> s b f"))
            load(mask_in, MASKS[:], a["c_masks"])
            def load_ring(i):
                if 4 <= i < 12:
                    pool.wait_ge(memK_turned, i - 3)
                elif 12 <= i < 15:
                    pool.wait_ge(ring_used, i - 11)
                elif i == 15:
                    pool.wait_ge(pv_ready, att_no["ms", 0] + 1)
                src = a["mem_k_s"] if i < 8 else a["mem_v_s"]
                load(ring_in[i % 4], RING[i % 4][:], src[i % 8].rearrange("(c p) n -> p c n", p=P))

            for j in range(4):
                out_saved(pool, ("sq", j, 1))
            pool.tensor_copy(QSB[:].rearrange("p b (j i) -> p b j i", j=4),
                             SQ[:, :, SEQ:T].rearrange("p j (b i) -> p b j i", b=NB)).then_inc(sample_q, 1)
            for i in range(4):
                load_ring(i)
            load(cache_moved, outs_["k_win_s"][:, 0:WIN - NS, :], a["cache_k"][:, NS:WIN, :])
            load(cache_moved, outs_["v_win_s"][:, 0:WIN - NS, :], a["cache_v"][:, NS:WIN, :])
            for idx in range(8):
                saved(pool, "turn_mem", idx)
            for name, buf in (("mem_k_p", MKTM), ("mem_v_p", MV)):
                load(kv_stored, outs_[name].rearrange("(c p) n -> p c n", p=P), buf[:])
            saved(pool, "turn", "sk", 0, 0)
            saved(pool, "turn", "sk", 0, 1)
            load(kv_stored, outs_["k_win_p"], SKTM[:, 0, :])
            load(kv_stored, outs_["k_win_s"][:, WIN - NS:WIN, :], SKTM[0:64, 1, :])
            saved(pool, "turn", "sv", 0, 0)
            saved(pool, "turn", "sv", 0, 1)
            load(kv_stored, outs_["v_win_p"], SV[:, 3, :])
            load(kv_stored, outs_["v_win_s"][:, WIN - NS:WIN, :], SV[0:64, NBLK, :])
            pool.wait_ge(kv_stored, 96)
            pool.memset(QM[:], 0.0).then_inc(pool_step, 1)
            pool.wait_ge(pool_step, 1)
            for h in range(4):
                out_saved(pool, ("mq", h, 1))
            for b in range(NB):
                o8 = NS * (b % 4)
                pool.tensor_copy(QM[:, b, :, o8:o8 + NS], MQ[:, :, SEQ + NS * b:SEQ + NS * b + NS])\
                    .then_inc(qm_ready, 1)
            for i in range(4, 16):
                load_ring(i)
            def hgrn_distances(u):
                _, n, h = u
                t0, w, levels = hg_cols(n)
                no = hg_no[u]
                e = E[no % 2]
                if no == 0:
                    pool.wait_ge(branch_split, 4)
                    pool.wait_ge(b_ready, 4)
                if no >= 2:
                    pool.wait_ge(ekq_ready, no - 1)
                b = HB[:, h, t0:t0 + w]
                for i, m in enumerate(levels):
                    v = level_view(b, m)
                    pool.tensor_tensor(level_view(e[:, i, 0:w], m), v,
                                      v[:, :, m - 1:m].to_broadcast([P, w // (2 * m), 2 * m]), ALU.subtract)
                c = w if n < NBLK else NS
                v = b.rearrange("p (b m) -> p b m", m=c)
                pool.tensor_tensor(e[:, 7, 0:w].rearrange("p (b m) -> p b m", m=c), v,
                                  v[:, :, c - 1:c].to_broadcast([P, w // c, c]), ALU.subtract).then_inc(d_ready, 1)

            def load_states(h):
                load(state_in[h % 2], SIN[h % 2][:], a["state_in"][:, h].rearrange("b d e -> d b e"))

            pool.wait_ge(pv_ready, n_att)
            load_states(0)
            n_sums, last_sum = 0, [0, 0]
            for s in SCHEDULE:
                if s[0] == "D" and s[1] == "h":
                    hgrn_distances(s[1:])
                elif s[:3] == ("N", "h", NBLK):
                    h = s[3]
                    no = hg_no["h", NBLK, h]
                    if h == 0:
                        pool.wait_ge(branch_split, 8)
                        load_states(1)
                    if h:
                        pool.wait_ge(ho_ready, no - 1)
                    pool.tensor_tensor(VB[h % 2][:, :, :], over(HV[0:NB * NS, NBLK, P * h:P * h + P], NB),
                                       bcast(SMALL[0:NB * NS, 1:9], P), ALU.mult).then_inc(vb_ready, 1)
                    pool.wait_ge(e_ready, no + 1)
                    pool.wait_ge(state_in[h % 2], 16 * (h // 2 + 1))
                    if h >= 2:
                        pool.wait_ge(state_out[h % 2], 16)
                    pool.tensor_tensor(SOUT[h % 2][:], SIN[h % 2][:], bcast(EBL[:, no % 4, :], P), ALU.mult)\
                        .then_inc(state_decayed, 1)
                elif s[:3] == ("C", "h", NBLK):
                    h = s[3]
                    no = hg_no["h", NBLK, h]
                    if h == 0:
                        for hh in range(4):
                            saved(pool, "state", hg_no["h", NBLK - 1, hh])
                        load(prompt_state_out, outs_["state_p"].rearrange("h d e -> d h e"), STATE[:])
                    pool.wait_ge(ho_ready, no + 1)
                    saved(pool, "state", no, 0)
                    saved(pool, "state", no, 1)
                    load(state_out[h % 2], outs_["state_s"][:, h].rearrange("b d e -> d b e"), SOUT[h % 2][:])
                    if h < 2:
                        load_states(h + 2)
                elif s[0] == "split_lo" and s[1] in POOL_UNITS and s[1] not in EARLY_UNITS:
                    split_lo(pool, s[1])
                elif s[0] == "mean" and not s[4] and not s[5]:
                    _, ln, half, c, _, _ = s
                    pool.wait_ge(y_ready, Y_NO[ln, half, c])
                    second = last_sum[half] in (0, SUM_NO[1, half])
                    if not second:
                        pool.wait_ge(tiles_summed, last_sum[half])
                    elif ln == 2:
                        pool.wait_ge(mean_ready, half + 1)
                    cols = slice(half * TH, half * TH + TH)
                    pool.tensor_tensor(EX[half][:], Y[:, 0, cols] if second else EX[half][:], Y[:, c, cols], ALU.add)\
                        .then_inc(tiles_summed, 1)
                    n_sums += 1
                    last_sum[half] = n_sums
                elif s[0] == "fold":
                    ln = s[1]
                    pool.wait_ge(squared, 16 * (ln - 1) + KT)
                    for i, n in enumerate((4, 2, 1)):
                        if i:
                            pool.wait_ge(pool_step, 2 * ln + i - 1)
                        pool.tensor_tensor(SQR[:, 0:n, :], SQR[:, 0:n, :], SQR[:, n:2 * n, :], ALU.add)\
                            .then_inc(pool_step if n > 1 else folded, 1)
            pool.wait_ge(cache_moved, 32)
            pool.wait_ge(kv_stored, 96)
            pool.wait_ge(prompt_state_out, 16)
            pool.wait_ge(state_out[0], 32)
            pool.wait_ge(state_out[1], 32)

        @block.scalar
        def _(act):
            steps = [0]
            ex_use = [0, 0]
            n_turn = [0]

            def wait_gate_free(key):
                kind, idx, half = key
                if kind == "fg":
                    if idx >= 2:
                        out_saved(act, ("fu", idx - 2, half))
                        act.wait_ge(hidden_done, 2 * (idx - 2) + half + 1)
                elif idx >= 2:
                    act.wait_ge(gate_used, gate_used_no["up" + kind[4], idx - 2, half])
                elif kind != "gate0":
                    act.wait_ge(gate_used, gate_used_no["up" + str(int(kind[4]) - 1), KT - 2 + idx, half])

            def step(ins):
                steps[0] += 1
                ins.then_inc(act_step, 1)
                act.wait_ge(act_step, steps[0])

            def copy(dst, src):
                return act.activation(dst, src, ACT.Copy)

            def main(key):
                kind, idx, half = key
                no = OUT_NO[key]
                b = main_bank(key)
                bank = BANK[b][:, 0:TH]
                cols = slice(half * TH, half * TH + TH)
                if kind == "mem":
                    act.wait_ge(out_ready, no + 1)
                    dst = MKT[:, idx, :] if idx < 4 else FT[idx % 2][:, 0:MEM]
                    copy(dst, BANK[b][:, 0:MEM]).then_inc(bank_free[b], 1)
                elif kind in ("sq", "mq", "sk", "sv", "hi"):
                    act.wait_ge(out_ready, no + 1)
                    dst = {"sq": SQ, "mq": MQ}[kind][:, idx, cols] if kind in ("sq", "mq") else \
                        (SK[:, cols] if kind == "sk" else FT[idx % 2][:, cols])
                    copy(dst, bank).then_inc(bank_free[b], 1)
                elif kind == "hf":
                    act.wait_ge(out_ready, no + 1)
                    if ex_use[half]:
                        act.wait_ge(ex_free[half], ex_use[half])
                    ex_use[half] += 1
                    act.activation(EX[half][:], bank, ACT.Exp, scale=-1.0).then_inc(bank_free[b], 1)
                elif kind in SILU or kind[:4] == "gate":
                    act.wait_ge(out_ready, no + 1)
                    if kind == "fg" and idx == 0:
                        act.wait_ge(ln_lo[half], KT)
                    if kind in ("fg", "gate0", "gate1", "gate2"):
                        wait_gate_free(key)
                    act.activation(sig_dst(key), bank, ACT.Tanh, scale=0.5)\
                        .then_inc(silu_tanh if kind in SILU else bank_free[b], 1)

            def softmax_exp(u):
                kind, no = u[0], att_no[u]
                st = ST[:, no % 2]
                if kind == "ms":
                    for bl in range(4):
                        keys_free(act, 4 * u[1] + bl)
                        copy(MKB[bl % 2][:, 0:2, :].rearrange("p h t -> p (h t)"), BANK[T0_][:, :])\
                            .then_inc(bank_free[T0_], 1)
                act.wait_ge(max_ready, no + 1)
                lo, w = lo_of(u), {"ws": 192}.get(kind, 256)
                if kind[0] == "w":
                    act.activation(st[:, 16:20], st[:, 8:12], ACT.Exp, scale=0.125)
                    for s in range(4):
                        x = XP[:, no % 2, s, lo:w]
                        ins = act.activation(x, x, ACT.Exp, bias=st[:, 4 + s:5 + s], scale=0.125,
                                             accum_out=st[:, 12 + s:13 + s])
                    ins.then_inc(p_exp, 1)
                else:
                    for s in range(4 if kind == "mp" else 1):
                        src = BANK[S0_ + s // 2][:, 256 * (s % 2):256 * (s % 2) + 256]
                        ins = act.activation(XP[:, no % 2, s, :], src, ACT.Exp, bias=st[:, 4 + s:5 + s],
                                             scale=P ** -0.5, accum_out=st[:, 12 + s:13 + s])
                        if s % 2 or kind == "ms":
                            ins.then_inc(bank_free[S0_ + s // 2], 1)

            def save_probs_T(u):
                kind, no = u[0], att_no[u]
                act.wait_ge(pT_ready, no + 1)
                if no:
                    act.wait_ge(pv_ready, no)
                ptf = PT[:].rearrange("p a c t -> p (a c t)")
                if kind == "ws":
                    copy(ptf[:, 0:512], BANK[T0_][:, :]).then_inc(bank_free[T0_], 1)
                    copy(ptf[0:64, 512:1024], BANK[T1_][0:64, :]).then_inc(bank_free[T1_], 1)
                elif kind == "ms":
                    copy(ptf[:, 0:256], BANK[T0_][:, 0:256]).then_inc(bank_free[T0_], 1)
                else:
                    c0 = lo_of(u) // P
                    for i in range(2):
                        src = BANK[T0_ + i][:, :].rearrange("p (a c t) -> p a c t", a=2, c=2)
                        copy(PT[:, 2 * i:2 * i + 2, c0:2, :], src[:, :, c0:2, :]).then_inc(bank_free[T0_ + i], 1)

            def save_values(u):
                kind, no = u[0], att_no[u]
                act.wait_ge(pv_ready, no + 1)
                bank = BANK[V_]
                if kind == "w":
                    n, g = u[1:]
                    ins = copy(SQ[:, 2 * g:2 * g + 2, P * n:P * n + P],
                               bank[:, 0:256].rearrange("p (j t) -> p j t", j=2))
                elif kind == "ws":
                    ins = copy(SQ[:, :, SEQ:T].rearrange("p j (b i) -> p b j i", b=NB),
                               bank[:, 0:256].rearrange("p (b j i) -> p b j i", b=NB, j=4))
                elif kind == "mp":
                    n = u[1]
                    ins = copy(MQ[:, :, P * n:P * n + P], bank[:, :].rearrange("p (h t) -> p h t", h=4))
                else:
                    c0 = SEQ + 32 * u[1]
                    ins = copy(MQ[:, :, c0:c0 + 32], bank[:, 0:P].rearrange("p (h t) -> p h t", h=4))
                ins.then_inc(bank_free[V_], 1)

            def hgrn_decays(u):
                _, n, h = u
                no = hg_no[u]
                t0, w, levels = hg_cols(n)
                nl = len(levels)
                act.wait_ge(d_ready, no + 1)
                if no:
                    act.wait_ge(ekq_ready, no)
                if no == 0:
                    act.wait_ge(kv_stored, 96)
                act.activation(QE[:, 0:w], HB[:, h, t0:t0 + w], ACT.Exp)
                if n < NBLK:
                    act.activation(EBL[:, no % 4, 0:1], HB[:, h, t0 + P - 1:t0 + P], ACT.Exp)
                else:
                    act.activation(EBL[:, no % 4, :], HB[:, h, t0 + NS - 1:t0 + w:NS], ACT.Exp)
                e = E[no % 2]
                parts = [e[:, :, :]] if n < NBLK else [e[:, 0:nl, 0:w], e[:, 7:8, 0:w]]
                for part in parts:
                    step(act.activation(part, part, ACT.Abs))
                for i, part in enumerate(parts):
                    ins = act.activation(part, part, ACT.Exp, scale=-1.0)
                ins.then_inc(e_ready, 1)

            def save_decayed_keys(u):
                no = hg_no[u]
                w = hg_cols(u[1])[1]
                act.wait_ge(kT_ready, no + 1)
                copy(KTM[no % 2][0:w, :], BANK[T0_][0:w, 0:P]).then_inc(bank_free[T0_], 1)

            def split(u):
                act.wait_ge(raw_in[u % NRAW], raw_full[u])
                if u >= NHI:
                    unit_used(act, u - NHI)
                n = unit_tiles(u)
                copy(WH[u % NHI][:, 0:n, :], RAW[u % NRAW][:, 0:n, :]).then_inc(w_hi, 1)

            for s in SCHEDULE:
                what, rest = s[0], s[1:]
                if what == "out":
                    main(rest)
                elif what == "split_hi":
                    split(rest[0])
                elif what == "setup":
                    act.wait_ge(vecT_ready, 1)
                    copy(VEC[:, 0:57], BANK[V_][:, 0:57]).then_inc(bank_free[V_], 1)
                    saved(act, "vec")
                    act.wait_ge(lb_shifted, 1)
                    act.activation(LBT[:, 0:8], LBT[:, 0:8], ACT.Exp).then_inc(lb_exp, 1)
                elif what == "memx":
                    t = rest[0]
                    act.wait_ge(memT_ready, t + 1)
                    for i in range(2):
                        copy(MH[:, 4 * i:4 * i + 4, P * t:P * t + P],
                             BANK[T0_ + i][:, :].rearrange("p (k t) -> p k t", k=4)).then_inc(mem_hi_done, 1)
                elif what == "x_load":
                    for i in range(5):
                        src = a["x_sample"] if i == NBLK else a["x_prompt"][P * i:P * i + P, :]
                        act.dma_start(XS[i][0:TOKENS[i][1], :], src).then_inc(xs_in[i], 16)
                elif what == "rstd0":
                    act.wait_ge(x_var, 1)
                    step(act.activation(BNR[:], BNV[:, :, 1], ACT.Ln, bias=EPS[:, 0:1]))
                    act.activation(BNR[:], BNR[:], ACT.Exp, scale=-0.5).then_inc(x_rstd, 1)
                elif what == "ln0":
                    t = rest[0]
                    t0, n = TOKENS[t]
                    act.wait_ge(xT_ready, t + 1)
                    if t >= 2:
                        act.wait_ge(x_lo_done, t - 1)
                    for k in range(KT // 2, KT):
                        ins = act.activation(XT[t % 2][:, k, 0:n],
                                             BANK[T1_][:, P * (k % 4):P * (k % 4) + n], ACT.Identity,
                                             scale=vec["ln0_w"][:, k:k + 1], bias=vec["ln0_b"][:, k:k + 1])
                    ins.then_inc(bank_free[T1_], 1)
                elif what == "turn_mem":
                    idx = rest[0]
                    n_turn[0] += 1
                    act.wait_ge(turn_ready, n_turn[0])
                    dst = (MKTM if idx < 4 else MV)[:, :, P * (idx % 4):P * (idx % 4) + P]
                    copy(dst, BANK[V_][:, 0:MEM].rearrange("p (c n) -> p c n", c=2)).then_inc(bank_free[V_], 1)
                elif what == "turn":
                    kind, idx = rest
                    n_turn[0] += 1
                    act.wait_ge(turn_ready, n_turn[0])
                    b0, b1 = BANK[T0_], BANK[T1_]
                    if kind == "sk":
                        copy(SKTM[:, 0, :], b0[:, 384:512]).then_inc(bank_free[T0_], 1)
                        copy(SKTM[0:64, 1, :], b1[0:64, 0:P]).then_inc(bank_free[T1_], 1)
                    else:
                        full = SV[:, 0:4, :] if kind == "sv" else HV[:, 0:4, P * idx:P * idx + P]
                        tail = SV[0:64, 4, :] if kind == "sv" else HV[0:64, 4, P * idx:P * idx + P]
                        copy(full, b0[:, :].rearrange("p (t n) -> p t n", t=4)).then_inc(bank_free[T0_], 1)
                        copy(tail, b1[0:64, 0:P]).then_inc(bank_free[T1_], 1)
                elif what == "wk":
                    act.wait_ge(cacheT_ready, 1)
                    for i in range(2):
                        copy(KTS[:, 4 * i:4 * i + 4, :].rearrange("p b t -> p (b t)"), BANK[T0_ + i][:, :])\
                            .then_inc(bank_free[T0_ + i], 1)
                elif what == "scan":
                    j = rest[0]
                    act.wait_ge(f_ready, 2 * j + 2)
                    act.activation(HB[:, j, :], HB[:, j, :], ACT.Ln).then_inc(logf_done, 1)
                elif what == "P" and rest[0] == "h":
                    hgrn_decays(rest)
                elif what == "A":
                    (save_decayed_keys if rest[0] == "h" else softmax_exp)(rest)
                elif what == "B" and rest[0] != "h":
                    save_probs_T(rest)
                elif what == "C":
                    if rest[0] == "h":
                        _, n, h = rest
                        t0, w, _ = hg_cols(n)
                        act.wait_ge(ho_ready, hg_no[rest] + 1)
                        copy(HQ[:, h, t0:t0 + w], BANK[V_][:, 0:w]).then_inc(bank_free[V_], 1)
                    else:
                        save_values(rest)
                elif what == "rms_sum":
                    h = rest[0]
                    for half in range(2):
                        act.wait_ge(rms_sum, 2 * h + half + 1)
                        bank = (V_, T1_)[half]
                        copy(RRS[:, 2 * h + half, :], BANK[bank][:, 0:TH]).then_inc(bank_free[bank], 1)
                elif what == "rms":
                    h = rest[0]
                    if h == 0:
                        saved(act, "rms", 3, 1)
                        for i in range(0, 8, 2):
                            ins = act.activation(RRS[:, i:i + 2, :], RRS[:, i:i + 2, :], ACT.Ln, bias=EPS[:, 1:2],
                                                 scale=float(D // P))
                        step(ins)
                    act.activation(RRS[:, 2 * h:2 * h + 2, :], RRS[:, 2 * h:2 * h + 2, :], ACT.Exp, scale=-0.5)\
                        .then_inc(rms_rstd, 1)
                elif what == "center":
                    ln, half = rest
                    if ln > 1 or half:
                        act.wait_ge(var_ready, 2 * (ln - 1) + half)
                    for c in range(KT):
                        if c < KT - 1:
                            act.wait_ge(centered, 14 * (ln - 1) + 7 * half + c + 1)
                        else:
                            saved(act, "mean", ln, half)
                        act.activation(SQR[:, c, :], Y[:, c, half * TH:half * TH + TH], ACT.Square)\
                            .then_inc(squared, 1)
                elif what == "var":
                    ln, half = rest
                    act.wait_ge(var_ready, 2 * (ln - 1) + half + 1)
                    act.activation(SG[half][:], BANK[T0_][:, 0:TH], ACT.Ln, bias=EPS[:, 0:1])\
                        .then_inc(bank_free[T0_], 1)
                    saved(act, "var", ln, half)
                    act.activation(SG[half][:], SG[half][:], ACT.Exp, scale=-0.5).then_inc(ln_rstd, 1)
                elif what == "norm":
                    ln, half = rest
                    cols = slice(half * TH, half * TH + TH)
                    for c in range(KT):
                        act.wait_ge(ln_scaled, 16 * (ln - 1) + 8 * half + c + 1)
                        dst = XH[:, c, cols] if ln == 1 else Y[:, c, cols]
                        act.activation(dst, Y[:, c, cols], ACT.Identity, bias=vec[f"ln{ln}_b"][:, c:c + 1])\
                            .then_inc(ln_hi, 1)
                elif what == "store":
                    no = rest[0]
                    n = OUT_CHUNKS[no][1]
                    act.wait_ge(outT_ready, no + 1)
                    if no >= 2:
                        act.wait_ge(out_dma[no % 2], 16 * (no // 2))
                    bank = bank_use["outT", no, 0][0]
                    copy(OUTT[no % 2][0:n, 0:512], BANK[bank][0:n, :]).then_inc(bank_free[bank], 1)

        @block.vector
        def _(dve):
            steps = [0]
            ex_use = [0, 0]
            n_silu = [0]

            def step(ins):
                steps[0] += 1
                ins.then_inc(dve_step, 1)
                dve.wait_ge(dve_step, steps[0])

            def main(key):
                kind, idx, half = key
                b = main_bank(key)
                bank = BANK[b][:, 0:TH]
                cols = slice(half * TH, half * TH + TH)
                if kind == "hf":
                    out_saved(dve, key)
                    dst = HB[:, idx, cols]
                    step(dve.tensor_scalar(EX[half][:], EX[half][:], 1.0, None, ALU.add))
                    dve.reciprocal(dst, EX[half][:]).then_inc(ex_free[half], 1)
                    ex_use[half] += 1
                    dve.wait_ge(ex_free[half], ex_use[half])
                    step(dve.tensor_scalar(dst, dst, LB[:, 4 + idx:5 + idx], LB[:, idx:idx + 1],
                                           ALU.mult, ALU.add))
                    dve.tensor_scalar(HK[:, idx, cols], dst, -1.0, 1.0, ALU.mult, ALU.add).then_inc(f_ready, 1)
                elif kind in SILU:
                    n_silu[0] += 1
                    dve.wait_ge(silu_tanh, n_silu[0])
                    dst = sig_dst(key)
                    dve.scalar_tensor_tensor(out=dst, in0=dst, scalar=1.0, in1=bank, op0=ALU.add, op1=ALU.mult)\
                        .then_inc(bank_free[b], 1)
                    if kind == "hq":
                        out_saved(dve, key)
                        step(dve.tensor_scalar(dst, dst, 0.5, None, ALU.mult))
                elif kind[:2] == "up":
                    dve.wait_ge(out_ready, OUT_NO[key] + 1)
                    gate = SG[2 * (idx % 2) + half][:]
                    out_saved(dve, ("gate" + kind[2], idx, half))
                    mix = MIX[:, idx, cols]
                    dst = mix if kind == "up0" else gate
                    dve.scalar_tensor_tensor(out=dst, in0=gate, scalar=1.0, in1=bank, op0=ALU.add, op1=ALU.mult)\
                        .then_inc(bank_free[b], 1)
                    out_saved(dve, key)
                    if kind == "up0":
                        dve.engine_nop().then_inc(gate_used, 1)
                    else:
                        dve.tensor_tensor(mix, mix, gate, ALU.add).then_inc(gate_used, 1)
                elif kind == "fu":
                    dve.wait_ge(out_ready, OUT_NO[key] + 1)
                    gate = SG[2 * (idx % 2) + half][:]
                    out_saved(dve, ("fg", idx, half))
                    dve.scalar_tensor_tensor(out=gate, in0=gate, scalar=0.5, in1=bank, op0=ALU.mult, op1=ALU.mult)\
                        .then_inc(bank_free[b], 1)
                    out_saved(dve, key)
                    step(dve.tensor_copy(GH[:, idx, cols], gate))
                    dve.tensor_tensor(GL[:, idx, cols], gate, f32(GH[:, idx, cols]), ALU.subtract)\
                        .then_inc(hidden_done, 1)
                elif kind in ("o", "y"):
                    dve.wait_ge(out_ready, OUT_NO[key] + 1)
                    if key == ("o", 0, 0):
                        dve.wait_ge(prompt_state_out, 16)
                    y = Y[:, idx, cols]
                    dve.scalar_tensor_tensor(out=y, in0=f32(XH[:, idx, cols]), scalar=ALPHA, in1=bank,
                                             op0=ALU.mult, op1=ALU.add).then_inc(bank_free[b], 1)
                    out_saved(dve, key)
                    dve.scalar_tensor_tensor(out=y, in0=f32(XL[:, idx, cols]), scalar=ALPHA, in1=y,
                                             op0=ALU.mult, op1=ALU.add).then_inc(y_ready, 1)

            def norm_lo(half, c):
                cols = slice(half * TH, half * TH + TH)
                dve.wait_ge(ln_hi, KT * half + c + 1)
                dve.scalar_tensor_tensor(out=XL[:, c, cols], in0=Y[:, c, cols], scalar=vec["ln1_b"][:, c:c + 1],
                                         in1=f32(XH[:, c, cols]), op0=ALU.add, op1=ALU.subtract)\
                    .then_inc(ln_lo[half], 1)

            def softmax_max(u):
                kind, no = u[0], att_no[u]
                st = ST[:, no % 2]
                x = XP[:, no % 2]
                if kind == "ms":
                    for bl in range(4):
                        keys_free(dve, 4 * u[1] + bl)
                        dve.tensor_copy(MKB[bl % 2][:, 2:4, :].rearrange("p h t -> p (h t)"), BANK[T1_][:, :])\
                            .then_inc(bank_free[T1_], 1)
                dve.wait_ge(scores_ready, no + 1)
                if no >= 2:
                    dve.wait_ge(pT_ready, no - 1)
                if kind[0] == "w":
                    lo, w = lo_of(u), {"ws": 192}.get(kind, 256)
                    for s in range(4):
                        kv, jj = s // 2, s % 2
                        if kind == "w":
                            bias, slope = NEGD[:, lo:w], 8.0 * 2.0 ** -(2 * u[2] + jj + 4 * kv + 1)
                            src = BANK[S0_ + kv][:, 256 * jj + lo:256 * jj + 256]
                        else:
                            bias, slope = NEGS[:, s, :], SMALL[:, 0:1]
                            src = BANK[S0_ + kv][:, 192 * jj:192 * jj + 192]
                        ins = dve.scalar_tensor_tensor(out=x[:, s, lo:w], in0=bias, scalar=slope, in1=src,
                                                       op0=ALU.mult, op1=ALU.add)
                        if jj:
                            ins.then_inc(bank_free[S0_ + kv], 1)
                    saved(dve, "scores", no, 0)
                    saved(dve, "scores", no, 1)
                    step(dve.tensor_reduce(st[:, 0:4], x[:, :, lo:w], AX.X, ALU.max))
                    sink = SINK[:, 4 * u[2]:4 * u[2] + 4] if kind == "w" else SINK[:, 8:9].to_broadcast([P, 4])
                    step(dve.tensor_tensor(st[:, 0:4], st[:, 0:4], sink, ALU.max))
                    dve.tensor_tensor(st[:, 8:12], sink, st[:, 0:4], ALU.subtract)
                    dve.tensor_scalar(st[:, 4:8], st[:, 0:4], -0.125, None, ALU.mult).then_inc(max_ready, 1)
                else:
                    nbank = 2 if kind == "mp" else 1
                    for i in range(nbank):
                        src = BANK[S0_ + i][:, :].rearrange("p (s k) -> p s k", s=2)[:, 0:nbank]
                        ins = dve.tensor_reduce(st[:, 2 * i:2 * i + nbank], src, AX.X, ALU.max)
                    step(ins)
                    ns = nbank * nbank
                    dve.tensor_scalar(st[:, 4:4 + ns], st[:, 0:ns], -(P ** -0.5), None, ALU.mult)\
                        .then_inc(max_ready, 1)

            def softmax_divide(u):
                kind, no = u[0], att_no[u]
                st = ST[:, no % 2]
                ns = 1 if kind == "ms" else 4
                lo, w = lo_of(u), {"ws": 192}.get(kind, 256)
                if kind[0] == "w":
                    dve.wait_ge(p_exp, n_window_exps[u])
                    step(dve.tensor_tensor(st[:, 20:24], st[:, 12:16], st[:, 16:20], ALU.add))
                    step(dve.reciprocal(st[:, 24:28], st[:, 20:24]))
                else:
                    saved(dve, "scores", no, 0)
                    if kind == "mp":
                        saved(dve, "scores", no, 1)
                    step(dve.reciprocal(st[:, 24:24 + ns], st[:, 12:12 + ns]))
                x = XP[:, no % 2, 0:ns, lo:w]
                dve.tensor_tensor(x, x, bcast(st[:, 24:24 + ns], w - lo), ALU.mult).then_inc(p_ready, 1)

            window_units = [u for u in att_units if u[0][0] == "w"]
            n_window_exps = {u: i + 1 for i, u in enumerate(window_units)}

            def hgrn_decayed(u):
                _, n, h = u
                no = hg_no[u]
                t0, w, levels = hg_cols(n)
                nl = len(levels)
                e = E[no % 2]
                if no == 0:
                    dve.wait_ge(pv_ready, n_att)
                    dve.wait_ge(kv_stored, 96)
                    dve.wait_ge(mask_in, 16)
                    for hh in range(4):
                        saved(dve, "turn", "hi", hh, 0)
                k, q = HK[:, h, t0:t0 + w], HQ[:, h, t0:t0 + w]
                dve.wait_ge(e_ready, no + 1)
                if no:
                    dve.wait_ge(kT_ready, no)
                if n < NBLK:
                    dve.tensor_tensor(EK[:, :, :], e[:, :, :], over(k, 8), ALU.mult)
                else:
                    dve.tensor_tensor(EK[:, 0:nl, 0:w], e[:, 0:nl, 0:w], over(k, nl), ALU.mult)
                    dve.tensor_tensor(EK[:, 7, 0:w], e[:, 7, 0:w], k, ALU.mult)
                dve.tensor_tensor(QW[no % 3][:, 0:w], QE[:, 0:w], q, ALU.mult)
                dve.tensor_tensor(EQ[:, 0:nl, 0:w], e[:, 0:nl, 0:w], over(q, nl), ALU.mult).then_inc(ekq_ready, 1)

            def hgrn_mask(u):
                _, n, h = u
                no = hg_no[u]
                _, w, levels = hg_cols(n)
                nl = len(levels)
                if no:
                    dve.wait_ge(a_sum, no)
                dve.wait_ge(a_ready, no + 1)
                if n < NBLK:
                    for i in range(2):
                        src = BANK[S0_ + i][:, :].rearrange("p (l t) -> p l t", l=4)
                        dve.tensor_tensor(AM[:, 4 * i:4 * i + 4, :], src, MASKS[:, 4 * i:4 * i + 4, :], ALU.mult)\
                            .then_inc(bank_free[S0_ + i], 1)
                        saved(dve, "a", no, i)
                else:
                    src = BANK[S0_][:, :].rearrange("p (l t) -> p l t", l=4)
                    dve.tensor_tensor(AM[0:w, 0:4, 0:w], src[0:w, :, 0:w], MASKS[0:w, 4:8, 0:w], ALU.mult)\
                        .then_inc(bank_free[S0_], 1)
                    saved(dve, "a", no, 0)
                if no >= 2:
                    dve.wait_ge(ho_ready, no - 1)
                dve.tensor_reduce(ASB[no % 2][0:w, 0:w], AM[0:w, 0:nl + 1, 0:w].rearrange("p l t -> p t l"), AX.X, ALU.add)\
                    .then_inc(a_sum, 1)

            def hgrn_state(u):
                _, n, h = u
                no = hg_no[u]
                dve.wait_ge(ho_ready, no + 1)
                if n == 0:
                    dve.tensor_copy(STATE[:, h, :], BANK[T1_][:, 0:P]).then_inc(bank_free[T1_], 1)
                elif n < NBLK:
                    dve.scalar_tensor_tensor(out=STATE[:, h, :], in0=STATE[:, h, :], scalar=EBL[:, no % 4, 0:1],
                                             in1=BANK[T1_][:, 0:P], op0=ALU.mult, op1=ALU.add)\
                        .then_inc(bank_free[T1_], 1)
                else:
                    dve.wait_ge(state_decayed, h + 1)
                    for i in range(2):
                        o = SOUT[h % 2][:, 4 * i:4 * i + 4, :]
                        dve.tensor_tensor(o, o, BANK[T0_ + i][:, :].rearrange("p (b e) -> p b e", b=4), ALU.add)\
                            .then_inc(bank_free[T0_ + i], 1)

            for s in SCHEDULE:
                what, rest = s[0], s[1:]
                if what == "out":
                    main(rest)
                elif what == "split_lo" and rest[0] in VECTOR_UNITS:
                    split_lo(dve, rest[0])
                elif what == "init":
                    dve.memset(ONES[:], 1.0 / D)
                    dve.memset(EPS[:, 0:1], LN_EPS)
                    dve.memset(EPS[:, 1:2], RMS_EPS)
                    dve.memset(BNV[:], 1.0)
                    step(dve.memset(RST[:], 1.0))
                    dve.memset(RST[:, 0:SEQ:P], 0.0)
                    step(dve.memset(RST[:, SEQ:T:NS], 0.0))
                elif what == "setup":
                    dve.wait_ge(sink_in, 16)
                    step(dve.tensor_scalar(SINK[:], SINK[:], 8.0, None, ALU.mult))
                    saved(dve, "vec")
                    lb = vec["hg_lb"]
                    step(dve.tensor_tensor(LBT[:, 8:12], lb[:, 0:4], lb[:, 4:8], ALU.max))
                    dve.tensor_tensor(LBT[:, 0:4], lb[:, 0:4], LBT[:, 8:12], ALU.subtract)
                    dve.tensor_tensor(LBT[:, 4:8], lb[:, 4:8], LBT[:, 8:12], ALU.subtract).then_inc(lb_shifted, 1)
                    dve.wait_ge(lb_exp, 1)
                    step(dve.tensor_tensor(LBT[:, 8:12], LBT[:, 0:4], LBT[:, 4:8], ALU.add))
                    step(dve.reciprocal(LBT[:, 8:12], LBT[:, 8:12]))
                    step(dve.tensor_tensor(LB[:, 0:4], LBT[:, 0:4], LBT[:, 8:12], ALU.mult))
                    step(dve.tensor_scalar(LB[:, 4:8], LB[:, 0:4], -1.0, 1.0, ALU.mult, ALU.add))
                elif what == "memx":
                    t = rest[0]
                    for i in range(2):
                        dve.wait_ge(mem_hi_done, 2 * t + i + 1)
                        sl = (slice(None), slice(4 * i, 4 * i + 4), slice(P * t, P * t + P))
                        dve.tensor_tensor(ML[sl], BANK[T0_ + i][:, :].rearrange("p (k t) -> p k t", k=4),
                                          f32(MH[sl]), ALU.subtract).then_inc(bank_free[T0_ + i], 1)
                elif what == "stat":
                    t = rest[0]
                    n = TOKENS[t][1]
                    dve.wait_ge(xs_in[t], 16)
                    for i in range(2):
                        ins = dve.bn_stats(BNS[0:n, t, 6 * i:6 * i + 6], XS[t][0:n, 512 * i:512 * i + 512])
                    step(ins)
                    ins = dve.bn_aggr(BNV[0:n, t, :], BNS[0:n, t, :])
                    if t == NBLK:
                        ins.then_inc(x_var, 1)
                elif what == "scale0":
                    t = rest[0]
                    x = XS[t][0:TOKENS[t][1], :]
                    dve.wait_ge(x_rstd, 1)
                    dve.tensor_scalar(x, x, BNV[0:TOKENS[t][1], t, 0:1], BNR[0:TOKENS[t][1], t:t + 1],
                                      ALU.subtract, ALU.mult).then_inc(x_scaled, 1)
                elif what == "ln0":
                    t = rest[0]
                    t0, n = TOKENS[t]
                    dve.wait_ge(xT_ready, t + 1)
                    if t >= 2:
                        dve.wait_ge(x_lo_done, t - 1)
                    for k in range(KT // 2):
                        ins = dve.tensor_scalar(XT[t % 2][:, k, 0:n], BANK[T0_][:, P * k:P * k + n],
                                                vec["ln0_w"][:, k:k + 1], vec["ln0_b"][:, k:k + 1],
                                                ALU.mult, ALU.add)
                    ins.then_inc(bank_free[T0_], 1)
                    saved(dve, "xT", t, 0)
                    saved(dve, "xT", t, 1)
                    step(dve.tensor_copy(XH[:, :, t0:t0 + n], XT[t % 2][:, :, 0:n]))
                    dve.tensor_tensor(XL[:, :, t0:t0 + n], XT[t % 2][:, :, 0:n], f32(XH[:, :, t0:t0 + n]),
                                      ALU.subtract).then_inc(x_lo_done, 1)
                    if t == NBLK:
                        dve.wait_ge(attc_in, 48)
                elif what == "scan":
                    j = rest[0]
                    dve.wait_ge(logf_done, j + 1)
                    dve.tensor_tensor_scan(HB[:, j, :], RST[:], HB[:, j, :], 0.0, ALU.mult, ALU.add)\
                        .then_inc(b_ready, 1)
                elif what == "K" and rest[0] == "h":
                    hgrn_decayed(rest)
                elif what == "A" and rest[0] != "h":
                    softmax_max(rest)
                elif what == "N":
                    (hgrn_mask if rest[0] == "h" else softmax_divide)(rest)
                elif what == "C" and rest[0] == "h":
                    hgrn_state(rest)
                elif what == "rms_squares":
                    h = rest[0]
                    if h == 0:
                        for hh in range(4):
                            saved(dve, "ho", hg_no["h", NBLK, hh])
                        dve.wait_ge(kT_ready, len(hg_units))
                    if h >= 2:
                        dve.wait_ge(rms_sum, 2 * h - 2)
                    for half in range(2):
                        o = HQ[:, h, half * TH:half * TH + TH]
                        dve.tensor_tensor(RSQ[:, 2 * (h % 2) + half, :], o, o, ALU.mult).then_inc(rms_sq, 1)
                elif what == "rms":
                    h = rest[0]
                    dve.wait_ge(rms_rstd, h + 1)
                    o = HQ[:, h, :]
                    step(dve.scalar_tensor_tensor(out=o, in0=o, scalar=NORMW,
                                                  in1=RRS[:, 2 * h:2 * h + 2, :].rearrange("p a t -> p (a t)"),
                                                  op0=ALU.mult, op1=ALU.mult))
                    step(dve.scalar_tensor_tensor(out=o, in0=o, scalar=0.5, in1=HG[:, h, :],
                                                  op0=ALU.mult, op1=ALU.mult))
                elif what == "branch":
                    br, j = rest
                    if j == 0:
                        if br == 0:
                            saved(dve, "pv", n_att - 1)
                        else:
                            dve.wait_ge(out_ready, OUT_NO[f"up{br - 1}", KT - 1, 1] + 1)
                    src = (SQ, MQ, HQ)[br][:, j, :]
                    step(dve.tensor_copy(OSH[:, j, :], src))
                    dve.tensor_tensor(OSL[:, j, :], src, f32(OSH[:, j, :]), ALU.subtract)\
                        .then_inc(branch_split, 1)
                elif what == "mix":
                    c, half = rest
                    cols = slice(half * TH, half * TH + TH)
                    if (c, half) == (0, 0):
                        dve.wait_ge(state_out[0], 32)
                        dve.wait_ge(state_out[1], 32)
                    dve.wait_ge(gate_used, gate_used_no["up2", c, half])
                    step(dve.tensor_scalar(MIXH[:, c, cols], MIX[:, c, cols], 0.5, None, ALU.mult))
                    dve.scalar_tensor_tensor(out=MIXL[:, c, cols], in0=MIX[:, c, cols], scalar=0.5,
                                             in1=f32(MIXH[:, c, cols]), op0=ALU.mult, op1=ALU.subtract)\
                        .then_inc(mix_split, 1)
                elif what == "center":
                    ln, half = rest
                    mb = MEAN_BANK[half]
                    dve.wait_ge(mean_ready, 2 * (ln - 1) + half + 1)
                    for c in range(KT):
                        y = Y[:, c, half * TH:half * TH + TH]
                        dve.tensor_tensor(y, y, BANK[mb][:, 0:TH], ALU.subtract)\
                            .then_inc(centered if c < KT - 1 else bank_free[mb], 1)
                elif what == "norm":
                    ln, half = rest
                    cols = slice(half * TH, half * TH + TH)
                    dve.wait_ge(ln_rstd, 2 * (ln - 1) + half + 1)
                    saved(dve, "mean", ln, half)
                    for c in range(KT):
                        y = Y[:, c, cols]
                        dve.scalar_tensor_tensor(out=y, in0=y, scalar=vec[f"ln{ln}_w"][:, c:c + 1],
                                                 in1=SG[half][:], op0=ALU.mult, op1=ALU.mult)\
                            .then_inc(ln_scaled, 1)
                        if ln == 1 and c >= 2:
                            norm_lo(half, c - 2)
                    if ln == 1:
                        norm_lo(half, KT - 2)
                        norm_lo(half, KT - 1)
                elif what == "store":
                    no = rest[0]
                    n = OUT_CHUNKS[no][1]
                    dve.wait_ge(outT_ready, no + 1)
                    if no >= 2:
                        dve.wait_ge(out_dma[no % 2], 16 * (no // 2))
                    bank = bank_use["outT", no, 1][0]
                    dve.tensor_copy(OUTT[no % 2][0:n, 512:1024], BANK[bank][0:n, :]).then_inc(bank_free[bank], 1)


def kernel(x_prompt, x_sample, cache_k_win, cache_v_win, state_hgrn, cache_mem_k, cache_mem_v, mem_prompt,
           ln0_w, ln0_b, w_in, w_up_sw, w_up_hg, w_up_mx, sw_sinks, hg_lower_bound, hg_norm_w, w_mem_kv,
           w_o, ln1_w, ln1_b, w_ffn_in, w_ffn_out, ln2_w, ln2_b):
    import concourse.bacc as bacc
    from concourse.bass_utils import run_bass_kernel_spmd

    sinks = np.asarray(sw_sinks)[0]
    order = [2 * g + jj + 4 * kv for g in range(2) for kv in range(2) for jj in range(2)]
    row = np.arange(P)
    rows = np.concatenate([np.broadcast_to(sinks[order], (P, 8)),
                           sinks[(row // 8) % 4 + 4 * ((row // 32) % 2)][:, None]], axis=1)
    data = {
        "x_prompt": np.asarray(x_prompt)[0], "x_sample": np.asarray(x_sample).reshape(NB * NS, D),
        "cache_k": np.asarray(cache_k_win)[0].reshape(NB, WIN, P),
        "cache_v": np.asarray(cache_v_win)[0].reshape(NB, WIN, P),
        "state_in": np.asarray(state_hgrn)[0],
        "mem_k_s": np.asarray(cache_mem_k)[0].reshape(NB, MEM, 512),
        "mem_v_s": np.asarray(cache_mem_v)[0].reshape(NB, MEM, 512),
        "mem_prompt": np.asarray(mem_prompt)[0],
        "ln0_w": ln0_w, "ln0_b": ln0_b, "w_in": np.asarray(w_in)[0], "w_up_sw": np.asarray(w_up_sw)[0],
        "w_up_hg": np.asarray(w_up_hg)[0], "w_up_mx": np.asarray(w_up_mx)[0], "sink_rows": rows,
        "hg_lb": hg_lower_bound, "hg_norm_w": hg_norm_w, "w_mem_kv": np.asarray(w_mem_kv)[0],
        "w_o": np.asarray(w_o)[0], "ln1_w": np.asarray(ln1_w)[0], "ln1_b": np.asarray(ln1_b)[0],
        "w_ffn_in": np.asarray(w_ffn_in)[0], "w_ffn_out": np.asarray(w_ffn_out)[0],
        "ln2_w": np.asarray(ln2_w)[0], "ln2_b": np.asarray(ln2_b)[0],
        **shape_constants(),
    }
    shapes = {
        "y_p": (SEQ, D), "y_s": (NB * NS, D), "k_win_p": (WIN, P), "v_win_p": (WIN, P), "state_p": (4, P, P),
        "mem_k_p": (MEM, 512), "mem_v_p": (MEM, 512), "k_win_s": (NB, WIN, P), "v_win_s": (NB, WIN, P),
        "state_s": (NB, 4, P, P),
    }
    nc = bacc.Bacc("TRN2", target_bir_lowering=False, num_devices=1)
    arrays, ins, outs = {}, {}, {}
    for name, value in data.items():
        value = np.ascontiguousarray(value)
        arrays[f"in_{name}"] = value
        ins[name] = nc.dram_tensor(f"in_{name}", value.shape, mybir.dt.from_np(value.dtype),
                                   kind="ExternalInput").ap()
    for name, shape in shapes.items():
        outs[name] = nc.dram_tensor(f"out_{name}", shape, F32, kind="ExternalOutput").ap()
    build_decoder_layer(nc, ins, outs)
    r = run_bass_kernel_spmd(nc, [arrays], core_ids=[0]).results[0]
    got = {name: r[f"out_{name}"] for name in shapes}
    return (got["y_p"][None], got["y_s"].reshape(NB, NS, D),
            got["k_win_p"].reshape(1, 1, WIN, 2, 64), got["v_win_p"].reshape(1, 1, WIN, 2, 64),
            got["state_p"].reshape(1, 1, 4, P, P),
            got["mem_k_p"].reshape(1, 1, MEM, 4, P), got["mem_v_p"].reshape(1, 1, MEM, 4, P),
            got["k_win_s"].reshape(1, NB, WIN, 2, 64), got["v_win_s"].reshape(1, NB, WIN, 2, 64),
            got["state_s"][None])
```
